# Optimizing a Trainium2 kernel written in Bass

```python
import math
import jax, jax.numpy as jnp
from jax import lax
import numpy as np
import jax
import jax.numpy as jnp

D_MODEL = 1024
BATCH = 1
SEQ = 256
DEPTH = 1

CTX_LEN = 256
GRID_W = 64
A_HEADS = 4
A_DK = 128
A_DV = 128
A_KW = A_HEADS * A_DK
A_VW = A_HEADS * A_DV
A_CHUNK = 64
B_WIDTH = 512
HYENA_ORDER = 2
HYENA_SHORT = 3
HYENA_EMB = 33
HYENA_BANDS = (HYENA_EMB - 1) // 2
HYENA_FFN = 64
HYENA_FAST_DECAY = 0.3
HYENA_SLOW_DECAY = 1.5
HYENA_TARGET = 1e-2
HYENA_SHIFT = 0.05
HYENA_L1_EPS = 1e-6
D_FF = 2816
N_MOD = 9
RMS_EPS = 1e-6
COL_V = 0
COL_FFW = COL_V + A_VW
COL_FBW = COL_FFW + A_KW
COL_Q = COL_FBW + A_KW
COL_G = COL_Q + A_KW
COL_HY = COL_G + A_VW
COL_MERGE = COL_HY + 3 * B_WIDTH
IN_COLS = COL_MERGE + 2 * D_MODEL


def rms_norm(x):
    xf = x.astype(jnp.float32)
    return (xf * lax.rsqrt(jnp.mean(xf * xf, axis=-1, keepdims=True) + RMS_EPS)).astype(x.dtype)

def modulate(x, shift, scale):
    return x * (1.0 + scale) + shift

def swiglu(x, wg, wu, wd):
    return (jax.nn.silu(x @ wg) * (x @ wu)) @ wd

def half_ffn(h, shift, scale, gate, wg, wu, wd):
    return h + 0.5 * gate * swiglu(modulate(rms_norm(h), shift, scale), wg, wu, wd)

def grid_pos_embed(n_tokens):
    rows = n_tokens // GRID_W
    quarter = D_MODEL // 4
    omega = 1.0 / (10000.0 ** (jnp.arange(quarter, dtype=jnp.float32) / quarter))
    ar = jnp.arange(rows, dtype=jnp.float32)[:, None] * omega
    ac = jnp.arange(GRID_W, dtype=jnp.float32)[:, None] * omega
    er = jnp.concatenate([jnp.sin(ar), jnp.cos(ar)], axis=-1)
    ec = jnp.concatenate([jnp.sin(ac), jnp.cos(ac)], axis=-1)
    emb = jnp.concatenate([jnp.broadcast_to(er[:, None, :], (rows, GRID_W, D_MODEL // 2)),
                           jnp.broadcast_to(ec[None, :, :], (rows, GRID_W, D_MODEL // 2))], axis=-1)
    return emb.reshape(rows * GRID_W, D_MODEL)

def to_heads(a):
    b, l, w = a.shape
    return a.reshape(b, l, A_HEADS, w // A_HEADS).transpose(0, 2, 1, 3)

def hgrn2_forget(z, lb):
    f = lb + (1.0 - lb) * jax.nn.sigmoid(z.astype(jnp.float32))
    return to_heads(jnp.log(f)), to_heads(1.0 - f)

def hgrn2_chunk_scan(q, k, v, logf, s0):
    b, h, l, dk = q.shape
    n_chunks = l // A_CHUNK

    def to_chunks(a):
        return a.reshape(b, h, n_chunks, A_CHUNK, a.shape[-1]).transpose(2, 0, 1, 3, 4)

    within_scan = jnp.tril(jnp.ones((A_CHUNK, A_CHUNK), dtype=bool))[:, :, None]

    def step(s, inp):
        qb, kb, vb, gb = inp
        cum = jnp.cumsum(gb, axis=2)
        diff = cum[:, :, :, None, :] - cum[:, :, None, :, :]
        decay = jnp.exp(jnp.where(within_scan, diff, -jnp.inf))
        scores = jnp.einsum('bhtsd,bhsd->bhts', qb[:, :, :, None, :] * decay, kb)
        o = scores @ vb + (qb * jnp.exp(cum)) @ s
        last = cum[:, :, -1:, :]
        s_new = jnp.exp(last[:, :, 0, :])[..., None] * s + jnp.einsum('bhsd,bhse->bhde', kb * jnp.exp(last - cum), vb)
        return s_new, o

    s_final, oc = lax.scan(step, s0, (to_chunks(q), to_chunks(k), to_chunks(v), to_chunks(logf)))
    o = oc.transpose(1, 2, 0, 3, 4).reshape(b, h, l, v.shape[-1])
    return o, s_final

def hgrn2_final_state(k, v, logf):
    cum = jnp.cumsum(logf, axis=2)
    return jnp.einsum('bhld,bhle->bhde', k * jnp.exp(cum[:, :, -1:, :] - cum), v)

def flip_seq(a):
    return jnp.flip(a, axis=2)

def hgrn2_bidir(q, v, logf_fw, k_fw, logf_bw, k_bw, s0_fw, s0_bw):
    o_fw, s_fw = hgrn2_chunk_scan(q, k_fw, v, logf_fw, s0_fw)
    o_bw, s_bw = hgrn2_chunk_scan(flip_seq(q), flip_seq(k_bw), flip_seq(v), flip_seq(logf_bw), s0_bw)
    return o_fw + flip_seq(o_bw), s_fw, s_bw

def context_states(nc, w_in, lb):
    p = nc @ w_in[:, :COL_Q]
    v = to_heads(p[..., COL_V:COL_FFW]).astype(jnp.float32)
    logf_fw, k_fw = hgrn2_forget(p[..., COL_FFW:COL_FBW], lb[0])
    logf_bw, k_bw = hgrn2_forget(p[..., COL_FBW:COL_Q], lb[1])
    s_fw = hgrn2_final_state(k_fw, v, logf_fw)
    s_bw = hgrn2_final_state(flip_seq(k_bw), flip_seq(v), flip_seq(logf_bw))
    return s_fw, s_bw

def short_conv(u, w, bias):
    l = u.shape[1]
    pad = HYENA_SHORT // 2
    up = jnp.pad(u, ((0, 0), (pad, pad), (0, 0)))
    out = bias
    for j in range(HYENA_SHORT):
        out = out + up[:, j:j + l] * w[j]
    return out

def hyena_pos_features(l):
    p = jnp.arange(l, dtype=jnp.float32)
    t = p / (l - 1)
    w = 2.0 * math.pi * p / l
    f = jnp.linspace(1e-4, HYENA_BANDS - 1, HYENA_BANDS, dtype=jnp.float32)
    ang = w[:, None] * f[None, :]
    z = jnp.concatenate([t[:, None], jnp.cos(ang), -jnp.sin(ang)], axis=-1)
    return t, z

def hyena_kernels(l, w1, b1, fr1, w2, b2, fr2, w3):
    t, z = hyena_pos_features(l)
    h = jnp.sin(fr1 * (z @ w1 + b1))
    h = jnp.sin(fr2 * (h @ w2 + b2))
    h = (h @ w3).astype(jnp.float32).reshape(l, HYENA_ORDER, 2, B_WIDTH)
    max_decay = math.log(HYENA_TARGET) / HYENA_FAST_DECAY
    min_decay = math.log(HYENA_TARGET) / HYENA_SLOW_DECAY
    deltas = jnp.abs(jnp.linspace(min_decay, max_decay, B_WIDTH, dtype=jnp.float32))
    window = jnp.exp(-t[:, None] * deltas[None, :]) + HYENA_SHIFT
    h = h * window[:, None, None, :]
    kern = jnp.concatenate([h[:, :, 0], jnp.flip(h[:, :, 1], axis=0)], axis=0)
    return kern / (jnp.sum(jnp.abs(kern), axis=0, keepdims=True) + HYENA_L1_EPS)

def fft_conv(u, kern):
    l = u.shape[1]
    uf = jnp.fft.rfft(u.astype(jnp.float32), n=2 * l, axis=1)
    kf = jnp.fft.rfft(kern, n=2 * l, axis=0)
    return jnp.fft.irfft(uf * kf[None], n=2 * l, axis=1)[:, :l]

def hyena(u3, kern, hy_bias):
    v, x1, x2 = jnp.split(u3, 3, axis=-1)
    z = v
    for o, gate in enumerate((x1, x2)):
        z = gate * (fft_conv(z, kern[:, o]).astype(z.dtype) + hy_bias[o] * z)
    return z

def token_mixers(n, s0_fw, s0_bw, kern, w_in, lb, a_norm_w, conv_w, conv_b, hy_bias, w_pa, w_pb, w_out):
    b, l, _ = n.shape
    p = n @ w_in
    v = to_heads(p[..., COL_V:COL_FFW]).astype(jnp.float32)
    logf_fw, k_fw = hgrn2_forget(p[..., COL_FFW:COL_FBW], lb[0])
    logf_bw, k_bw = hgrn2_forget(p[..., COL_FBW:COL_Q], lb[1])
    q = to_heads(jax.nn.silu(p[..., COL_Q:COL_G])).astype(jnp.float32)
    o, s_fw, s_bw = hgrn2_bidir(q, v, logf_fw, k_fw, logf_bw, k_bw, s0_fw, s0_bw)
    o = rms_norm(o.transpose(0, 2, 1, 3)) * a_norm_w
    o_a = o.reshape(b, l, A_VW).astype(n.dtype) * jax.nn.silu(p[..., COL_G:COL_HY])
    u3 = short_conv(p[..., COL_HY:COL_MERGE], conv_w, conv_b)
    o_b = hyena(u3, kern, hy_bias)
    g_a, g_b = jnp.split(p[..., COL_MERGE:], 2, axis=-1)
    y = jax.nn.sigmoid(g_a) * (o_a @ w_pa) + jax.nn.sigmoid(g_b) * (o_b @ w_pb)
    return y @ w_out, s_fw, s_bw

def first_inputs(seed: int = 0) -> dict:
    key = jax.random.key(seed)
    ks = jax.random.split(key, 32)
    nrm = jax.random.normal
    f32 = jnp.float32
    d = D_MODEL
    return {
        'x': nrm(ks[0], (BATCH, SEQ, d), f32),
        'c': nrm(ks[1], (BATCH, d), f32),
        'ctx': nrm(ks[2], (BATCH, CTX_LEN, d), f32),
        'c_ctx': nrm(ks[3], (d,), f32),
        'mod_w': nrm(ks[4], (DEPTH, d, N_MOD * d), f32) * d ** -0.5,
        'mod_b': nrm(ks[5], (DEPTH, N_MOD * d), f32) * 0.01,
        'ffn_w_gate': nrm(ks[6], (DEPTH, 2, d, D_FF), f32) * d ** -0.5,
        'ffn_w_up': nrm(ks[7], (DEPTH, 2, d, D_FF), f32) * d ** -0.5,
        'ffn_w_down': nrm(ks[8], (DEPTH, 2, D_FF, d), f32) * D_FF ** -0.5,
        'w_in': nrm(ks[9], (DEPTH, d, IN_COLS), f32) * d ** -0.5,
        'hgrn_lb_logits': nrm(ks[10], (DEPTH + 1, 2, A_KW), f32) * 0.1,
        'hgrn_norm_w': 1.0 + 0.1 * nrm(ks[11], (DEPTH, A_DV), f32),
        'hyena_conv_w': nrm(ks[12], (DEPTH, HYENA_SHORT, 3 * B_WIDTH), f32) * HYENA_SHORT ** -0.5,
        'hyena_conv_b': nrm(ks[13], (DEPTH, 3 * B_WIDTH), f32) * 0.01,
        'hyena_w1': nrm(ks[14], (DEPTH, HYENA_EMB, HYENA_FFN), f32) * HYENA_EMB ** -0.5,
        'hyena_b1': nrm(ks[15], (DEPTH, HYENA_FFN), f32) * 0.1,
        'hyena_freq1': 1.0 + 0.1 * nrm(ks[16], (DEPTH, HYENA_FFN), f32),
        'hyena_w2': nrm(ks[17], (DEPTH, HYENA_FFN, HYENA_FFN), f32) * HYENA_FFN ** -0.5,
        'hyena_b2': nrm(ks[18], (DEPTH, HYENA_FFN), f32) * 0.1,
        'hyena_freq2': 1.0 + 0.1 * nrm(ks[19], (DEPTH, HYENA_FFN), f32),
        'hyena_w3': nrm(ks[20], (DEPTH, HYENA_FFN, HYENA_ORDER * 2 * B_WIDTH), f32) * HYENA_FFN ** -0.5,
        'hyena_bias': nrm(ks[21], (DEPTH, HYENA_ORDER, B_WIDTH), f32),
        'w_proj_a': nrm(ks[22], (DEPTH, A_VW, d), f32) * A_VW ** -0.5,
        'w_proj_b': nrm(ks[23], (DEPTH, B_WIDTH, d), f32) * B_WIDTH ** -0.5,
        'w_out': nrm(ks[24], (DEPTH, d, d), f32) * d ** -0.5,
        'final_norm_w': 1.0 + 0.1 * nrm(ks[25], (d,), f32),
    }

def first_block(x, c, ctx, c_ctx, mod_w, mod_b, ffn_w_gate, ffn_w_up, ffn_w_down, w_in, hgrn_lb_logits,
              hgrn_norm_w, hyena_conv_w, hyena_conv_b, hyena_w1, hyena_b1, hyena_freq1, hyena_w2, hyena_b2,
              hyena_freq2, hyena_w3, hyena_bias, w_proj_a, w_proj_b, w_out, final_norm_w):
    n_lat = x.shape[1]
    n_ctx = ctx.shape[1]
    h = x + grid_pos_embed(n_lat).astype(x.dtype)[None]
    hc = ctx
    lb_all = jnp.cumsum(jax.nn.softmax(hgrn_lb_logits.astype(jnp.float32), axis=0), axis=0)
    for l in range(DEPTH):
        last = l == DEPTH - 1
        m = jnp.split((jax.nn.silu(c) @ mod_w[l] + mod_b[l])[:, None, :], N_MOD, axis=-1)
        mc = jnp.split((jax.nn.silu(c_ctx) @ mod_w[l] + mod_b[l])[None, None, :], N_MOD, axis=-1)
        h = half_ffn(h, m[0], m[1], m[2], ffn_w_gate[l, 0], ffn_w_up[l, 0], ffn_w_down[l, 0])
        hc = half_ffn(hc, mc[0], mc[1], mc[2], ffn_w_gate[l, 0], ffn_w_up[l, 0], ffn_w_down[l, 0])
        n = modulate(rms_norm(h), m[3], m[4])
        nc = modulate(rms_norm(hc), mc[3], mc[4])
        mix_w = (w_in[l], lb_all[l], hgrn_norm_w[l], hyena_conv_w[l], hyena_conv_b[l], hyena_bias[l],
                 w_proj_a[l], w_proj_b[l], w_out[l])
        filt_w = (hyena_w1[l], hyena_b1[l], hyena_freq1[l], hyena_w2[l], hyena_b2[l], hyena_freq2[l], hyena_w3[l])
        if last:
            s_fw, s_bw = context_states(nc, w_in[l], lb_all[l])
        else:
            zeros = jnp.zeros((hc.shape[0], A_HEADS, A_DK, A_DV), jnp.float32)
            out_c, s_fw, s_bw = token_mixers(nc, zeros, zeros, hyena_kernels(n_ctx, *filt_w), *mix_w)
            hc = hc + mc[5] * out_c
            hc = half_ffn(hc, mc[6], mc[7], mc[8], ffn_w_gate[l, 1], ffn_w_up[l, 1], ffn_w_down[l, 1])
        out, _, _ = token_mixers(n, s_fw, s_bw, hyena_kernels(n_lat, *filt_w), *mix_w)
        h = h + m[5] * out
        h = half_ffn(h, m[6], m[7], m[8], ffn_w_gate[l, 1], ffn_w_up[l, 1], ffn_w_down[l, 1])
    return rms_norm(h) * final_norm_w


DEPTH_2 = 2

CHUNK = 64

SSD_HEAD_DIM = 64
SSD_WIDTH = D_MODEL // 2
SSD_HEADS = SSD_WIDTH // SSD_HEAD_DIM
SSD_GROUPS = 2
SSD_HPG = SSD_HEADS // SSD_GROUPS
SSD_STATE = 64
SSD_CONV = 4
SSD_XBC = SSD_WIDTH + 2 * SSD_GROUPS * SSD_STATE

RWKV_HEAD_DIM = 64
RWKV_WIDTH = D_MODEL // 4
RWKV_HEADS = RWKV_WIDTH // RWKV_HEAD_DIM
RWKV_DECAY_RANK = 32
RWKV_ICLR_RANK = 32
RWKV_GATE_RANK = 64
RWKV_SPLITS = [RWKV_WIDTH, RWKV_WIDTH, RWKV_WIDTH, RWKV_DECAY_RANK, RWKV_ICLR_RANK, RWKV_GATE_RANK]
RWKV_IN = sum(RWKV_SPLITS)
RWKV_GN_EPS = 64e-5

GLA_VALUE_DIM = 64
GLA_WIDTH = D_MODEL // 4
GLA_HEADS = GLA_WIDTH // GLA_VALUE_DIM
GLA_KEY_DIM = GLA_VALUE_DIM // 2
GLA_QK_WIDTH = GLA_HEADS * GLA_KEY_DIM
GLA_GATE_RANK = 16
GLA_GATE_TEMP = 16.0

MIX_WIDTH = SSD_WIDTH + RWKV_WIDTH + GLA_WIDTH
IN_SPLITS = [SSD_WIDTH, SSD_XBC, SSD_HEADS, RWKV_IN, GLA_QK_WIDTH, GLA_QK_WIDTH, GLA_WIDTH, GLA_WIDTH, GLA_GATE_RANK]
N_IN = sum(IN_SPLITS)

N_GROUPS = 4
EXPERTS_PER_GROUP = 8
N_EXPERTS = N_GROUPS * EXPERTS_PER_GROUP
TOP_K = 2
EXPERT_FF = 512
ROW_BLOCK = 256

DEEPNORM_ALPHA = (2 * DEPTH_2) ** 0.25
DEEPNORM_BETA = (8 * DEPTH_2) ** -0.25
LN_EPS = 1e-5


F32 = jnp.float32

def _split(t, sizes):
    idx = [int(i) for i in np.cumsum(sizes)[:-1]]
    return jnp.split(t, idx, axis=-1)

def layer_norm(x, g, b):
    xf = x.astype(F32)
    mu = jnp.mean(xf, -1, keepdims=True)
    var = jnp.mean(jnp.square(xf - mu), -1, keepdims=True)
    return ((xf - mu) * lax.rsqrt(var + LN_EPS) * g + b).astype(x.dtype)

def causal_depthwise_conv(x, w, b):
    k, c = w.shape
    y = lax.conv_general_dilated(x, w[:, None, :], window_strides=(1,), padding=[(k - 1, 0)],
                                 dimension_numbers=('NWC', 'WIO', 'NWC'), feature_group_count=c)
    return y + b

def ssd_chunked_scan(x, a_dt, bm, cm):
    bsz, seq = x.shape[0], x.shape[1]
    nc = seq // CHUNK
    x = x.reshape(bsz, nc, CHUNK, *x.shape[2:])
    a_dt = a_dt.reshape(bsz, nc, CHUNK, *a_dt.shape[2:])
    bm = bm.reshape(bsz, nc, CHUNK, *bm.shape[2:])
    cm = cm.reshape(bsz, nc, CHUNK, *cm.shape[2:])
    a_cs = jnp.cumsum(a_dt, axis=2)
    mask = jnp.tril(jnp.ones((CHUNK, CHUNK), bool))[:, :, None, None]
    seg = jnp.exp(jnp.where(mask, a_cs[:, :, :, None] - a_cs[:, :, None, :], -jnp.inf))
    cb = jnp.einsum('bclgn,bcsgn->bclsg', cm, bm)
    y_diag = jnp.einsum('bclsgh,bcsghp->bclghp', cb[..., None] * seg, x)
    to_end = jnp.exp(a_cs[:, :, -1:] - a_cs)
    states = jnp.einsum('bclgn,bclghp->bcghpn', bm, to_end[..., None] * x)
    chunk_decay = jnp.exp(a_cs[:, :, -1])

    def step(s, inp):
        st, dec = inp
        return s * dec[..., None, None] + st, s

    s0 = jnp.zeros_like(states[:, 0])
    _, prev = lax.scan(step, s0, (jnp.moveaxis(states, 1, 0), jnp.moveaxis(chunk_decay, 1, 0)))
    prev = jnp.moveaxis(prev, 0, 1)
    y_off = jnp.einsum('bclgn,bcghpn->bclghp', cm, prev) * jnp.exp(a_cs)[..., None]
    return (y_diag + y_off).reshape(bsz, seq, *x.shape[3:])

def ssd_mixer(z, xbc, dt_raw, conv_w, conv_b, dt_bias, a_log, d_skip, norm_g):
    bsz, seq, _ = xbc.shape
    xbc = jax.nn.silu(causal_depthwise_conv(xbc, conv_w, conv_b))
    xh, bm, cm = _split(xbc, [SSD_WIDTH, SSD_GROUPS * SSD_STATE, SSD_GROUPS * SSD_STATE])
    xh = xh.astype(F32).reshape(bsz, seq, SSD_GROUPS, SSD_HPG, SSD_HEAD_DIM)
    bm = bm.astype(F32).reshape(bsz, seq, SSD_GROUPS, SSD_STATE)
    cm = cm.astype(F32).reshape(bsz, seq, SSD_GROUPS, SSD_STATE)
    dt = jax.nn.softplus((dt_raw + dt_bias).astype(F32)).reshape(bsz, seq, SSD_GROUPS, SSD_HPG)
    a = -jnp.exp(a_log.astype(F32)).reshape(SSD_GROUPS, SSD_HPG)
    y = ssd_chunked_scan(xh * dt[..., None], dt * a, bm, cm)
    y = y + d_skip.astype(F32).reshape(SSD_GROUPS, SSD_HPG)[:, :, None] * xh
    y = y.reshape(bsz, seq, SSD_WIDTH) * jax.nn.silu(z.astype(F32))
    y = y.reshape(bsz, seq, SSD_GROUPS, SSD_WIDTH // SSD_GROUPS)
    y = y * lax.rsqrt(jnp.mean(y * y, -1, keepdims=True) + RMS_EPS)
    return y.reshape(bsz, seq, SSD_WIDTH) * norm_g

def rwkv7_mixer(p, mu, w0, w2, a0, a2, g2, k_k, k_a, r_k, ln_g, ln_b):
    bsz, seq, _ = p.shape
    prev = jnp.pad(p, ((0, 0), (1, 0), (0, 0)))[:, :seq]
    p = p + (prev - p) * mu
    r, k, v, w_lr, a_lr, g_lr = _split(p, RWKV_SPLITS)
    w = -jax.nn.softplus(-(w0 + jnp.tanh(w_lr) @ w2).astype(F32)) - 0.5
    decay = jnp.exp(-jnp.exp(w))
    a = jax.nn.sigmoid((a0 + a_lr @ a2).astype(F32))
    g = (jax.nn.sigmoid(g_lr) @ g2).astype(F32)

    def heads(t):
        return t.astype(F32).reshape(bsz, seq, RWKV_HEADS, RWKV_HEAD_DIM)

    r, k, v, decay, a = heads(r), heads(k), heads(v), heads(decay), heads(a)
    kk = k * k_k.astype(F32).reshape(RWKV_HEADS, RWKV_HEAD_DIM)
    kk = kk * lax.rsqrt(jnp.sum(kk * kk, -1, keepdims=True) + 1e-12)
    k = k * (1.0 + (a - 1.0) * k_a.astype(F32).reshape(RWKV_HEADS, RWKV_HEAD_DIM))

    def step(state, inp):
        r_t, w_t, k_t, v_t, kk_t, a_t = inp
        sa = jnp.einsum('bhvk,bhk->bhv', state, -kk_t)
        state = (state * w_t[:, :, None, :] + sa[..., None] * (kk_t * a_t)[:, :, None, :]
                 + v_t[..., None] * k_t[:, :, None, :])
        return state, jnp.einsum('bhvk,bhk->bhv', state, r_t)

    s0 = jnp.zeros((bsz, RWKV_HEADS, RWKV_HEAD_DIM, RWKV_HEAD_DIM), F32)
    tm = lambda t: jnp.moveaxis(t, 1, 0)
    _, y = lax.scan(step, s0, (tm(r), tm(decay), tm(k), tm(v), tm(kk), tm(a)))
    y = jnp.moveaxis(y, 0, 1)
    mean = jnp.mean(y, -1, keepdims=True)
    var = jnp.mean(jnp.square(y - mean), -1, keepdims=True)
    y = ((y - mean) * lax.rsqrt(var + RWKV_GN_EPS)).reshape(bsz, seq, RWKV_WIDTH) * ln_g + ln_b
    bonus = jnp.sum(r * k * r_k.astype(F32), -1, keepdims=True) * v
    return (y + bonus.reshape(bsz, seq, RWKV_WIDTH)) * g

def gla_mixer(q, k, v, g, a_lr, w_a2, b_a, norm_g):
    bsz, seq, _ = q.shape
    nc = seq // CHUNK
    log_a = jax.nn.log_sigmoid((a_lr @ w_a2 + b_a).astype(F32)) / GLA_GATE_TEMP

    def chunks(t, d):
        return jnp.moveaxis(t.astype(F32).reshape(bsz, nc, CHUNK, GLA_HEADS, d), 1, 0)

    qc = chunks(q, GLA_KEY_DIM) * (GLA_KEY_DIM ** -0.5)
    kc = chunks(k, GLA_KEY_DIM)
    vc = chunks(v, GLA_VALUE_DIM)
    lac = chunks(log_a, GLA_KEY_DIM)
    mask = jnp.tril(jnp.ones((CHUNK, CHUNK), bool))[None, :, :, None, None]

    def step(state, inp):
        q_c, k_c, v_c, la_c = inp
        cum = jnp.cumsum(la_c, axis=1)
        o_inter = jnp.einsum('bihd,bhde->bihe', q_c * jnp.exp(cum), state)
        rel = jnp.exp(jnp.where(mask, cum[:, :, None] - cum[:, None, :], -jnp.inf))
        scores = jnp.einsum('bijhd,bjhd->bhij', q_c[:, :, None] * rel, k_c)
        o_intra = jnp.einsum('bhij,bjhe->bihe', scores, v_c)
        last = cum[:, -1]
        k_dec = k_c * jnp.exp(last[:, None] - cum)
        state = state * jnp.exp(last)[..., None] + jnp.einsum('bjhd,bjhe->bhde', k_dec, v_c)
        return state, o_inter + o_intra

    s0 = jnp.zeros((bsz, GLA_HEADS, GLA_KEY_DIM, GLA_VALUE_DIM), F32)
    _, o = lax.scan(step, s0, (qc, kc, vc, lac))
    o = jnp.moveaxis(o, 0, 1).reshape(bsz, seq, GLA_HEADS, GLA_VALUE_DIM)
    o = o * lax.rsqrt(jnp.mean(o * o, -1, keepdims=True) + RMS_EPS)
    return o.reshape(bsz, seq, GLA_WIDTH) * norm_g * jax.nn.silu(g.astype(F32))

def hybrid_mixer(x, w_in, ssd_conv_w, ssd_conv_b, ssd_dt_bias, ssd_a_log, ssd_d, ssd_norm_g,
                 rwkv_mu, rwkv_w0, rwkv_w2, rwkv_a0, rwkv_a2, rwkv_g2, rwkv_k_k, rwkv_k_a, rwkv_r_k,
                 rwkv_ln_g, rwkv_ln_b, gla_w_a2, gla_b_a, gla_norm_g, w_out):
    p = x @ w_in
    s_z, s_xbc, s_dt, rw, gq, gk, gv, gg, ga = _split(p, IN_SPLITS)
    y_ssd = ssd_mixer(s_z, s_xbc, s_dt, ssd_conv_w, ssd_conv_b, ssd_dt_bias, ssd_a_log, ssd_d, ssd_norm_g)
    y_rwkv = rwkv7_mixer(rw, rwkv_mu, rwkv_w0, rwkv_w2, rwkv_a0, rwkv_a2, rwkv_g2, rwkv_k_k, rwkv_k_a,
                         rwkv_r_k, rwkv_ln_g, rwkv_ln_b)
    y_gla = gla_mixer(gq, gk, gv, gg, ga, gla_w_a2, gla_b_a, gla_norm_g)
    y = jnp.concatenate([y_ssd, y_rwkv, y_gla], axis=-1).astype(x.dtype)
    return y @ w_out

def grouped_expert_mlp(xt, expert_id, gate, w_gate, w_up, w_down):
    n_tok, d = xt.shape
    n_assign = expert_id.size
    e_flat = expert_id.reshape(-1)
    order = jnp.argsort(e_flat)
    e_sorted = e_flat[order]
    counts = jnp.bincount(e_flat, length=N_EXPERTS)
    padded = (counts + ROW_BLOCK - 1) // ROW_BLOCK * ROW_BLOCK
    pad_end = jnp.cumsum(padded)
    pad_start = pad_end - padded
    start = jnp.cumsum(counts) - counts
    dest = pad_start[e_sorted] + jnp.arange(n_assign, dtype=jnp.int32) - start[e_sorted]
    n_blocks = -(-n_assign // ROW_BLOCK) + N_EXPERTS
    n_rows = n_blocks * ROW_BLOCK
    row_tok = jnp.full((n_rows,), n_tok, jnp.int32).at[dest].set((order // TOP_K).astype(jnp.int32))
    row_gate = jnp.zeros((n_rows,), xt.dtype).at[dest].set(gate.reshape(-1)[order].astype(xt.dtype))
    block_start = jnp.arange(n_blocks, dtype=jnp.int32) * ROW_BLOCK
    block_expert = jnp.minimum(jnp.searchsorted(pad_end, block_start, side='right'), N_EXPERTS - 1)
    x_pad = jnp.concatenate([xt, jnp.zeros((1, d), xt.dtype)], axis=0)
    xs = x_pad[row_tok].reshape(n_blocks, ROW_BLOCK, d)

    def block_mlp(args):
        xb, e = args
        h = jax.nn.silu(xb @ w_gate[e]) * (xb @ w_up[e])
        return h @ w_down[e]

    ys = lax.map(block_mlp, (xs, block_expert)).reshape(n_rows, d)
    out = jnp.zeros((n_tok + 1, d), ys.dtype).at[row_tok].add(ys * row_gate[:, None])
    return out[:n_tok]

def hierarchical_moe(x, w_rg, b_rg, w_re, b_re, w_gate, w_up, w_down):
    bsz, seq, d = x.shape
    xt = x.reshape(-1, d)
    n_tok = xt.shape[0]
    g_prob = jax.nn.softmax((xt @ w_rg + b_rg).astype(F32), axis=-1)
    g_w, g_idx = lax.top_k(g_prob, 1)
    e_logits = (xt @ w_re + b_re).astype(F32).reshape(n_tok, N_GROUPS, EXPERTS_PER_GROUP)
    e_logits = jnp.take_along_axis(e_logits, g_idx[:, :, None], axis=1)[:, 0]
    e_prob = jax.nn.softmax(e_logits, axis=-1)
    e_w, e_local = lax.top_k(e_prob, TOP_K)
    e_w = e_w / jnp.sum(e_w, -1, keepdims=True)
    gate = g_w * e_w
    expert_id = g_idx * EXPERTS_PER_GROUP + e_local
    y = grouped_expert_mlp(xt, expert_id, gate, w_gate, w_up, w_down)
    return y.reshape(bsz, seq, d).astype(x.dtype)

def second_inputs(seed: int = 0) -> dict:
    key = jax.random.key(seed)
    ks = iter(jax.random.split(key, 48))
    L = DEPTH_2

    def nrm(shape, scale):
        return scale * jax.random.normal(next(ks), shape, F32)

    def gain(shape):
        return 1.0 + nrm(shape, 0.02)

    x = nrm((BATCH, SEQ, D_MODEL), 1.0)
    ln_in_g = gain((D_MODEL,))
    ln_in_b = nrm((D_MODEL,), 0.02)
    w_in = nrm((L, D_MODEL, N_IN), D_MODEL ** -0.5)
    ssd_conv_w = nrm((L, SSD_CONV, SSD_XBC), SSD_CONV ** -0.5)
    ssd_conv_b = nrm((L, SSD_XBC), 0.02)
    dt = jnp.exp(jax.random.uniform(next(ks), (L, SSD_HEADS), F32, math.log(1e-3), math.log(1e-1)))
    ssd_dt_bias = dt + jnp.log(-jnp.expm1(-dt))
    ssd_a_log = jnp.log(jax.random.uniform(next(ks), (L, SSD_HEADS), F32, 1.0, 16.0))
    ssd_d = 1.0 + nrm((L, SSD_HEADS), 0.1)
    ssd_norm_g = gain((L, SSD_WIDTH))
    rwkv_mu = jax.random.uniform(next(ks), (L, RWKV_IN), F32)
    rwkv_w0 = jnp.linspace(-6.5, -1.5, RWKV_WIDTH, dtype=F32)[None, :] + nrm((L, RWKV_WIDTH), 0.1)
    rwkv_w2 = nrm((L, RWKV_DECAY_RANK, RWKV_WIDTH), 0.1)
    rwkv_a0 = nrm((L, RWKV_WIDTH), 0.1)
    rwkv_a2 = nrm((L, RWKV_ICLR_RANK, RWKV_WIDTH), 0.1)
    rwkv_g2 = nrm((L, RWKV_GATE_RANK, RWKV_WIDTH), RWKV_GATE_RANK ** -0.5)
    rwkv_k_k = 1.0 + nrm((L, RWKV_WIDTH), 0.1)
    rwkv_k_a = 1.0 + nrm((L, RWKV_WIDTH), 0.1)
    rwkv_r_k = nrm((L, RWKV_HEADS, RWKV_HEAD_DIM), 0.1)
    rwkv_ln_g = gain((L, RWKV_WIDTH))
    rwkv_ln_b = nrm((L, RWKV_WIDTH), 0.02)
    gla_w_a2 = nrm((L, GLA_GATE_RANK, GLA_QK_WIDTH), GLA_GATE_RANK ** -0.5)
    gla_b_a = nrm((L, GLA_QK_WIDTH), 0.1)
    gla_norm_g = gain((L, GLA_WIDTH))
    w_out = nrm((L, MIX_WIDTH, D_MODEL), DEEPNORM_BETA * MIX_WIDTH ** -0.5)
    ln1_g = gain((L, D_MODEL))
    ln1_b = nrm((L, D_MODEL), 0.02)
    moe_w_rg = nrm((L, D_MODEL, N_GROUPS), D_MODEL ** -0.5)
    moe_b_rg = nrm((L, N_GROUPS), 0.01)
    moe_w_re = nrm((L, D_MODEL, N_EXPERTS), D_MODEL ** -0.5)
    moe_b_re = nrm((L, N_EXPERTS), 0.01)
    moe_w_gate = nrm((L, N_EXPERTS, D_MODEL, EXPERT_FF), D_MODEL ** -0.5)
    moe_w_up = nrm((L, N_EXPERTS, D_MODEL, EXPERT_FF), D_MODEL ** -0.5)
    moe_w_down = nrm((L, N_EXPERTS, EXPERT_FF, D_MODEL), DEEPNORM_BETA * EXPERT_FF ** -0.5)
    ln2_g = gain((L, D_MODEL))
    ln2_b = nrm((L, D_MODEL), 0.02)
    return {'x': x, 'ln_in_g': ln_in_g, 'ln_in_b': ln_in_b, 'w_in': w_in,
            'ssd_conv_w': ssd_conv_w, 'ssd_conv_b': ssd_conv_b, 'ssd_dt_bias': ssd_dt_bias,
            'ssd_a_log': ssd_a_log, 'ssd_d': ssd_d, 'ssd_norm_g': ssd_norm_g,
            'rwkv_mu': rwkv_mu, 'rwkv_w0': rwkv_w0, 'rwkv_w2': rwkv_w2, 'rwkv_a0': rwkv_a0,
            'rwkv_a2': rwkv_a2, 'rwkv_g2': rwkv_g2, 'rwkv_k_k': rwkv_k_k, 'rwkv_k_a': rwkv_k_a,
            'rwkv_r_k': rwkv_r_k, 'rwkv_ln_g': rwkv_ln_g, 'rwkv_ln_b': rwkv_ln_b,
            'gla_w_a2': gla_w_a2, 'gla_b_a': gla_b_a, 'gla_norm_g': gla_norm_g,
            'w_out': w_out, 'ln1_g': ln1_g, 'ln1_b': ln1_b,
            'moe_w_rg': moe_w_rg, 'moe_b_rg': moe_b_rg, 'moe_w_re': moe_w_re, 'moe_b_re': moe_b_re,
            'moe_w_gate': moe_w_gate, 'moe_w_up': moe_w_up, 'moe_w_down': moe_w_down,
            'ln2_g': ln2_g, 'ln2_b': ln2_b}

def second_block(x, ln_in_g, ln_in_b, w_in, ssd_conv_w, ssd_conv_b, ssd_dt_bias, ssd_a_log, ssd_d,
              ssd_norm_g, rwkv_mu, rwkv_w0, rwkv_w2, rwkv_a0, rwkv_a2, rwkv_g2, rwkv_k_k, rwkv_k_a,
              rwkv_r_k, rwkv_ln_g, rwkv_ln_b, gla_w_a2, gla_b_a, gla_norm_g, w_out, ln1_g, ln1_b,
              moe_w_rg, moe_b_rg, moe_w_re, moe_b_re, moe_w_gate, moe_w_up, moe_w_down, ln2_g, ln2_b):
    h = layer_norm(x, ln_in_g, ln_in_b)
    for i in range(DEPTH_2):
        mix = hybrid_mixer(h, w_in[i], ssd_conv_w[i], ssd_conv_b[i], ssd_dt_bias[i], ssd_a_log[i],
                           ssd_d[i], ssd_norm_g[i], rwkv_mu[i], rwkv_w0[i], rwkv_w2[i], rwkv_a0[i],
                           rwkv_a2[i], rwkv_g2[i], rwkv_k_k[i], rwkv_k_a[i], rwkv_r_k[i], rwkv_ln_g[i],
                           rwkv_ln_b[i], gla_w_a2[i], gla_b_a[i], gla_norm_g[i], w_out[i])
        h = layer_norm(DEEPNORM_ALPHA * h + mix, ln1_g[i], ln1_b[i])
        ffn = hierarchical_moe(h, moe_w_rg[i], moe_b_rg[i], moe_w_re[i], moe_b_re[i],
                               moe_w_gate[i], moe_w_up[i], moe_w_down[i])
        h = layer_norm(DEEPNORM_ALPHA * h + ffn, ln2_g[i], ln2_b[i])
    return h


def setup_inputs(seed=0):
    out = dict(first_inputs(seed))
    for name, value in second_inputs(seed + 1).items():
        if name != "x":
            out[name + "_2"] = value
    return out


def reference(
    x, c, ctx, c_ctx, mod_w, mod_b, ffn_w_gate, ffn_w_up, ffn_w_down, w_in, hgrn_lb_logits,
    hgrn_norm_w, hyena_conv_w, hyena_conv_b, hyena_w1, hyena_b1, hyena_freq1, hyena_w2,
    hyena_b2, hyena_freq2, hyena_w3, hyena_bias, w_proj_a, w_proj_b, w_out, final_norm_w,
    ln_in_g_2, ln_in_b_2, w_in_2, ssd_conv_w_2, ssd_conv_b_2, ssd_dt_bias_2, ssd_a_log_2,
    ssd_d_2, ssd_norm_g_2, rwkv_mu_2, rwkv_w0_2, rwkv_w2_2, rwkv_a0_2, rwkv_a2_2, rwkv_g2_2,
    rwkv_k_k_2, rwkv_k_a_2, rwkv_r_k_2, rwkv_ln_g_2, rwkv_ln_b_2, gla_w_a2_2, gla_b_a_2,
    gla_norm_g_2, w_out_2, ln1_g_2, ln1_b_2, moe_w_rg_2, moe_b_rg_2, moe_w_re_2, moe_b_re_2,
    moe_w_gate_2, moe_w_up_2, moe_w_down_2, ln2_g_2, ln2_b_2,
):
    x = first_block(
        x, c, ctx, c_ctx, mod_w, mod_b, ffn_w_gate, ffn_w_up, ffn_w_down, w_in, hgrn_lb_logits,
        hgrn_norm_w, hyena_conv_w, hyena_conv_b, hyena_w1, hyena_b1, hyena_freq1, hyena_w2,
        hyena_b2, hyena_freq2, hyena_w3, hyena_bias, w_proj_a, w_proj_b, w_out, final_norm_w,
    )
    return second_block(
        x, ln_in_g_2, ln_in_b_2, w_in_2, ssd_conv_w_2, ssd_conv_b_2, ssd_dt_bias_2, ssd_a_log_2,
        ssd_d_2, ssd_norm_g_2, rwkv_mu_2, rwkv_w0_2, rwkv_w2_2, rwkv_a0_2, rwkv_a2_2, rwkv_g2_2,
        rwkv_k_k_2, rwkv_k_a_2, rwkv_r_k_2, rwkv_ln_g_2, rwkv_ln_b_2, gla_w_a2_2, gla_b_a_2,
        gla_norm_g_2, w_out_2, ln1_g_2, ln1_b_2, moe_w_rg_2, moe_b_rg_2, moe_w_re_2, moe_b_re_2,
        moe_w_gate_2, moe_w_up_2, moe_w_down_2, ln2_g_2, ln2_b_2,
    )


_drawn_inputs = setup_inputs


def setup_inputs(seed=0):
    import zlib

    import numpy as np

    out = dict(_drawn_inputs(seed))
    spreads = {}
    factors = {'ctx': 5.38,
     'c_ctx': 4.169,
     'hgrn_lb_logits': 8.0,
     'hyena_conv_b': 4.546,
     'hyena_freq1': 3.112,
     'hyena_freq2': 4.166,
     'ssd_conv_b_2': 4.879,
     'ssd_norm_g_2': 4.275,
     'rwkv_w2_2': 3.471,
     'rwkv_a0_2': 5.182,
     'rwkv_ln_g_2': 8.0,
     'rwkv_ln_b_2': 6.212,
     'gla_b_a_2': 4.635,
     'gla_norm_g_2': 8.0,
     'moe_b_rg_2': 8.0,
     'moe_b_re_2': 5.254}
    for name, (base, spread) in spreads.items():
        noise = np.random.default_rng([zlib.crc32(name.encode()), seed]).standard_normal(out[name].shape)
        drawn = base * np.exp(spread * noise) if base else spread * noise
        out[name] = jnp.asarray(drawn.astype(out[name].dtype))
    for name, factor in factors.items():
        out[name] = (out[name] * factor).astype(out[name].dtype)
    return out
```

```python
from contextlib import ExitStack
import math

import numpy as np

import concourse.bass as bass
from concourse import mybir

ALU = mybir.AluOpType
ACT = mybir.ActivationFunctionType
AX = mybir.AxisListType
F32 = mybir.dt.float32
F32R = mybir.dt.float32r

P = 128
T = 256
TT = T // P
D = 1024
DT = D // P
CH = 512
SLOT = DT * CH
D_FF = 2816
FT = D_FF // P
N_MOD = 9
HEADS_A = 4
BW = 512
BT = BW // P
RMS_EPS = 1e-6
LN_EPS = 1e-5
HYENA_L1_EPS = 1e-6
LEVELS = 7
STAGE_SEMAPHORES = 160
SLOTS = 4
EXTRA_SLOTS = 2
LOG_FLOOR = 2.0 ** -63

VA_MODB, VA_C, VA_CCTX, VA_FNORM, VA_CONVB, VA_HYB, VA_HNORM = 0, 72, 80, 88, 96, 108, 116
VA_ROWS = 117
VB_CONVW, VB_LB = 0, 36
VB_ROWS = 52


class Chain:

    def __init__(self, eng, sem):
        self.eng, self.sem, self.n = eng, sem, 0

    def __call__(self, ins):
        self.n += 1
        ins.then_inc(self.sem, 1)
        self.eng.wait_ge(self.sem, self.n)


class Ring:

    def __init__(self, ctx, nc, name, buf):
        self.slots, self.buf = buf.shape[1], buf
        self.landed = [ctx.enter_context(nc.semaphore(f"{name}_landed{s}")) for s in range(self.slots)]
        self.used = ctx.enter_context(nc.semaphore(f"{name}_used"))

    def clear(self, nc):
        nc.all_engine_barrier(sems_to_clear=range(self.landed[0].num, self.used.num + 1))

    def view(self, n, a, b):
        return self.buf[:, n % self.slots, 0:a * b].rearrange("p (a b) -> p a b", a=a)

    def load(self, sp, n, src):
        if n >= self.slots:
            sp.wait_ge(self.used, n - self.slots + 1)
        sp.dma_start(self.view(n, src.shape[1], src.shape[2]), src).then_inc(self.landed[n % self.slots], 16)

    def arrived(self, pe, n):
        pe.wait_ge(self.landed[n % self.slots], 16 * (n // self.slots + 1))


class SplitTiles:

    DEPTH = 4

    def __init__(self, ring, first, shapes, high, low, high_ready, low_ready, tile_used):
        self.ring, self.high_part, self.low_part = ring, high, low
        self.high_ready, self.low_ready, self.tile_used = high_ready, low_ready, tile_used
        self.tiles = [(first + c, k, K, cols) for c, (K, cols) in enumerate(shapes) for k in range(K)]

    def __len__(self):
        return len(self.tiles)

    def source(self, q):
        n, k, K, cols = self.tiles[q]
        return self.ring.view(n, K, cols)[:, k, :]

    def parts(self, q):
        cols = self.tiles[q][3]
        return [x[:, (q % self.DEPTH) * CH:(q % self.DEPTH) * CH + cols] for x in (self.high_part, self.low_part)]

    def upper(self, act, q):
        n, k = self.tiles[q][:2]
        if k == 0:
            self.ring.arrived(act, n)
        if q >= self.DEPTH:
            act.wait_ge(self.tile_used, q - self.DEPTH + 1)
        act.activation(self.parts(q)[0], self.source(q), ACT.Copy).then_inc(self.high_ready, 1)

    def lower(self, dve, q):
        dve.wait_ge(self.high_ready, q + 1)
        high, low = self.parts(q)
        dve.tensor_tensor(low, self.source(q), high.bitcast(F32), ALU.subtract).then_inc(self.low_ready, 1)

    def products(self, pe, q, outs, first, last, tokens_out=False):
        n, k, K, cols = self.tiles[q]
        pe.wait_ge(self.low_ready, q + 1)
        high, low = self.parts(q)
        for j, (out, x_high, x_low) in enumerate(outs):
            c = slice(0, cols) if tokens_out else slice(j * P, (j + 1) * P)
            for i, (w, x) in enumerate(((high, x_high), (high, x_low), (low, x_high))):
                w = w[:, c]
                a, b = (x, w) if tokens_out else (w, x)
                ins = pe.matmul(out, a, b, start=(first and i == 0), stop=(last and i == 2))
            if j == 0 and k == K - 1:
                ins.then_inc(self.ring.used, 1)
        ins.then_inc(self.tile_used, 1)


def semaphores(ctx, nc, names):
    sems = [ctx.enter_context(nc.semaphore(n, num=STAGE_SEMAPHORES + i)) for i, n in enumerate(names.split())]
    ctx.callback(lambda: nc.all_engine_barrier(
        sems_to_clear=range(STAGE_SEMAPHORES, STAGE_SEMAPHORES + len(sems))))
    return sems


def column_chunks(w, bounds):
    v = w.rearrange("(k p) n -> p k n", p=P)
    return [v[:, :, a:b] for a, b in bounds]


def down_chunks(w):
    v = w.rearrange("(k p) n -> p k n", p=P)
    return [v[:, a:b, h * CH:(h + 1) * CH] for h in range(2) for a, b in ((0, 8), (8, 16), (16, 22))]


def ffn_chunks(wg, wu, wd):
    bounds = [(a, min(a + CH, D_FF)) for a in range(0, D_FF, CH)]
    out = []
    for g, u in zip(column_chunks(wg, bounds), column_chunks(wu, bounds)):
        out += [g, u]
    return out + down_chunks(wd)


FFN_CHUNKS = 18
WIN_ORDER = [0, 1, 2, 8, 9, 10, 11, 3, 4, 5, 6, 7]


def first_block_chunks(t):
    mod = t["mod_w"][0]
    out = column_chunks(mod, [(a, a + CH) for a in range(0, N_MOD * D, CH)])
    out += ffn_chunks(t["ffn_w_gate"][0, 0], t["ffn_w_up"][0, 0], t["ffn_w_down"][0, 0])
    out += column_chunks(t["w_in"][0], [(CH * c, CH * c + CH) for c in WIN_ORDER])
    out += [t["w_proj_a"][0].rearrange("(k p) n -> p k n", p=P), t["w_proj_b"][0].rearrange("(k p) n -> p k n", p=P)]
    out += column_chunks(t["w_out"][0], [(0, CH), (CH, D)])
    out += ffn_chunks(t["ffn_w_gate"][0, 1], t["ffn_w_up"][0, 1], t["ffn_w_down"][0, 1])
    return out


C_MOD = 0
C_FFN0 = 18
C_WIN = C_FFN0 + FFN_CHUNKS
C_PROJ = C_WIN + 12
C_WOUT = C_PROJ + 2
C_FFN1 = C_WOUT + 2
C_END = C_FFN1 + FFN_CHUNKS


def refill(sp, ring, chunks, first, count):
    for n in range(first + ring.slots, min(first + count + ring.slots, len(chunks))):
        ring.load(sp, n, chunks[n])


def modulation(nc, t, S, ring, chunks):
    ps, ident = S["ps"], S["ident"]
    H, modv, VA, VB, VC = S["H"], S["modv"], S["VA"], S["VB"], S["VC"]
    with ExitStack() as ctx:
        rowsA = ctx.enter_context(nc.sbuf_tensor("rowsA", [P, P], F32))
        rowsB = ctx.enter_context(nc.sbuf_tensor("rowsB", [P, P], F32))
        rowsC = ctx.enter_context(nc.sbuf_tensor("rowsC", [4, 64], F32))
        xin = ctx.enter_context(nc.sbuf_tensor("xin", [P, 2 * TT, D], F32))
        pos = ctx.enter_context(nc.sbuf_tensor("pos", [P, TT, D], F32))
        silc = ctx.enter_context(nc.sbuf_tensor("silc", [P, DT, 32], F32))
        rows = ctx.enter_context(nc.sbuf_tensor("mod_rows", [P, 2, CH], F32))
        fold = ctx.enter_context(nc.sbuf_tensor("fold", [P, 2], F32))
        (ident_in, vec_in, x_in, x_ready, vec_turned, vec_out, silc_zero, c_ready, turned, turned_out, rows_out,
         folded, dve_step) = semaphores(
            ctx, nc, """ident_in vec_in x_in x_ready vec_turned vec_out silc_zero c_ready turned turned_out
            mod_rows_out mod_folded mod_dve_step""")
        block = ctx.enter_context(nc.Block())

        @block.sync
        def _(sp):
            sp.dma_start(ident[:], t["c_ident"]).then_inc(ident_in, 16)
            sp.dma_start(fold[:], t["c_fold"]).then_inc(ident_in, 16)
            row = lambda a, n: a.rearrange("(r c) -> r c", c=n)
            for at, src in ((VA_MODB, row(t["mod_b"][0], P)), (VA_C, row(t["c"][0], P)),
                            (VA_CCTX, row(t["c_ctx"], P)), (VA_FNORM, row(t["final_norm_w"], P)),
                            (VA_CONVB, row(t["hyena_conv_b"][0], P)),
                            (VA_HYB, t["hyena_bias"][0].rearrange("o (r c) -> (o r) c", c=P)),
                            (VA_HNORM, t["hgrn_norm_w"])):
                sp.dma_start(rowsA[at:at + src.shape[0], :], src).then_inc(vec_in, 16)
            for at, src in ((VB_CONVW, t["hyena_conv_w"][0].rearrange("j (r c) -> (j r) c", c=P)),
                            (VB_LB, t["hgrn_lb_logits"].rearrange("l d (r c) -> (l d r) c", c=P))):
                sp.dma_start(rowsB[at:at + src.shape[0], :], src).then_inc(vec_in, 16)
            for i, name in enumerate(("hyena_b1", "hyena_freq1", "hyena_b2", "hyena_freq2")):
                sp.dma_start(rowsC[i:i + 1, :], t[name]).then_inc(vec_in, 16)
            sp.dma_start(xin[:, 0:TT, :], t["x"][0].rearrange("(a p) d -> p a d", p=P)).then_inc(x_in, 16)
            sp.dma_start(xin[:, TT:2 * TT, :], t["ctx"][0].rearrange("(a p) d -> p a d", p=P)).then_inc(x_in, 16)
            sp.dma_start(pos[:], t["c_pos"].rearrange("(a p) d -> p a d", p=P)).then_inc(x_in, 16)
            for n in range(ring.slots):
                ring.load(sp, n, chunks[n])
            refill(sp, ring, chunks, C_MOD, 18)

        @block.vector
        def _(dve):
            dve.memset(silc[:], 0.0).then_inc(silc_zero, 1)
            dve.wait_ge(x_in, 48)
            dve.tensor_tensor(xin[:, 0:TT, :], xin[:, 0:TT, :], pos[:], ALU.add).then_inc(x_ready, 1)
            dve.wait_ge(vec_turned, 1)
            dve.tensor_copy(VA[:], ps[:, 7, 0:VA_ROWS]).then_inc(vec_out, 1)
            dve.tensor_copy(VB[:], ps[:, 7, 128:128 + VB_ROWS]).then_inc(vec_out, 1)
            dve.tensor_copy(VC[:], ps[0:64, 7, 256:260]).then_inc(vec_out, 1)
            for i in range(2 * TT * DT // 4):
                a, d = i // 2, 4 * (i % 2)
                dve.wait_ge(turned, i + 1)
                dve.tensor_copy(H[:, d:d + 4, a * P:(a + 1) * P],
                                ps[:, 1 + i % 4, :].rearrange("p (d t) -> p d t", d=4)).then_inc(turned_out, 1)
            for n in range(18):
                dve.wait_ge(ring.used, n + 1)
                if n >= 2:
                    dve.wait_ge(folded, n - 1)
                dve.tensor_copy(rows[:, n % 2, :], ps[:, 5 + n % 2, :]).then_inc(rows_out, 1)
            dve.wait_ge(vec_out, 3)
            dve.wait_ge(folded, 18)
            raw = ps[:, 0, 0:2 * N_MOD * DT].rearrange("p (m s) -> p m s", s=2)
            step = Chain(dve, dve_step)
            for s in range(2):
                ins = dve.tensor_tensor(modv[:, s, :], raw[:, :, s], VA[:, VA_MODB:VA_MODB + 72], ALU.add)
            step(ins)
            for part in (1, 4, 7):
                v = modv[:, :, part * DT:(part + 1) * DT]
                dve.tensor_scalar(v, v, 1.0, None, ALU.add)
            for part in (2, 8):
                v = modv[:, :, part * DT:(part + 1) * DT]
                ins = dve.tensor_scalar(v, v, 0.5, None, ALU.mult)
            step(ins)

        @block.scalar
        def _(act):
            act.wait_ge(vec_out, 1)
            act.wait_ge(silc_zero, 1)
            act.activation(silc[:, :, 0:2], VA[:, VA_C:VA_C + 2 * DT].rearrange("p (s k) -> p k s", s=2),
                           ACT.Silu).then_inc(c_ready, 1)

        @block.tensor
        def _(pe):
            pe.wait_ge(ident_in, 32)
            pe.wait_ge(vec_in, 16 * 13)
            pe.transpose(ps[:, 7, 0:VA_ROWS], rowsA[0:VA_ROWS, :], ident[0:VA_ROWS, 0:VA_ROWS])
            pe.transpose(ps[:, 7, 128:128 + VB_ROWS], rowsB[0:VB_ROWS, :], ident[0:VB_ROWS, 0:VB_ROWS])
            pe.transpose(ps[0:64, 7, 256:260], rowsC[:, :], ident[0:4, 0:4]).then_inc(vec_turned, 1)
            pe.wait_ge(x_ready, 1)
            for i in range(2 * TT * DT // 4):
                a, d = i // 2, 4 * (i % 2)
                if i >= 4:
                    pe.wait_ge(turned_out, i - 3)
                for j in range(4):
                    ins = pe.transpose(ps[:, 1 + i % 4, j * P:(j + 1) * P], xin[:, a, (d + j) * P:(d + j + 1) * P],
                                       ident[:])
                ins.then_inc(turned, 1)
            pe.wait_ge(c_ready, 1)

            def fold_rows(n):
                pe.wait_ge(rows_out, n + 1)
                for m in range(4 * n, 4 * n + 4):
                    ins = pe.matmul(ps[:, 0, 2 * m:2 * m + 2], rows[:, n % 2, (m % 4) * P:(m % 4 + 1) * P], fold[:],
                                    start=True, stop=True)
                ins.then_inc(folded, 1)

            for n in range(18):
                ring.arrived(pe, n)
                if n >= 2:
                    pe.wait_ge(rows_out, n - 1)
                w = ring.view(n, DT, CH)
                for k in range(DT):
                    g = k % 4
                    ins = pe.matmul(ps[32 * g:32 * g + 32, 5 + n % 2, :], silc[:, k, :], w[:, k, :],
                                    start=(k < 4), stop=(k >= 4))
                ins.then_inc(ring.used, 1)
                if n:
                    fold_rows(n - 1)
            fold_rows(17)


def norm_modulate(nc, S, W, part, name, room=None):
    ps, ones, H, modv, NH, NL = S["ps"], S["ones"], S["H"], S["modv"], S["NH"], S["NL"]
    with ExitStack() as ctx:
        rstd = ctx.enter_context(nc.sbuf_tensor(f"{name}_rstd", [P, W], F32))
        N = room if room is not None else ctx.enter_context(nc.sbuf_tensor(f"{name}_n", [P, DT, W], F32))
        squares, summed, mean_ready, root_ready, dve_step, scaled, act_step, high_ready = semaphores(
            ctx, nc, " ".join(f"{name}_{s}" for s in
                              "squares summed mean_ready root_ready dve_step scaled act_step high_ready".split()))
        block = ctx.enter_context(nc.Block())

        @block.scalar
        def _(act):
            for d in range(DT):
                act.activation(N[:, d, 0:W], H[:, d, 0:W], ACT.Square).then_inc(squares, 1)
            act.wait_ge(mean_ready, 1)
            act.activation(rstd[:], rstd[:], ACT.Sqrt).then_inc(root_ready, 1)
            for d in range(DT):
                act.wait_ge(scaled, d + 1)
                for s in range(W // T):
                    v = N[:, d, s * T:(s + 1) * T]
                    ins = act.activation(v, v, ACT.Identity, scale=modv[:, s, (part + 1) * DT + d:(part + 1) * DT + d + 1],
                                         bias=modv[:, s, part * DT + d:part * DT + d + 1])
                ins.then_inc(act_step, 1)
                if d:
                    act.wait_ge(act_step, d)
                    act.activation(NH[:, d - 1, 0:W], N[:, d - 1, 0:W], ACT.Copy).then_inc(high_ready, 1)
            act.wait_ge(act_step, DT)
            act.activation(NH[:, DT - 1, 0:W], N[:, DT - 1, 0:W], ACT.Copy).then_inc(high_ready, 1)

        @block.tensor
        def _(pe):
            for d in range(DT):
                pe.wait_ge(squares, d + 1)
                ins = pe.matmul(ps[:, 0, 0:W], ones[:], N[:, d, 0:W], start=(d == 0), stop=(d == DT - 1))
            ins.then_inc(summed, 1)

        @block.vector
        def _(dve):
            step = Chain(dve, dve_step)
            dve.wait_ge(summed, 1)
            dve.tensor_scalar(rstd[:], ps[:, 0, 0:W], 1.0 / D, RMS_EPS, ALU.mult, ALU.add).then_inc(mean_ready, 1)
            dve.wait_ge(root_ready, 1)
            step(dve.reciprocal(rstd[:], rstd[:]))
            for d in range(DT):
                dve.tensor_tensor(N[:, d, 0:W], H[:, d, 0:W], rstd[:], ALU.mult).then_inc(scaled, 1)
            for d in range(DT):
                dve.wait_ge(high_ready, d + 1)
                dve.tensor_tensor(NL[:, d, 0:W], N[:, d, :], NH[:, d, 0:W].bitcast(F32), ALU.subtract)


def feed_forward(nc, S, ring, chunks, W, part, base, name):
    ps, H, NH, NL, modv = S["ps"], S["H"], S["NH"], S["NL"], S["modv"]
    GROUPS = -(-FT // 4)
    tiles_of = lambda g: range(4 * g, min(4 * g + 4, FT))
    GATED = 2 * GROUPS * DT
    with ExitStack() as ctx:
        hid = ctx.enter_context(nc.sbuf_tensor(f"{name}_hid", [P, FT, W], F32))
        sg = S["X"][:].rearrange("p a (b n) -> p (a b) n", b=2)[:, :, 0:W]
        hid_high = ctx.enter_context(nc.sbuf_tensor(f"{name}_hid_high", [P, 4, W], F32R))
        hid_low = ctx.enter_context(nc.sbuf_tensor(f"{name}_hid_low", [P, 4, W], F32R))
        high_ready, low_ready, tile_used, silu_ready, hid_ready, hid_high_ready, hid_low_ready = semaphores(
            ctx, nc, " ".join(f"{name}_{s}" for s in """high_ready low_ready tile_used silu_ready hid_ready
            hid_high_ready hid_low_ready""".split()))
        block = ctx.enter_context(nc.Block())
        shapes = [(DT, P * len(tiles_of(g))) for g in range(GROUPS) for _ in range(2)] + [(8, CH), (8, CH), (6, CH)] * 2
        W_ = SplitTiles(ring, base, shapes, S["w_high"], S["w_low"], high_ready, low_ready, tile_used)

        @block.sync
        def _(sp):
            refill(sp, ring, chunks, base, FFN_CHUNKS)

        @block.tensor
        def _(pe):
            for g in range(GROUPS):
                for u in range(2):
                    if g:
                        pe.wait_ge((silu_ready, hid_ready)[u], 4 * g)
                    for k in range(DT):
                        outs = [(ps[:, 4 * u + j, 0:W], NH[:, k, 0:W], NL[:, k, 0:W]) for j in range(len(tiles_of(g)))]
                        W_.products(pe, (2 * g + u) * DT + k, outs, k == 0, k == DT - 1)
            for half in range(2):
                pe.wait_ge((silu_ready, hid_ready)[half], FT)
                for k in range(FT):
                    r = half * FT + k
                    pe.wait_ge(hid_low_ready, r + 1)
                    outs = [(ps[:, 4 * half + d, 0:W], hid_high[:, r % 4, :], hid_low[:, r % 4, :]) for d in range(4)]
                    W_.products(pe, GATED + r, outs, k == 0, k == FT - 1)

        @block.scalar
        def _(act):
            for q in range(len(W_)):
                W_.upper(act, q)
                g, at = divmod(q, 2 * DT)
                if q < GATED and at == DT + 4:
                    act.wait_ge(tile_used, (2 * g + 1) * DT)
                    if g:
                        act.wait_ge(hid_ready, 4 * g)
                    for i in tiles_of(g):
                        act.activation(sg[:, i % 4, :], ps[:, i % 4, 0:W], ACT.Silu).then_inc(silu_ready, 1)
                if q >= GATED:
                    r = q - GATED
                    act.wait_ge(hid_ready, r % FT + 1)
                    act.activation(hid_high[:, r % 4, :], hid[:, r % FT, :], ACT.Copy).then_inc(hid_high_ready, 1)

        @block.vector
        def _(dve):
            def add_output(half):
                dve.wait_ge(tile_used, GATED + (half + 1) * FT)
                for d in range(4):
                    m = 4 * half + d
                    for s in range(W // T):
                        v = H[:, m, s * T:(s + 1) * T]
                        dve.scalar_tensor_tensor(v, ps[:, m, s * T:(s + 1) * T],
                                                 modv[:, s, part * DT + m:part * DT + m + 1], v, ALU.mult, ALU.add)

            for q in range(len(W_)):
                W_.lower(dve, q)
                if q >= GATED:
                    r = q - GATED
                    dve.wait_ge(hid_high_ready, r + 1)
                    dve.tensor_tensor(hid_low[:, r % 4, :], hid[:, r % FT, :], hid_high[:, r % 4, :].bitcast(F32),
                                      ALU.subtract).then_inc(hid_low_ready, 1)
                g, at = divmod(q - 2 * DT, 2 * DT)
                if 0 <= g < GROUPS and at == 4:
                    dve.wait_ge(tile_used, (2 * g + 2) * DT)
                    for i in tiles_of(g):
                        dve.wait_ge(silu_ready, i + 1)
                        dve.tensor_tensor(hid[:, i, :], sg[:, i % 4, :], ps[:, 4 + i % 4, 0:W],
                                          ALU.mult).then_inc(hid_ready, 1)
                if q == GATED + FT + 4:
                    add_output(0)
            add_output(1)


WIN_KINDS = [("v", 0), ("f0", 0), ("f1", 0), ("merge", 0), ("merge", 4), ("merge", 8), ("merge", 12), ("q", 0), ("g", 0),
             ("hy", 0), ("hy", 4), ("hy", 8)]
DVE_KINDS = ("v", "hy")


def input_projection(nc, S, ring, chunks):
    ps, NH, NL = S["ps"], S["NH"], S["NL"]
    V, SG, MG, Q, G, HY = S["V"], S["SG"], S["MG"], S["Q"], S["G"], S["HY"]
    with ExitStack() as ctx:
        high_ready, low_ready, tile_used, act_out, dve_out = semaphores(
            ctx, nc, "win_high_ready win_low_ready win_tile_used win_act_out win_dve_out")
        block = ctx.enter_context(nc.Block())
        W_ = SplitTiles(ring, C_WIN, [(DT, CH)] * len(WIN_KINDS), S["w_high"], S["w_low"], high_ready, low_ready, tile_used)
        by_dve = [kind in DVE_KINDS for kind, _ in WIN_KINDS]
        bank = lambda c, j: 4 * (c % 2) + j

        @block.sync
        def _(sp):
            refill(sp, ring, chunks, C_WIN, 12)

        @block.tensor
        def _(pe):
            for c, (kind, _) in enumerate(WIN_KINDS):
                if c >= 2:
                    pe.wait_ge(dve_out if by_dve[c - 2] else act_out, by_dve[:c - 1].count(by_dve[c - 2]))
                W = 2 * T if kind in ("f0", "f1") else T
                for k in range(DT):
                    if kind == "v":
                        outs = [(ps[:, bank(c, j), :], NH[:, k, j * P:(j + 1) * P], NL[:, k, j * P:(j + 1) * P])
                                for j in range(2 * TT)]
                    else:
                        outs = [(ps[:, bank(c, j), 0:W], NH[:, k, 0:W], NL[:, k, 0:W]) for j in range(4)]
                    W_.products(pe, c * DT + k, outs, k == 0, k == DT - 1, tokens_out=(kind == "v"))

        @block.scalar
        def _(act):
            def take(c):
                kind, first = WIN_KINDS[c]
                act.wait_ge(tile_used, (c + 1) * DT)
                for j in range(4):
                    src = ps[:, bank(c, j), :]
                    if kind in ("f0", "f1"):
                        ins = act.activation(SG[:, int(kind[1]), j, :], src, ACT.Sigmoid)
                    elif kind == "merge":
                        ins = act.activation(MG[:, first + j, :], src[:, 0:T], ACT.Sigmoid)
                    else:
                        ins = act.activation((Q if kind == "q" else G)[:, j, :], src[:, 0:T], ACT.Silu)
                ins.then_inc(act_out, 1)

            for q in range(len(W_)):
                W_.upper(act, q)
                c, at = divmod(q, DT)
                if at == 4 and c and not by_dve[c - 1]:
                    take(c - 1)

        @block.vector
        def _(dve):
            def take(c):
                kind, first = WIN_KINDS[c]
                dve.wait_ge(tile_used, (c + 1) * DT)
                for j in range(4):
                    if kind == "v":
                        ins = dve.tensor_copy(V[:, j, :], ps[:, bank(c, j), :])
                    else:
                        ins = dve.tensor_copy(HY[:, first + j, 1:T + 1], ps[:, bank(c, j), 0:T])
                ins.then_inc(dve_out, 1)

            dve.memset(HY[:, :, 0:1], 0.0)
            dve.memset(HY[:, :, T + 1:T + 2], 0.0)
            for q in range(len(W_)):
                W_.lower(dve, q)
                c, at = divmod(q, DT)
                if at == 4 and c and by_dve[c - 1]:
                    take(c - 1)
            take(len(WIN_KINDS) - 1)


def block_differences(dve, out, cum, size, backward):
    half = size // 2
    v = cum.rearrange("p (n s) -> p n s", s=size)
    o = out.rearrange("p (n s) -> p n s", s=size)
    m = half if backward else half - 1
    ref = v[:, :, m:m + 1].to_broadcast([P, v.shape[1], half])
    late, early = (slice(0, half), slice(half, size)) if backward else (slice(half, size), slice(0, half))
    dve.tensor_tensor(o[:, :, late], v[:, :, late], ref, ALU.subtract)
    return dve.tensor_tensor(o[:, :, early], ref, v[:, :, early], ALU.subtract)


def hgrn2(nc, S):
    ps, ident, ones, VA, VB = S["ps"], S["ident"], S["ones"], S["VA"], S["VB"]
    V, SG, Q, G = S["V"], S["SG"], S["Q"], S["G"]
    NL = LEVELS + 1
    with ExitStack() as ctx:
        sb = lambda n, s: ctx.enter_context(nc.sbuf_tensor(f"hg_{n}", s, F32))
        lbv = sb("lb", [P, 8])
        lb1 = sb("lb1", [P, 8])
        cum = S["N"][:].rearrange("p (r h) t -> p r h t", r=2)         
        keep = sb("keep", [P, T])
        EB = sb("EB", [P, 2, NL, T])
        prod = sb("prod", [P, 2, NL * P])
        cross = sb("cross", [P, 2, P])
        spare = S["X"][:].rearrange("p a d -> p (a d)")
        kd, kdt, qc = (spare[:, 512 * i:512 * (i + 1)].rearrange("p (a t) -> p a t", a=2) for i in range(3))
        sq, rs = spare[:, 1536:1792], spare[:, 1792:2048]
        s0 = sb("s0", [P, 2, P])
        on = sb("on", [P, T])
        masks = S["masks"]
        (lb_diff, lb_ready, masks_in, f_ready, log_ready, cum_ready, diff_ready, e_ready, ctx_decay, eb_ready, kd_ready,
         q_decay, kd_turned, kdt_ready, s0_made, s0_out, scores, prod_ready, cross_done, o_done, sq_ready,
         summed, mean_ready, root_ready, head_done, act_step, dve_step, pool_step) = semaphores(
            ctx, nc, " ".join(f"hg_{s}" for s in """lb_diff lb_ready masks_in f_ready log_ready cum_ready diff_ready
            e_ready ctx_decay eb_ready kd_ready q_decay kd_turned kdt_ready s0_made s0_out scores prod_ready
            cross_done o_done sq_ready summed mean_ready root_ready head_done act_step dve_step pool_step""".split()))
        block = ctx.enter_context(nc.Block())
        HD = [(h, r) for h in range(HEADS_A) for r in range(2)]

        @block.sync
        def _(sp):
            sp.dma_start(masks[:], S["t"]["c_masks"].rearrange("p (r l c) -> p r l c", r=2, l=NL)).then_inc(masks_in, 16)

        @block.vector
        def _(dve):
            step = Chain(dve, dve_step)
            dve.memset(keep[:], 1.0)
            dve.tensor_tensor(lbv[:], VB[:, VB_LB:VB_LB + 8], VB[:, VB_LB + 8:VB_LB + 16],
                              ALU.subtract).then_inc(lb_diff, 1)
            dve.wait_ge(lb_ready, 1)
            step(dve.tensor_scalar(lb1[:], lbv[:], -1.0, 1.0, ALU.mult, ALU.add))
            for h, r in HD:
                c = 4 * r + h
                ins = dve.tensor_scalar(SG[:, r, h, :], SG[:, r, h, :], lb1[:, c:c + 1], lbv[:, c:c + 1], ALU.mult, ALU.add)
            step(ins)
            for r in range(2):
                ins = dve.tensor_scalar(cum[:, r], SG[:, r], LOG_FLOOR, None, ALU.max)
                ins.then_inc(f_ready, 1)
            for r in range(2):
                dve.tensor_scalar(SG[:, r], SG[:, r], -1.0, 1.0, ALU.mult, ALU.add)
            for r in range(2):
                dve.wait_ge(log_ready, r + 1)
                for h in range(HEADS_A):
                    v = cum[:, r, h, :]
                    for s in range(2):
                        w = v[:, s * T:(s + 1) * T]
                        w = w[:, ::-1] if r else w
                        ins = dve.tensor_tensor_scan(w, keep[:], w, 0.0, ALU.mult, ALU.add)
            ins.then_inc(cum_ready, 1)
            dve.wait_ge(cum_ready, 1)

            def differences(x):
                h, r = HD[x]
                if x >= 2:
                    dve.wait_ge(scores, 3 * (x - 1))
                for l in range(NL):
                    ins = block_differences(dve, EB[:, x % 2, l, :], cum[:, r, h, 0:T], 2 << l, r)
                ins.then_inc(diff_ready, 1)

            def merge_kq(x):
                h, r = HD[x]
                dve.wait_ge(e_ready, x + 1)
                for l in range(NL):
                    s = 1 << l
                    e = EB[:, x % 2, l, :].rearrange("p (n two s) -> p n two s", two=2, s=s)
                    kv = SG[:, r, h, 0:T].rearrange("p (n two s) -> p n two s", two=2, s=s)
                    qv = Q[:, h, :].rearrange("p (n two s) -> p n two s", two=2, s=s)
                    dve.tensor_tensor(e[:, :, r, :], e[:, :, r, :], kv[:, :, r, :], ALU.mult)
                    ins = dve.tensor_tensor(e[:, :, 1 - r, :], e[:, :, 1 - r, :], qv[:, :, 1 - r, :], ALU.mult)
                ins.then_inc(eb_ready, 1)
                dve.wait_ge(ctx_decay, x + 1)
                dve.tensor_tensor(kd[:, x % 2, :], kd[:, x % 2, :], SG[:, r, h, T:2 * T], ALU.mult).then_inc(kd_ready, 1)
                dve.tensor_tensor(qc[:, x % 2, :], qc[:, x % 2, :], Q[:, h, :], ALU.mult).then_inc(q_decay, 1)

            def context_state(x):
                dve.wait_ge(kd_turned, x + 1)
                if x >= 2:
                    dve.wait_ge(s0_made, x - 1)
                dve.tensor_copy(kdt[:, x % 2, :], ps[:, 4, 0:T]).then_inc(kdt_ready, 1)
                dve.wait_ge(s0_made, x + 1)
                if x >= 2:
                    dve.wait_ge(cross_done, 3 * (x - 2) + 1)
                dve.tensor_copy(s0[:, x % 2, :], ps[:, 4, T:T + P]).then_inc(s0_out, 1)

            def mask(x):
                h, r = HD[x]
                for tt in range(TT):
                    y = 2 * x + tt
                    dve.wait_ge(scores, 3 * x + tt + 1)
                    if y >= 2:
                        dve.wait_ge(prod_ready, y - 1)
                        dve.wait_ge(cross_done, 3 * ((y - 2) // 2) + (y - 2) % 2 + 1)
                    dve.tensor_tensor(prod[:, y % 2, :], ps[:, 2 * (y % 2):2 * (y % 2) + 2, :].rearrange("p a b -> p (a b)"),
                                      masks[:, r].rearrange("p l c -> p (l c)"), ALU.mult).then_inc(prod_ready, 1)
                dve.wait_ge(scores, 3 * x + 3)
                if x >= 2:
                    dve.wait_ge(cross_done, 3 * (x - 1))
                dve.tensor_copy(cross[:, x % 2, :], ps[:, 4, T + P:T + 2 * P]).then_inc(s0_out, 1)

            def normalise(h):
                dve.wait_ge(summed, h + 1)
                dve.tensor_scalar(rs, ps[:, 7, 0:T], 1.0 / P, RMS_EPS, ALU.mult, ALU.add).then_inc(mean_ready, 1)
                dve.wait_ge(root_ready, h + 1)
                step(dve.reciprocal(rs, rs))
                step(dve.tensor_tensor(on[:], ps[:, 5 + h % 2, 0:T], rs, ALU.mult))
                dve.scalar_tensor_tensor(G[:, h, :], on[:], VA[:, VA_HNORM:VA_HNORM + 1], G[:, h, :],
                                         ALU.mult, ALU.mult).then_inc(head_done, 1)

            differences(0)
            for x in range(8):
                if x + 1 < 8:
                    differences(x + 1)
                merge_kq(x)
                context_state(x)
                mask(x)
                if x % 2 == 1 and x >= 3:
                    normalise(x // 2 - 1)
            normalise(3)

        @block.scalar
        def _(act):
            def norm_act(h):
                act.wait_ge(cross_done, 3 * (2 * h + 2))
                act.activation(sq, ps[:, 5 + h % 2, 0:T], ACT.Square).then_inc(sq_ready, 1)
                act.wait_ge(mean_ready, h + 1)
                act.activation(rs, rs, ACT.Sqrt).then_inc(root_ready, 1)

            act.wait_ge(lb_diff, 1)
            act.activation(lbv[:], lbv[:], ACT.Sigmoid).then_inc(lb_ready, 1)
            for r in range(2):
                act.wait_ge(f_ready, r + 1)
                act.activation(cum[:, r], cum[:, r], ACT.Ln).then_inc(log_ready, 1)
            act.wait_ge(cum_ready, 1)
            for x, (h, r) in enumerate(HD):
                act.wait_ge(diff_ready, x + 1)
                act.activation(EB[:, x % 2], EB[:, x % 2], ACT.Exp).then_inc(e_ready, 1)
                if x >= 2:
                    act.wait_ge(kd_turned, x - 1)
                    act.wait_ge(cross_done, 3 * (x - 1))
                end = T if r else 2 * T - 1
                act.activation(kd[:, x % 2, :], cum[:, r, h, T:2 * T], ACT.Exp, scale=-1.0, bias=cum[:, r, h, end:end + 1])
                act.activation(qc[:, x % 2, :], cum[:, r, h, 0:T], ACT.Exp).then_inc(ctx_decay, 1)
                if x % 2 == 1 and x >= 3:
                    norm_act(x // 2 - 1)
            norm_act(3)

        @block.tensor
        def _(pe):
            def state_part(x):
                h, r = HD[x]
                pe.wait_ge(kd_ready, x + 1)
                if x >= 1:
                    pe.wait_ge(s0_out, 2 * x)
                for s in range(TT):
                    ins = pe.transpose(ps[:, 4, s * P:(s + 1) * P], kd[:, x % 2, s * P:(s + 1) * P], ident[:])
                ins.then_inc(kd_turned, 1)
                pe.wait_ge(kdt_ready, x + 1)
                for s in range(TT):
                    ins = pe.matmul(ps[:, 4, T:T + P], kdt[:, x % 2, s * P:(s + 1) * P],
                                    V[:, TT + s, h * P:(h + 1) * P], start=(s == 0), stop=(s == TT - 1))
                ins.then_inc(s0_made, 1)

            def score_part(x):
                h, r = HD[x]
                pe.wait_ge(eb_ready, x + 1)
                for tt in range(TT):
                    y = 2 * x + tt
                    if y >= 2:
                        pe.wait_ge(prod_ready, y - 1)
                    c = slice(tt * P, (tt + 1) * P)
                    for l in range(NL):
                        a, b = (SG[:, r, h, c], Q[:, h, c]) if l == 0 else (EB[:, x % 2, l - 1, c],) * 2
                        ins = pe.matmul(ps[:, 2 * (y % 2) + l // 4, (l % 4) * P:(l % 4 + 1) * P], a, b,
                                        start=True, stop=True)
                    ins.then_inc(scores, 1)
                early, late = (slice(P, T), slice(0, P)) if r else (slice(0, P), slice(P, T))
                pe.wait_ge(s0_out, 2 * x + 1)
                pe.matmul(ps[:, 4, T + P:T + 2 * P], EB[:, x % 2, NL - 1, early], EB[:, x % 2, NL - 1, late],
                          start=True, stop=True).then_inc(scores, 1)

            def out_part(x):
                h, r = HD[x]
                bank = 5 + h % 2
                if r == 0 and h >= 2:
                    pe.wait_ge(head_done, h - 1)
                pe.wait_ge(q_decay, x + 1)
                pe.matmul(ps[:, bank, 0:T], s0[:, x % 2, :], qc[:, x % 2, :], start=(r == 0), stop=False,
                          skip_group_check=True)
                for tt in range(TT):
                    y = 2 * x + tt
                    pe.wait_ge(prod_ready, y + 1)
                    for l in range(NL):
                        ins = pe.matmul(ps[:, bank, tt * P:(tt + 1) * P], V[:, tt, h * P:(h + 1) * P],
                                        prod[:, y % 2, l * P:(l + 1) * P], start=False, stop=False, skip_group_check=True)
                    ins.then_inc(cross_done, 1)
                early, late = (1, 0) if r else (0, 1)
                pe.wait_ge(s0_out, 2 * x + 2)
                pe.matmul(ps[:, bank, late * P:(late + 1) * P], V[:, early, h * P:(h + 1) * P], cross[:, x % 2, :],
                          start=False, stop=(r == 1), skip_group_check=True).then_inc(cross_done, 1)

            def norm_part(h):
                pe.wait_ge(sq_ready, h + 1)
                if h >= 1:
                    pe.wait_ge(mean_ready, h)
                pe.matmul(ps[:, 7, 0:T], ones[:], sq, start=True, stop=True).then_inc(summed, 1)

            pe.wait_ge(masks_in, 16)
            for x in range(8):
                state_part(x)
                score_part(x)
                out_part(x)
                if x % 2 == 1 and x >= 3:
                    norm_part(x // 2 - 1)
            norm_part(3)


TWO_PI_PARTS = (6.28125, 0.0019353071693331003, 2 * math.pi - 6.28125 - 0.0019353071693331003)
ROUND = 1.5 * 2.0 ** 23
PI_INSIDE = 3.1415925


def hyena_filters(nc, S):
    ps, ones, VC, t = S["ps"], S["ones"], S["VC"], S["t"]
    CF, KS = S["CF"], S["KS"]
    with ExitStack() as ctx:
        sb = lambda n, s: ctx.enter_context(nc.sbuf_tensor(f"hf_{n}", s, F32))
        CG = sb("CG", [P, TT, 2 * T])
        feat = sb("feat", [33, T])
        window = sb("window", [P, TT, BW])
        w1, w2 = sb("w1", [33, 64]), sb("w2", [64, 64])
        w3 = S["V"][0:64].rearrange("p a b -> p (a b)")
        arg, rnd, hid = sb("arg", [64, T]), sb("rnd", [64, T]), sb("hid", [64, T])
        hk = S["X"][:].rearrange("p a (b n) -> p (a b) n", b=2)
        mag = sb("mag", [P, 2, BW])
        rn = sb("rn", [P, BW])
        (consts, lin, arg_ready, sin_ready, taps_lin, taps_ready, mag_ready, mag_read, scaled,
         spectrum, spectrum_out, dve_step) = semaphores(
            ctx, nc, " ".join(f"hf_{s}" for s in """consts lin arg_ready sin_ready taps_lin taps_ready mag_ready
            mag_read scaled spectrum spectrum_out dve_step""".split()))
        block = ctx.enter_context(nc.Block())

        @block.sync
        def _(sp):
            tiled = lambda a: a.rearrange("(a p) n -> p a n", p=P)
            for dst, src in ((feat[:], t["c_feat"]), (w1[:], t["hyena_w1"][0]), (w2[:], t["hyena_w2"][0]),
                             (w3, t["hyena_w3"][0]), (window[:], tiled(t["c_window"])), (CF[:], tiled(t["c_cf"])),
                             (CG[:], tiled(t["c_cg"])), (S["CI"][:], tiled(t["c_ci"]))):
                sp.dma_start(dst, src).then_inc(consts, 16)

        @block.tensor
        def _(pe):
            pe.wait_ge(consts, 128)
            pe.matmul(ps[0:64, 0, 0:T], w1[:], feat[:], start=True, stop=True).then_inc(lin, 1)
            pe.wait_ge(sin_ready, 1)
            pe.matmul(ps[0:64, 0, 0:T], w2[:], hid[:], start=True, stop=True).then_inc(lin, 1)
            pe.wait_ge(sin_ready, 2)
            for o in range(2):
                for i in range(4):
                    r, tt = i // 2, i % 2
                    if o:
                        pe.wait_ge(taps_ready, i + 1)
                    pe.matmul(ps[:, i, :], hid[:, tt * P:(tt + 1) * P], w3[:, (2 * o + r) * BW:(2 * o + r + 1) * BW],
                              start=True, stop=True).then_inc(taps_lin, 1)
                if o:
                    pe.wait_ge(scaled, 1)
                for i in range(4):
                    pe.wait_ge(mag_ready, 4 * o + i + 1)
                    pe.matmul(ps[:, 4, :], ones[:], mag[:, i % 2, :], start=(i == 0), stop=(i == 3)).then_inc(mag_read, 1)
                pe.wait_ge(scaled, o + 1)
                if o:
                    pe.wait_ge(spectrum_out, 4)
                for m in range(4):
                    bank = 5 + m % 3
                    if m == 3 or o:
                        pe.wait_ge(spectrum_out, 4 * o + max(m - 2, 0))
                    for i in range(4):
                        basis = (CF, CG)[i // 2]
                        ins = pe.matmul(ps[:, bank, :], basis[:, i % 2, m * P:(m + 1) * P], hk[:, i, :],
                                        start=(i == 0), stop=(i == 3))
                    ins.then_inc(spectrum, 1)

        @block.vector
        def _(dve):
            step = Chain(dve, dve_step)
            for layer in range(2):
                dve.wait_ge(lin, layer + 1)
                b, fr = VC[:, 2 * layer:2 * layer + 1], VC[:, 2 * layer + 1:2 * layer + 2]
                step(dve.tensor_scalar(arg[:], ps[0:64, 0, 0:T], b, fr, ALU.add, ALU.mult))
                step(dve.tensor_scalar(rnd[:], arg[:], 1.0 / (2 * math.pi), ROUND, ALU.mult, ALU.add))
                step(dve.tensor_scalar(rnd[:], rnd[:], ROUND, None, ALU.subtract))
                for part in TWO_PI_PARTS:
                    step(dve.scalar_tensor_tensor(arg[:], rnd[:], -part, arg[:], ALU.mult, ALU.add))
                dve.tensor_scalar(arg[:], arg[:], PI_INSIDE, -PI_INSIDE, ALU.min, ALU.max).then_inc(arg_ready, 1)
            for o in range(2):
                for i in range(4):
                    dve.wait_ge(taps_lin, 4 * o + i + 1)
                    if o:
                        dve.wait_ge(spectrum, 4)
                    dve.tensor_tensor(hk[:, i, :], ps[:, i, :], window[:, i % 2, :], ALU.mult).then_inc(taps_ready, 1)
                dve.wait_ge(mag_read, 4 * o + 4)
                step(dve.tensor_scalar(rn[:], ps[:, 4, :], HYENA_L1_EPS, None, ALU.add))
                step(dve.reciprocal(rn[:], rn[:]))
                dve.wait_ge(taps_ready, 4 * o + 4)
                dve.tensor_tensor(hk, hk, rn[:].unsqueeze(1).to_broadcast([P, 4, BW]), ALU.mult).then_inc(scaled, 1)

        @block.scalar
        def _(act):
            for layer in range(2):
                act.wait_ge(arg_ready, layer + 1)
                act.activation(hid[:], arg[:], ACT.Sin).then_inc(sin_ready, 1)
            for o in range(2):
                for i in range(4):
                    act.wait_ge(taps_ready, 4 * o + i + 1)
                    if 4 * o + i >= 2:
                        act.wait_ge(mag_read, 4 * o + i - 1)
                    act.activation(mag[:, i % 2, :], hk[:, i, :], ACT.Abs).then_inc(mag_ready, 1)
                for m in range(4):
                    act.wait_ge(spectrum, 4 * o + m + 1)
                    act.activation(KS[:, o, m, :], ps[:, 5 + m % 3, :], ACT.Copy).then_inc(spectrum_out, 1)


def hyena_mix(nc, S):
    ps, ident, VA, VB, HY = S["ps"], S["ident"], S["VA"], S["VB"], S["HY"]
    CF, CI, KS, OB = S["CF"], S["CI"], S["KS"], S["OB"]
    with ExitStack() as ctx:
        sb = lambda n, s: ctx.enter_context(nc.sbuf_tensor(f"hm_{n}", s, F32))
        u3 = S["N"][:].rearrange("p d t -> p (d t)")[:, 0:12 * T].rearrange("p (c t) -> p c t", c=12)
        zt = sb("zt", [P, TT, BW])
        Y = S["X"][:].rearrange("p a (b n) -> p (a b) n", b=2)
        ta, tb = sb("ta", [P, 2, BW]), sb("tb", [P, 2, BW])
        z_ready, turned, zt_ready, spectrum, y_ready, conv_done, dve_step = semaphores(
            ctx, nc, " ".join(f"hm_{s}" for s in "z_ready turned zt_ready spectrum y_ready conv_done dve_step".split()))
        block = ctx.enter_context(nc.Block())

        @block.vector
        def _(dve):
            step = Chain(dve, dve_step)
            conv_w = lambda j, c: VB[:, VB_CONVW + 12 * j + c:VB_CONVW + 12 * j + c + 1]
            for c in range(12):
                ins = dve.tensor_scalar(u3[:, c, :], HY[:, c, 0:T], conv_w(0, c),
                                        VA[:, VA_CONVB + c:VA_CONVB + c + 1], ALU.mult, ALU.add)
            step(ins)
            for j in (1, 2):
                for c in range(12):
                    ins = dve.scalar_tensor_tensor(u3[:, c, :], HY[:, c, j:j + T], conv_w(j, c), u3[:, c, :],
                                                   ALU.mult, ALU.add)
                if j == 1:
                    step(ins)
            ins.then_inc(z_ready, 1)
            for o in range(2):
                z = u3[:, 0:4, :]
                for tt in range(TT):
                    dve.wait_ge(turned, TT * o + tt + 1)
                    dve.tensor_copy(zt[:, tt, :], ps[:, tt, :]).then_inc(zt_ready, 1)
                dve.wait_ge(spectrum, o + 1)
                ur, ui = ps[:, 2:4, :], ps[:, 4:6, :]
                kr, ki = KS[:, o, 0:2, :], KS[:, o, 2:4, :]
                dve.tensor_tensor(ta[:], ur, kr, ALU.mult)
                step(dve.tensor_tensor(tb[:], ui, ki, ALU.mult))
                step(dve.tensor_tensor(Y[:, 0:2, :], ta[:], tb[:], ALU.subtract))
                dve.tensor_tensor(ta[:], ur, ki, ALU.mult)
                step(dve.tensor_tensor(tb[:], ui, kr, ALU.mult))
                dve.tensor_tensor(Y[:, 2:4, :], ta[:], tb[:], ALU.add).then_inc(y_ready, 1)
                dve.wait_ge(conv_done, o + 1)
                if o:
                    dve.wait_ge(z_ready, 2)
                for c in range(4):
                    b = VA[:, VA_HYB + 4 * o + c:VA_HYB + 4 * o + c + 1]
                    ins = dve.scalar_tensor_tensor(ta[:, c // 2, (c % 2) * T:(c % 2 + 1) * T], z[:, c, :], b,
                                                   ps[:, 6 + c // 2, (c % 2) * T:(c % 2 + 1) * T], ALU.mult, ALU.add)
                step(ins)
                dst = OB[:] if o else z
                dve.tensor_tensor(dst, ta[:].rearrange("p a (b t) -> p (a b) t", b=2), u3[:, 4 + 4 * o:8 + 4 * o, :],
                                  ALU.mult).then_inc(z_ready, 1)

        @block.tensor
        def _(pe):
            for o in range(2):
                pe.wait_ge(z_ready, o + 1)
                for tt in range(TT):
                    for c in range(4):
                        ins = pe.transpose(ps[:, tt, c * P:(c + 1) * P], u3[:, c, tt * P:(tt + 1) * P], ident[:])
                    ins.then_inc(turned, 1)
                pe.wait_ge(zt_ready, TT * (o + 1))
                for m in range(4):
                    for tt in range(TT):
                        ins = pe.matmul(ps[:, 2 + m, :], CF[:, tt, m * P:(m + 1) * P], zt[:, tt, :],
                                        start=(tt == 0), stop=(tt == TT - 1))
                ins.then_inc(spectrum, 1)
                pe.wait_ge(y_ready, o + 1)
                for c in range(4):
                    for m in range(4):
                        ins = pe.matmul(ps[:, 6 + c // 2, (c % 2) * T:(c % 2 + 1) * T], Y[:, m, c * P:(c + 1) * P],
                                        CI[:, m, :], start=(m == 0), stop=(m == 3))
                ins.then_inc(conv_done, 1)


def merge_heads(nc, S, ring, chunks):
    ps, H, MG, modv = S["ps"], S["H"], S["MG"], S["modv"]
    OA, OB, Y = S["G"], S["OB"], S["N"]
    with ExitStack() as ctx:
        ta = ctx.enter_context(nc.sbuf_tensor("mh_ta", [P, 2, 2, T], F32))
        pair_ready, ta_done, y_ready, out_ready, h_done, dve_step = semaphores(
            ctx, nc, " ".join(f"mh_{s}" for s in "pair_ready ta_done y_ready out_ready h_done dve_step".split()))
        block = ctx.enter_context(nc.Block())

        @block.sync
        def _(sp):
            refill(sp, ring, chunks, C_PROJ, 4)

        @block.tensor
        def _(pe):
            for i in range(2):
                ring.arrived(pe, C_PROJ + i)
            for d in range(DT):
                if d >= 4:
                    pe.wait_ge(ta_done, d - 3)
                for i, src in enumerate((OA, OB)):
                    w = ring.view(C_PROJ + i, 4, D)
                    for k in range(4):
                        ins = pe.matmul(ps[:, 2 * (d % 4) + i, 0:T], w[:, k, d * P:(d + 1) * P], src[:, k, :],
                                        start=(k == 0), stop=(k == 3))
                    if d == DT - 1:
                        ins.then_inc(ring.used, 1)
                    elif i == 1:
                        ins.then_inc(pair_ready, 1)
            pe.wait_ge(y_ready, DT)
            for d in range(DT):
                w = ring.view(C_WOUT + d // 4, DT, CH)
                if d % 4 == 0:
                    ring.arrived(pe, C_WOUT + d // 4)
                for k in range(DT):
                    ins = pe.matmul(ps[:, d, 0:T], w[:, k, (d % 4) * P:(d % 4 + 1) * P], Y[:, k, 0:T],
                                    start=(k == 0), stop=(k == DT - 1))
                ins.then_inc(ring.used if d % 4 == 3 else out_ready, 1)

        @block.vector
        def _(dve):
            step = Chain(dve, dve_step)
            for d in range(DT):
                if d == DT - 1:
                    dve.wait_ge(ring.used, C_PROJ + 2)
                else:
                    dve.wait_ge(pair_ready, d + 1)
                dve.tensor_tensor(ta[:, d % 2, 0, :], MG[:, d, :], ps[:, 2 * (d % 4), 0:T], ALU.mult)
                dve.tensor_tensor(ta[:, d % 2, 1, :], MG[:, DT + d, :], ps[:, 2 * (d % 4) + 1, 0:T],
                                  ALU.mult).then_inc(ta_done, 1)
                dve.wait_ge(ta_done, d + 1)
                dve.tensor_tensor(Y[:, d, 0:T], ta[:, d % 2, 0, :], ta[:, d % 2, 1, :], ALU.add).then_inc(y_ready, 1)
            for d in range(DT):
                if d % 4 == 3:
                    dve.wait_ge(ring.used, C_WOUT + d // 4 + 1)
                else:
                    dve.wait_ge(out_ready, d - d // 4 + 1)
                v = H[:, d, 0:T]
                dve.scalar_tensor_tensor(v, ps[:, d, 0:T], modv[:, 0, 5 * DT + d:5 * DT + d + 1], v, ALU.mult, ALU.add)


ALPHA = (2 * 2) ** 0.25
E_FF = 512
N_EXP = 32
RB_SSDN, RB_LNG, RB_LNB, RB_GLAN, RB_DTB, RB_ALOG, RB_DSKIP, RB_END = 0, 512, 768, 1024, 1280, 1288, 1296, 1304
VL_CONVW, VL_CONVB, VL_MU, VL_W0, VL_A0, VL_KK, VL_KA, VL_RK, VL_GBA, VL_ROWS = 0, 24, 30, 37, 39, 41, 43, 45, 47, 48
WIN2_BOUNDS = [(0, 512), (512, 1024), (1024, 1288), (1288, 1800), (1800, 2312), (2312, 2696), (2696, 2968)]
WIN2_OUTPUTS = [
    [("z", 0, 512, 0), ("z", 0, 512, 1)],
    [("xbc", P * j, P, j) for j in range(4)],
    [("xbc", 0, P, 4), ("xbc", P, P, 5), ("dt", 256, 8, 0), ("dt", 256, 8, 1)],
    [("rw", P * j, P, j) for j in range(4)],
    [("rw", P * j, P, 4 + j) for j in range(3)] + [("gq", 384, P, 0)],
    [("gk", 0, P, 0), ("gv", P, 256, 0), ("gv", P, 256, 1)],
    [("gg", 0, 256, 0), ("gg", 0, 256, 1), ("ga", 256, 16, 0)],
]
C2_WIN, C2_WOUT, C2_END = 0, len(WIN2_BOUNDS), len(WIN2_BOUNDS) + 2
TOKEN_MAJOR = ("z", "dt", "gv", "gg")
BY_ACT = ("z", "gg")


def to_tokens(nc, t, S):
    ps, ident, ones, H, VA, X = S["ps"], S["ident"], S["ones"], S["H"], S["VA"], S["X"]
    with ExitStack() as ctx:
        rstd = ctx.enter_context(nc.sbuf_tensor("tk_rstd", [P, T], F32))
        N = ctx.enter_context(nc.sbuf_tensor("tk_n", [P, DT, T], F32))
        squares, summed, mean_ready, root_ready, dve_step, scaled, turned = semaphores(
            ctx, nc, " ".join(f"tk_{s}" for s in "squares summed mean_ready root_ready dve_step scaled turned".split()))
        block = ctx.enter_context(nc.Block())

        @block.scalar
        def _(act):
            for d in range(DT):
                act.activation(N[:, d, 0:T], H[:, d, 0:T], ACT.Square).then_inc(squares, 1)
            act.wait_ge(mean_ready, 1)
            act.activation(rstd[:], rstd[:], ACT.Sqrt).then_inc(root_ready, 1)

        @block.tensor
        def _(pe):
            for d in range(DT):
                pe.wait_ge(squares, d + 1)
                ins = pe.matmul(ps[:, 0, 0:T], ones[:], N[:, d, 0:T], start=(d == 0), stop=(d == DT - 1))
            ins.then_inc(summed, 1)
            for d in range(DT):
                pe.wait_ge(scaled, d + 1)
                for a in range(TT):
                    ins = pe.transpose(ps[:, 2 + 2 * a + d // 4, (d % 4) * P:(d % 4 + 1) * P],
                                       N[:, d, a * P:(a + 1) * P], ident[:])
            ins.then_inc(turned, 1)

        @block.vector
        def _(dve):
            step = Chain(dve, dve_step)
            dve.wait_ge(summed, 1)
            dve.tensor_scalar(rstd[:], ps[:, 0, 0:T], 1.0 / D, RMS_EPS, ALU.mult, ALU.add).then_inc(mean_ready, 1)
            dve.wait_ge(root_ready, 1)
            step(dve.reciprocal(rstd[:], rstd[:]))
            for d in range(DT):
                dve.scalar_tensor_tensor(N[:, d, 0:T], H[:, d, 0:T], VA[:, VA_FNORM + d:VA_FNORM + d + 1], rstd[:],
                                         ALU.mult, ALU.mult).then_inc(scaled, 1)
            dve.wait_ge(turned, 1)
            for a in range(TT):
                dve.tensor_copy(X[:, a, :], ps[:, 2 + 2 * a:4 + 2 * a, :].rearrange("p a n -> p (a n)"))


def residual_norm(nc, S, name, g_row, b_row, add, out=None):
    ps, ident, X, XT = S["ps"], S["ident"], S["X"], S["XT"]
    with ExitStack() as ctx:
        g = ctx.enter_context(nc.sbuf_tensor(f"{name}_g", [P, D], F32))
        b = ctx.enter_context(nc.sbuf_tensor(f"{name}_b", [P, D], F32))
        stats = ctx.enter_context(nc.sbuf_tensor(f"{name}_stats", [P, TT, 2, 6], F32))
        mv = ctx.enter_context(nc.sbuf_tensor(f"{name}_mv", [P, TT, 2], F32))
        sd = ctx.enter_context(nc.sbuf_tensor(f"{name}_sd", [P, TT], F32))
        rows_in, var_ready, sd_ready, x_ready, turned, xt_ready, dve_step, stored = sems = semaphores(
            ctx, nc, " ".join(f"{name}_{s}" for s in
                              "rows_in var_ready sd_ready x_ready turned xt_ready dve_step stored".split()))
        with nc.Block() as block:

            @block.sync
            def _(sp):
                sp.dma_start(g[:], g_row.partition_broadcast(P)).then_inc(rows_in, 16)
                sp.dma_start(b[:], b_row.partition_broadcast(P)).then_inc(rows_in, 16)
                sp.wait_ge(rows_in, 32)
                if out is not None:
                    for a in range(TT):
                        sp.wait_ge(x_ready, a + 1)
                        sp.dma_start(out[0, a * P:(a + 1) * P, :], X[:, a, :]).then_inc(stored, 16)
                    sp.wait_ge(stored, 16 * TT)

            @block.vector
            def _(dve):
                step = Chain(dve, dve_step)
                if add:
                    for a in range(TT):
                        v = X[:, a, :]
                        ins = dve.scalar_tensor_tensor(v, v, ALPHA, ps[:, 2 * a:2 * a + 2, :].rearrange("p a n -> p (a n)"),
                                                       ALU.mult, ALU.add)
                    step(ins)
                for a in range(TT):
                    for h in range(2):
                        ins = dve.bn_stats(stats[:, a, h, :], X[:, a, h * CH:(h + 1) * CH])
                step(ins)
                for a in range(TT):
                    ins = dve.bn_aggr(mv[:, a, :], stats[:, a, :, :].rearrange("p a b -> p (a b)"))
                step(ins)
                dve.tensor_scalar(sd[:], mv[:, :, 1], LN_EPS, None, ALU.add).then_inc(var_ready, 1)
                dve.wait_ge(sd_ready, 1)
                step(dve.reciprocal(sd[:], sd[:]))
                dve.wait_ge(rows_in, 32)
                for a in range(TT):
                    v = X[:, a, :]
                    step(dve.tensor_scalar(v, v, mv[:, a, 0:1], sd[:, a:a + 1], ALU.subtract, ALU.mult))
                    step(dve.tensor_tensor(v, v, g[:], ALU.mult))
                    dve.tensor_tensor(v, v, b[:], ALU.add).then_inc(x_ready, 1)

            @block.tensor
            def _(pe):
                for a in range(TT):
                    pe.wait_ge(x_ready, a + 1)
                    for d in range(DT):
                        ins = pe.transpose(ps[:, 4 + 2 * a + d // 4, (d % 4) * P:(d % 4 + 1) * P],
                                           X[:, a, d * P:(d + 1) * P], ident[:])
                    ins.then_inc(turned, 1)

            @block.scalar
            def _(act):
                act.wait_ge(var_ready, 1)
                act.activation(sd[:], sd[:], ACT.Sqrt).then_inc(sd_ready, 1)
                for a in range(TT):
                    act.wait_ge(turned, a + 1)
                    act.activation(XT[:, :, a * P:(a + 1) * P],
                                   ps[:, 4 + 2 * a:6 + 2 * a, :].rearrange("p a (d t) -> p (a d) t", d=4), ACT.Copy)
        return sems


def input_projection2(nc, S, ring, l):
    ps, ident, XT, t = S["ps"], S["ident"], S["XT"], S["t"]
    VL, RB, LR, WA2 = S["VL"], S["RB"], S["LR"], S["WA2"]
    with ExitStack() as ctx:
        rows = ctx.enter_context(nc.sbuf_tensor("rows2", [VL_ROWS, P], F32))
        vec_in, vec_turned, vec_out, tile_ready, act_out, dve_out = sems = semaphores(
            ctx, nc, "w2_vec_in w2_vec_turned w2_vec_out w2_tile_ready w2_act_out w2_dve_out")
        flat = [(n, kind, col, w, j, m == len(outs) - 1) for n, outs in enumerate(WIN2_OUTPUTS)
                for m, (kind, col, w, j) in enumerate(outs)]
        dest = {"z": lambda j: S["Z"][:, j, :], "gg": lambda j: S["GG"][:, j, :], "gv": lambda j: S["GV"][:, j, :],
                "dt": lambda j: S["DTR"][:, j, :], "xbc": lambda j: S["XBC"][:, j, 3:T + 3],
                "rw": lambda j: S["RW"][:, j, 1:T + 1], "gq": lambda j: S["GQ"][:], "gk": lambda j: S["GK"][:],
                "ga": lambda j: S["GA"][:]}
        layer = lambda name: t[name + "_2"][bass.ds(l, 1)]
        with nc.Block() as block:

            def copied(eng, i):
                mine = flat[i][1] in BY_ACT
                eng.wait_ge(act_out if mine else dve_out, sum((f[1] in BY_ACT) == mine for f in flat[:i + 1]))

            def ready(eng, i):
                if flat[i][5]:
                    eng.wait_ge(ring.used, C2_WIN + flat[i][0] + 1)
                else:
                    eng.wait_ge(tile_ready, sum(not f[5] for f in flat[:i + 1]))

            @block.sync
            def _(sp):
                for n in range(ring.slots):
                    ring.load(sp, n, layer_chunk(t, n, l))
                for at, name in ((VL_CONVB, "ssd_conv_b"), (VL_MU, "rwkv_mu"), (VL_W0, "rwkv_w0"), (VL_A0, "rwkv_a0"),
                                 (VL_KK, "rwkv_k_k"), (VL_KA, "rwkv_k_a"), (VL_GBA, "gla_b_a")):
                    src = layer(name).rearrange("a (r c) -> (a r) c", c=P)
                    sp.dma_start(rows[at:at + src.shape[0], :], src).then_inc(vec_in, 16)
                sp.dma_start(rows[VL_CONVW:VL_CONVW + 24, :],
                             layer("ssd_conv_w").rearrange("a j (r c) -> (a j r) c", c=P)).then_inc(vec_in, 16)
                sp.dma_start(rows[VL_RK:VL_RK + 2, :],
                             layer("rwkv_r_k").rearrange("a (r h) c -> (a r) (h c)", h=2)).then_inc(vec_in, 16)
                for at, name in ((RB_SSDN, "ssd_norm_g"), (RB_LNG, "rwkv_ln_g"), (RB_LNB, "rwkv_ln_b"),
                                 (RB_GLAN, "gla_norm_g"), (RB_DTB, "ssd_dt_bias"), (RB_ALOG, "ssd_a_log"),
                                 (RB_DSKIP, "ssd_d")):
                    src = layer(name).rearrange("a n -> (a n)")
                    sp.dma_start(RB[:, at:at + src.shape[0]], src.partition_broadcast(P)).then_inc(vec_in, 16)
                for i, (name, a, b) in enumerate((("rwkv_w2", 0, 32), ("rwkv_a2", 32, 64), ("rwkv_g2", 64, 128))):
                    sp.dma_start(LR[a:b, i, :], layer(name).rearrange("a r n -> (a r) n")).then_inc(vec_in, 16)
                sp.dma_start(WA2[:], layer("gla_w_a2").rearrange("a r n -> (a r) n")).then_inc(vec_in, 16)
                sp.dma_start(S["WR"][:, :, 0:4], layer("moe_w_rg").rearrange("a (k p) n -> p (a k) n", p=P)).then_inc(vec_in, 16)
                sp.dma_start(S["WR"][:, :, 4:36], layer("moe_w_re").rearrange("a (k p) n -> p (a k) n", p=P)).then_inc(vec_in, 16)
                sp.dma_start(S["BR"][:, 0:4], layer("moe_b_rg").rearrange("a n -> (a n)").partition_broadcast(P)).then_inc(vec_in, 16)
                sp.dma_start(S["BR"][:, 4:36], layer("moe_b_re").rearrange("a n -> (a n)").partition_broadcast(P)).then_inc(vec_in, 16)
                for n in range(ring.slots, C2_END):
                    ring.load(sp, n, layer_chunk(t, n, l))

            @block.tensor
            def _(pe):
                for i, (n, kind, col, w, j, last) in enumerate(flat):
                    if i == 0 or flat[i - 1][0] != n:
                        ring.arrived(pe, C2_WIN + n)
                    if i >= 7:
                        copied(pe, i - 7)
                    a, b = WIN2_BOUNDS[n]
                    wv = ring.view(C2_WIN + n, DT, b - a)
                    for k in range(DT):
                        if kind in TOKEN_MAJOR:
                            ins = pe.matmul(ps[:, i % 7, 0:w], XT[:, k, j * P:(j + 1) * P], wv[:, k, col:col + w],
                                            start=(k == 0), stop=(k == DT - 1))
                        else:
                            ins = pe.matmul(ps[0:w, i % 7, 0:T], wv[:, k, col:col + w], XT[:, k, :],
                                            start=(k == 0), stop=(k == DT - 1))
                    ins.then_inc(ring.used if last else tile_ready, 1)
                pe.wait_ge(vec_in, 16 * 24)
                pe.transpose(ps[:, 7, 0:VL_ROWS], rows[:], ident[0:VL_ROWS, 0:VL_ROWS]).then_inc(vec_turned, 1)

            @block.scalar
            def _(act):
                for i, (n, kind, col, w, j, last) in enumerate(flat):
                    if kind in BY_ACT:
                        ready(act, i)
                        act.activation(dest[kind](j), ps[:, i % 7, 0:w], ACT.Silu).then_inc(act_out, 1)

            @block.vector
            def _(dve):
                dve.memset(S["XBC"][:, :, 0:3], 0.0)
                dve.memset(S["RW"][:, :, 0:1], 0.0)
                for i, (n, kind, col, w, j, last) in enumerate(flat):
                    if kind not in BY_ACT:
                        ready(dve, i)
                        src = ps[:, i % 7, 0:w] if kind in TOKEN_MAJOR else ps[0:w, i % 7, 0:T]
                        dve.tensor_copy(dest[kind](j), src).then_inc(dve_out, 1)
                dve.wait_ge(vec_turned, 1)
                dve.tensor_copy(VL[:], ps[:, 7, 0:VL_ROWS])
        return sems


def layer_chunk(t, n, l):
    at = bass.ds(l, 1)
    if n < C2_WOUT:
        a, b = WIN2_BOUNDS[n]
        return t["w_in_2"][at].rearrange("a (k p) n -> p (a k) n", p=P)[:, :, a:b]
    a = CH * (n - C2_WOUT)
    return t["w_out_2"][at].rearrange("a (k p) n -> p (a k) n", p=P)[:, :, a:a + CH]


def expert_chunk(t, le, part):
    w = t[("moe_w_gate_2", "moe_w_up_2", "moe_w_down_2")[part]].rearrange("l e a b -> (l e) a b")
    return w[bass.ds(le, 1)].rearrange("o (k p) n -> p (o k) n", p=P)


SSD_H, HD64 = 8, 64
CB_W = T + P


def ssd_mixer(nc, S):
    ps, ident, ones, triu = S["ps"], S["ident"], S["ones"], S["triu"]
    VL, RB, XBC, Z, DTR, YT, hm2 = S["VL"], S["RB"], S["XBC"], S["Z"], S["DTR"], S["YT"], S["hm2"]
    with ExitStack() as ctx:
        sb = lambda n, s: ctx.enter_context(nc.sbuf_tensor(f"sd_{n}", s, F32))
        xc = sb("xc", [P, 6, T])
        xh = sb("xh", [P, TT, BW])
        xdt = sb("xdt", [P, TT, BW])
        dt, m, e = sb("dt", [P, TT, 8]), sb("m", [P, TT, 8]), sb("e", [P, TT, 8])
        aexp = sb("aexp", [P, 8])
        adt = sb("adt", [P, TT, 8])
        acs = sb("acs", [P, TT, 8])
        adtb = sb("adtb", [P, TT, 8, P])
        bm = sb("bm", [P, 2, T])
        cbm = sb("cbm", [P, 2, CB_W])
        SD = sb("SD", [P, 8, CB_W])
        sq = sb("sq", [P, TT, BW])
        rs = sb("rs", [P, 2 * TT])
        (conv_ready, silu_ready, turned, m_ready, exp_ready, ln_ready, adt_ready, acs_made, rows_made, cb_made,
         diff_ready, decay_ready, sd_ready, y_made, mean_ready, root_ready, bm_ready, dve_step) = sems = semaphores(
            ctx, nc, " ".join(f"sd_{s}" for s in """conv_ready silu_ready turned m_ready exp_ready ln_ready adt_ready
            acs_made rows_made cb_made diff_ready decay_ready sd_ready y_made mean_ready root_ready bm_ready
            dve_step""".split()))
        heads = lambda v: v.rearrange("p a (h c) -> p (a h) c", c=HD64)
        per_head = lambda v: v.rearrange("p a h -> p (a h)").unsqueeze(2).to_broadcast([P, TT * SSD_H, HD64])
        with nc.Block() as block:

            @block.vector
            def _(dve):
                step = Chain(dve, dve_step)
                step(dve.tensor_tensor(dt[:], DTR[:], RB[:, RB_DTB:RB_DTB + 8].unsqueeze(1).to_broadcast([P, TT, 8]), ALU.add))
                step(dve.tensor_scalar(m[:], dt[:], -1.0, None, ALU.mult))
                dve.tensor_tensor(m[:], m[:], dt[:], ALU.min).then_inc(m_ready, 1)
                step(dve.tensor_scalar(dt[:], dt[:], 0.0, None, ALU.max))
                cw = lambda j, c: VL[:, VL_CONVW + 6 * j + c:VL_CONVW + 6 * j + c + 1]
                for c in range(6):
                    ins = dve.tensor_scalar(xc[:, c, :], XBC[:, c, 0:T], cw(0, c), VL[:, VL_CONVB + c:VL_CONVB + c + 1],
                                            ALU.mult, ALU.add)
                step(ins)
                for j in (1, 2, 3):
                    for c in range(6):
                        ins = dve.scalar_tensor_tensor(xc[:, c, :], XBC[:, c, j:j + T], cw(j, c), xc[:, c, :],
                                                       ALU.mult, ALU.add)
                    if j < 3:
                        step(ins)
                ins.then_inc(conv_ready, 1)
                dve.wait_ge(ln_ready, 1)
                step(dve.tensor_tensor(dt[:], dt[:], m[:], ALU.add))
                dve.scalar_tensor_tensor(adt[:], dt[:], -1.0, aexp[:].unsqueeze(1).to_broadcast([P, TT, 8]),
                                         ALU.mult, ALU.mult).then_inc(adt_ready, 1)
                dve.wait_ge(adt_ready, 1)
                for a in range(TT):
                    ins = dve.tensor_copy(adtb[:, a], adt[:, a, :].unsqueeze(2).to_broadcast([P, 8, P]))
                ins.then_inc(adt_ready, 1)
                dve.wait_ge(silu_ready, 1)
                for g in range(2):
                    ins = dve.tensor_scalar(bm[:, g, :], xc[:, 4, :], hm2[:, g:g + 1], None, ALU.mult)
                ins.then_inc(bm_ready, 1)
                dve.wait_ge(turned, 1)
                step(dve.tensor_copy(xh[:], ps[:, 6:8, :]))
                dve.tensor_tensor(heads(xdt[:]), heads(xh[:]), per_head(dt[:]), ALU.mult)
                dve.wait_ge(acs_made, 1)
                step(dve.tensor_copy(acs[:], ps[:, 4, 0:16].rearrange("p (a h) -> p a h", a=TT)))
                dve.wait_ge(rows_made, 1)
                for h in range(SSD_H):
                    row = ps[:, h // 2, (h % 2) * T:(h % 2 + 1) * T]
                    dve.tensor_scalar(SD[:, h, 0:T], row, acs[:, 0, h:h + 1], 0.0, ALU.subtract, ALU.min)
                    ins = dve.tensor_scalar(SD[:, h, T:], row[:, P:T], acs[:, 1, h:h + 1], 0.0, ALU.subtract, ALU.min)
                ins.then_inc(diff_ready, 1)
                dve.wait_ge(cb_made, 1)
                for g in range(2):
                    dve.tensor_tensor(cbm[:, g, 0:P], ps[:, 6 + g, 0:P], triu[:], ALU.mult)
                    dve.tensor_copy(cbm[:, g, P:T], ps[:, 6 + g, P:T])
                    ins = dve.tensor_tensor(cbm[:, g, T:], ps[:, 6 + g, T:CB_W], triu[:], ALU.mult)
                step(ins)
                dve.wait_ge(decay_ready, 1)
                for g in range(2):
                    v = SD[:, 4 * g:4 * g + 4, :]
                    dve.tensor_tensor(v, v, cbm[:, g, :].unsqueeze(1).to_broadcast([P, 4, CB_W]), ALU.mult).then_inc(sd_ready, 1)
                for a in range(TT):
                    v = xh[:, a, :].rearrange("p (h c) -> p h c", c=HD64)
                    ins = dve.tensor_tensor(v, v, RB[:, RB_DSKIP:RB_DSKIP + 8].unsqueeze(2).to_broadcast([P, 8, HD64]), ALU.mult)
                step(ins)
                dve.wait_ge(y_made, 1)
                y = YT[:, :, 0:BW]
                step(dve.tensor_tensor(y, ps[:, 4:6, :], xh[:], ALU.add))
                step(dve.tensor_tensor(y, y, Z[:], ALU.mult))
                step(dve.tensor_tensor(sq[:], y, y, ALU.mult))
                step(dve.tensor_reduce(rs[:], sq[:].rearrange("p a (g c) -> p (a g) c", g=2), AX.X, ALU.add))
                dve.tensor_scalar(rs[:], rs[:], 1.0 / 256, RMS_EPS, ALU.mult, ALU.add).then_inc(mean_ready, 1)
                dve.wait_ge(root_ready, 1)
                step(dve.reciprocal(rs[:], rs[:]))
                for a in range(TT):
                    for g in range(2):
                        c = slice(256 * g, 256 * g + 256)
                        dve.scalar_tensor_tensor(YT[:, a, c], YT[:, a, c], rs[:, 2 * a + g:2 * a + g + 1],
                                                 RB[:, RB_SSDN + 256 * g:RB_SSDN + 256 * g + 256], ALU.mult, ALU.mult)

            @block.scalar
            def _(act):
                act.wait_ge(m_ready, 1)
                act.activation(aexp[:], RB[:, RB_ALOG:RB_ALOG + 8], ACT.Exp)
                act.activation(e[:], m[:], ACT.Exp).then_inc(exp_ready, 1)
                act.wait_ge(exp_ready, 1)
                act.activation(m[:], e[:], ACT.Ln, bias=1.0).then_inc(ln_ready, 1)
                act.wait_ge(conv_ready, 1)
                act.activation(xc[:], xc[:], ACT.Silu).then_inc(silu_ready, 1)
                act.wait_ge(diff_ready, 1)
                act.activation(SD[:], SD[:], ACT.Exp).then_inc(decay_ready, 1)
                act.wait_ge(mean_ready, 1)
                act.activation(rs[:], rs[:], ACT.Sqrt).then_inc(root_ready, 1)

            @block.tensor
            def _(pe):
                pe.wait_ge(adt_ready, 1)
                pe.matmul(ps[:, 4, 0:8], triu[:], adt[:, 0, :], start=True, stop=True)
                pe.matmul(ps[:, 4, 8:16], triu[:], adt[:, 1, :], start=True, stop=False)
                pe.matmul(ps[:, 4, 8:16], ones[:], adt[:, 0, :], start=False, stop=True).then_inc(acs_made, 1)
                pe.wait_ge(adt_ready, 2)
                for h in range(SSD_H):
                    bank, c = h // 2, (h % 2) * T
                    pe.matmul(ps[:, bank, c:c + P], adtb[:, 0, h, :], triu[:], start=True, stop=True)
                    pe.matmul(ps[:, bank, c + P:c + T], adtb[:, 0, h, :], ones[:], start=True, stop=False)
                    ins = pe.matmul(ps[:, bank, c + P:c + T], adtb[:, 1, h, :], triu[:], start=False, stop=True)
                ins.then_inc(rows_made, 1)
                pe.wait_ge(silu_ready, 1)
                for a in range(TT):
                    for c in range(4):
                        ins = pe.transpose(ps[:, 6 + a, c * P:(c + 1) * P], xc[:, c, a * P:(a + 1) * P], ident[:])
                ins.then_inc(turned, 1)
                pe.wait_ge(bm_ready, 1)
                pe.wait_ge(diff_ready, 1)
                for g in range(2):
                    pe.matmul(ps[:, 6 + g, 0:T], bm[:, g, 0:P], xc[:, 5, :], start=True, stop=True)
                    ins = pe.matmul(ps[:, 6 + g, T:CB_W], bm[:, g, P:T], xc[:, 5, P:T], start=True, stop=True)
                ins.then_inc(cb_made, 1)
                for h in range(SSD_H):
                    pe.wait_ge(sd_ready, h // 4 + 1)
                    c = slice(h * HD64, (h + 1) * HD64)
                    pe.matmul(ps[:, 4, c], SD[:, h, 0:P], xdt[:, 0, c], start=True, stop=True)
                    pe.matmul(ps[:, 5, c], SD[:, h, P:T], xdt[:, 0, c], start=True, stop=False)
                    ins = pe.matmul(ps[:, 5, c], SD[:, h, T:], xdt[:, 1, c], start=False, stop=True)
                ins.then_inc(y_made, 1)
        return sems


def gla_mixer(nc, S):
    ps, ident, masks, VL, RB = S["ps"], S["ident"], S["masks"], S["VL"], S["RB"]
    GQ, GK, GV, GG, GA, WA2, YT, hm4 = S["GQ"], S["GK"], S["GV"], S["GG"], S["GA"], S["WA2"], S["YT"], S["hm4"]
    NL = LEVELS + 1
    with ExitStack() as ctx:
        sb = lambda n, s: ctx.enter_context(nc.sbuf_tensor(f"gl_{n}", s, F32))
        x, m, e, keep = sb("x", [P, T]), sb("m", [P, T]), sb("e", [P, T]), sb("keep", [P, T])
        EB = sb("EB", [P, NL, T])
        KM = sb("KM", [P, 2, NL + 1, T])
        prod = sb("prod", [P, 2, NL * P])
        cross = sb("cross", [P, 4, P])
        sq = sb("sq", [P, TT, 256])
        rs = sb("rs", [P, TT * 4])
        (gate_made, m_ready, e_ready, ln_ready, diff_ready, decay_ready, km_ready, scores, prod_ready, cross_ready, o_made,
         mean_ready, root_ready, dve_step) = sems = semaphores(
            ctx, nc, " ".join(f"gl_{s}" for s in """gate_made m_ready e_ready ln_ready diff_ready decay_ready km_ready
            scores prod_ready cross_ready o_made mean_ready root_ready dve_step""".split()))
        with nc.Block() as block:

            @block.tensor
            def _(pe):
                pe.matmul(ps[:, 7, 0:T], WA2[:], GA[:], start=True, stop=True).then_inc(gate_made, 1)
                for h in range(4):
                    pe.wait_ge(km_ready, h + 1)
                    for tt in range(TT):
                        y = 2 * h + tt
                        if y >= 2:
                            pe.wait_ge(prod_ready, y - 1)
                        c = slice(tt * P, (tt + 1) * P)
                        for l in range(NL):
                            ins = pe.matmul(ps[:, 2 * (y % 2) + l // 4, (l % 4) * P:(l % 4 + 1) * P],
                                            KM[:, h % 2, l, c], GQ[:, c] if l == 0 else EB[:, l - 1, c],
                                            start=True, stop=True)
                        ins.then_inc(scores, 1)
                    pe.matmul(ps[:, 4, h * P:(h + 1) * P], KM[:, h % 2, NL, 0:P], EB[:, NL - 1, P:T],
                              start=True, stop=True).then_inc(scores, 1)
                    for tt in range(TT):
                        y = 2 * h + tt
                        pe.wait_ge(prod_ready, y + 1)
                        v = GV[:, tt, h * HD64:(h + 1) * HD64]
                        for l in range(NL):
                            ins = pe.matmul(ps[:, 5 + tt, h * HD64:(h + 1) * HD64], prod[:, y % 2, l * P:(l + 1) * P], v,
                                            start=(l == 0), stop=(l == NL - 1 and tt == 0))
                        if tt == 0:
                            ins.then_inc(o_made, 1)
                    pe.wait_ge(cross_ready, h + 1)
                    pe.matmul(ps[:, 6, h * HD64:(h + 1) * HD64], cross[:, h, :], GV[:, 0, h * HD64:(h + 1) * HD64],
                              start=False, stop=True).then_inc(o_made, 1)

            @block.scalar
            def _(act):
                act.wait_ge(m_ready, 1)
                act.activation(e[:], m[:], ACT.Exp).then_inc(e_ready, 1)
                act.wait_ge(e_ready, 1)
                act.activation(m[:], e[:], ACT.Ln, bias=1.0).then_inc(ln_ready, 1)
                act.wait_ge(diff_ready, 1)
                act.activation(EB[:], EB[:], ACT.Exp).then_inc(decay_ready, 1)
                act.wait_ge(mean_ready, 1)
                act.activation(rs[:], rs[:], ACT.Sqrt).then_inc(root_ready, 1)

            @block.vector
            def _(dve):
                step = Chain(dve, dve_step)
                dve.memset(keep[:], 1.0)
                dve.tensor_scalar(GQ[:], GQ[:], 32 ** -0.5, None, ALU.mult)
                dve.wait_ge(gate_made, 1)
                step(dve.tensor_scalar(x[:], ps[:, 7, 0:T], VL[:, VL_GBA:VL_GBA + 1], None, ALU.add))
                step(dve.tensor_scalar(m[:], x[:], -1.0, None, ALU.mult))
                dve.tensor_tensor(m[:], m[:], x[:], ALU.min).then_inc(m_ready, 1)
                dve.wait_ge(ln_ready, 1)
                step(dve.scalar_tensor_tensor(x[:], x[:], 0.0, m[:], ALU.min, ALU.subtract))
                step(dve.tensor_scalar(x[:], x[:], 1.0 / 16.0, None, ALU.mult))
                step(dve.tensor_tensor_scan(e[:], keep[:], x[:], 0.0, ALU.mult, ALU.add))
                for l in range(NL):
                    ins = block_differences(dve, EB[:, l, :], e[:], 2 << l, False)
                ins.then_inc(diff_ready, 1)
                dve.wait_ge(decay_ready, 1)
                for l in range(NL):
                    v = EB[:, l, :].rearrange("p (n two s) -> p n two s", two=2, s=1 << l)
                    for side, src in ((0, GK), (1, GQ)):
                        w = src[:].rearrange("p (n two s) -> p n two s", two=2, s=1 << l)
                        ins = dve.tensor_tensor(v[:, :, side, :], v[:, :, side, :], w[:, :, side, :], ALU.mult)
                step(ins)

                def one_head(h):
                    if h >= 2:
                        dve.wait_ge(scores, 3 * (h - 1))
                    dve.tensor_scalar(KM[:, h % 2, 0, :], GK[:], hm4[:, h:h + 1], None, ALU.mult)
                    dve.tensor_scalar(KM[:, h % 2, 1:, :], EB[:], hm4[:, h:h + 1], None, ALU.mult).then_inc(km_ready, 1)

                one_head(0)
                for h in range(4):
                    if h < 3:
                        one_head(h + 1)
                    for tt in range(TT):
                        y = 2 * h + tt
                        dve.wait_ge(scores, 3 * h + tt + 1)
                        if y >= 2:
                            dve.wait_ge(o_made, y - 1)
                        dve.tensor_tensor(prod[:, y % 2, :], ps[:, 2 * (y % 2):2 * (y % 2) + 2, :].rearrange("p a b -> p (a b)"),
                                          masks[:, 0].rearrange("p l c -> p (l c)"), ALU.mult).then_inc(prod_ready, 1)
                    dve.wait_ge(scores, 3 * h + 3)
                    dve.tensor_copy(cross[:, h, :], ps[:, 4, h * P:(h + 1) * P]).then_inc(cross_ready, 1)
                dve.wait_ge(o_made, 8)
                o = ps[:, 5:7, 0:256]
                y = YT[:, :, 768:1024]
                step(dve.tensor_copy(y, o))
                step(dve.tensor_tensor(sq[:], y, y, ALU.mult))
                step(dve.tensor_reduce(rs[:], sq[:].rearrange("p a (h c) -> p (a h) c", c=HD64), AX.X, ALU.add))
                dve.tensor_scalar(rs[:], rs[:], 1.0 / HD64, RMS_EPS, ALU.mult, ALU.add).then_inc(mean_ready, 1)
                dve.tensor_tensor(GG[:], GG[:], RB[:, RB_GLAN:RB_GLAN + 256].unsqueeze(1).to_broadcast([P, TT, 256]), ALU.mult)
                dve.wait_ge(root_ready, 1)
                step(dve.reciprocal(rs[:], rs[:]))
                step(dve.tensor_tensor(y, y, GG[:], ALU.mult))
                for a in range(TT):
                    v = YT[:, a, 768:1024].rearrange("p (h c) -> p h c", c=HD64)
                    dve.tensor_tensor(v, v, rs[:, 4 * a:4 * a + 4].unsqueeze(2).to_broadcast([P, 4, HD64]), ALU.mult)
        return sems


def rwkv_mixer(nc, S):
    ps, ident, blockones = S["ps"], S["ident"], S["blockones"]
    masks, triu, VL, RB, LR, RW, YT, hm2 = S["masks"], S["triu"], S["VL"], S["RB"], S["LR"], S["RW"], S["YT"], S["hm2"]
    with ExitStack() as ctx:
        sb = lambda n, s: ctx.enter_context(nc.sbuf_tensor(f"rk_{n}", s, F32))
        p = sb("p", [P, 7, T])
        lact = sb("lact", [P, T])
        gl, av = sb("gl", [P, 2, T]), sb("av", [P, 2, T])
        cum, ce = sb("cum", [P, 2, T]), sb("ce", [P, 2, T])
        e1, e3 = sb("e1", [P, 2, T]), sb("e3", [P, 2, T])
        kk, sq = sb("kk", [P, 2, T]), sb("sq", [P, 2, T])
        keep = sb("keep", [P, P])
        emid = sb("emid", [P, 2, 2])
        bm, km = sb("bm", [P, 2, 2, T]), sb("km", [P, 2, 2, T])
        gt = sb("gt", [P, TT, 256])
        vt = sb("vt", [P, TT, 256])
        bonus = sb("bonus", [P, TT, 256])
        A8 = lambda n: sb(n, [P, 8, P])
        Tm, Ut, DTm, ET = (A8(n) for n in ("Tm", "Ut", "DT", "ET"))
        AT, BT, X, CT = (S["arena"][:, 1024 * i:1024 * (i + 1)].rearrange("p (x c) -> p x c", x=8)
                         for i in range(4))
        bt, kt = sb("bt", [P, 2, P]), sb("kt", [P, 2, P])
        s0 = sb("s0", [P, 2, P])
        R, U = sb("R", [P, 2, P]), sb("U", [P, 2, P])
        mean = sb("mean", [P, TT * 4])
        names = """mixed low_ready low_made sig_ready glog_ready cum_ready ssq_ready ssq_made exp_ready root_req root_ready
            ops_ready vt_made vt_ready bonus_made mats_a mats_a_out mats_b mats_b_out mats_d mats_d_out first_ready ct_ready
            x_made x_out tx_made t_ready tok_made tok_out r_made r_out u_made u_out y_made s_made s_out mean_ready
            sd_ready dve_step act_step pool_step""".split()
        sems = semaphores(ctx, nc, " ".join(f"rk_{s}" for s in names))
        s = dict(zip(names, sems))
        bank8 = lambda b: ps[:, b:b + 2, :].rearrange("p a (x c) -> p (a x) c", x=4)
        at8 = lambda b, x: ps[:, b + x // 4, (x % 4) * P:(x % 4 + 1) * P]
        ITEMS = [(c, m, h) for c in range(2) for m in range(2) for h in range(2)]
        cols = lambda c: slice(c * P, (c + 1) * P)
        wide = lambda v: v.unsqueeze(1).to_broadcast([P, 8, P])
        with nc.Block() as block:

            @block.vector
            def _(dve):
                step = Chain(dve, dve_step := s["dve_step"])
                dve.memset(keep[:], 1.0)
                step(dve.tensor_tensor(p[:], RW[:, :, 0:T], RW[:, :, 1:T + 1], ALU.subtract))
                for i in (6, 0, 1, 2, 3, 4, 5):
                    ins = dve.scalar_tensor_tensor(p[:, i, :], p[:, i, :], VL[:, VL_MU + i:VL_MU + i + 1], RW[:, i, 1:T + 1],
                                                   ALU.mult, ALU.add)
                    if i in (6, 5):
                        ins.then_inc(s["mixed"], 1)
                dve.wait_ge(s["mixed"], 2)
                for m in range(2):
                    ins = dve.tensor_scalar(kk[:, m, :], p[:, 2 + m, :], VL[:, VL_KK + m:VL_KK + m + 1], None, ALU.mult)
                step(ins)
                dve.tensor_tensor(sq[:], kk[:], kk[:], ALU.mult).then_inc(s["ssq_ready"], 1)
                dve.wait_ge(s["vt_made"], 1)
                dve.tensor_copy(vt[:], ps[:, 4:6, 0:256])
                dve.wait_ge(s["sig_ready"], 2)
                step(dve.tensor_scalar(gl[:], gl[:], -math.exp(-0.5), None, ALU.mult))
                for m in range(2):
                    for c in range(2):
                        ins = dve.tensor_tensor_scan(cum[:, m, cols(c)], keep[:], gl[:, m, cols(c)], 0.0, ALU.mult, ALU.add)
                step(ins)
                dve.tensor_copy(emid[:], cum[:].rearrange("p m (c t) -> p m c t", c=2)[:, :, :, P // 2 - 1])
                step(dve.tensor_tensor(ce[:], cum[:], gl[:], ALU.subtract))
                for m in range(2):
                    for c in range(2):
                        mid = emid[:, m, c:c + 1]
                        dve.tensor_scalar(cum[:, m, cols(c)], cum[:, m, cols(c)], mid, None, ALU.subtract)
                        ins = dve.tensor_scalar(ce[:, m, cols(c)], ce[:, m, cols(c)], mid, None, ALU.subtract)
                ins.then_inc(s["cum_ready"], 1)
                dve.wait_ge(s["ssq_made"], 1)
                for m in range(2):
                    ins = dve.tensor_scalar(sq[:, m, :], av[:, m, :], 1.0, VL[:, VL_KA + m:VL_KA + m + 1],
                                            ALU.subtract, ALU.mult)
                step(ins)
                step(dve.scalar_tensor_tensor(p[:, 2:4, :], sq[:], 1.0, p[:, 2:4, :], ALU.add, ALU.mult))
                dve.tensor_scalar(sq[:], ps[:, 3, :].rearrange("p (m t) -> p m t", m=2), 1e-12, None,
                                  ALU.add).then_inc(s["root_req"], 1)
                dve.wait_ge(s["root_ready"], 1)
                step(dve.reciprocal(sq[:], sq[:]))
                step(dve.tensor_tensor(kk[:], kk[:], sq[:], ALU.mult))
                step(dve.tensor_tensor(av[:], av[:], kk[:], ALU.mult))
                for m in range(2):
                    ins = dve.scalar_tensor_tensor(sq[:, m, :], p[:, m, :], VL[:, VL_RK + m:VL_RK + m + 1], p[:, 2 + m, :],
                                                   ALU.mult, ALU.mult)
                step(ins)
                dve.wait_ge(s["exp_ready"], 1)
                dve.tensor_tensor(kk[:], kk[:], ce[:], ALU.mult)
                dve.tensor_tensor(av[:], av[:], e3[:], ALU.mult)
                dve.tensor_tensor(p[:, 2:4, :], p[:, 2:4, :], e3[:], ALU.mult)
                step(dve.tensor_tensor(p[:, 0:2, :], p[:, 0:2, :], e1[:], ALU.mult))
                for h in range(2):
                    dve.tensor_scalar(bm[:, h], av[:], hm2[:, h:h + 1], None, ALU.mult)
                    ins = dve.tensor_scalar(km[:, h], p[:, 2:4, :], hm2[:, h:h + 1], None, ALU.mult)
                ins.then_inc(s["ops_ready"], 1)
                dve.wait_ge(s["mats_a"], 1)
                step(dve.tensor_copy(AT, bank8(0)))
                step(dve.tensor_tensor(Tm[:], bank8(2), wide(masks[:, 1, 1, :]), ALU.mult))
                step(dve.tensor_tensor(Tm[:], wide(ident[:]), Tm[:], ALU.subtract))
                step(dve.tensor_tensor(Ut[:], AT, wide(masks[:, 0, 1, :]), ALU.mult))
                dve.tensor_tensor(Ut[:], wide(ident[:]), Ut[:], ALU.subtract).then_inc(s["first_ready"], 1)
                dve.wait_ge(s["first_ready"], 1)
                for l in range(2, LEVELS + 1):
                    step(dve.tensor_tensor(CT, AT, wide(masks[:, 0, l, :]), ALU.mult))
                    dve.sem_inc(s["ct_ready"], 1)
                    if l == 2:
                        dve.wait_ge(s["mats_b"], 1)
                        step(dve.tensor_tensor(BT, bank8(4), wide(S["triu_strict"][:]), ALU.mult))
                        step(dve.tensor_tensor(DTm[:], bank8(6), wide(triu[:]), ALU.mult))
                        dve.sem_inc(s["mats_b_out"], 1)
                        dve.wait_ge(s["mats_d"], 1)
                        step(dve.tensor_tensor(ET[:], bank8(4), wide(triu[:]), ALU.mult))
                        dve.sem_inc(s["mats_d_out"], 1)
                    dve.wait_ge(s["tx_made"], l - 1)
                    dve.tensor_tensor(Tm[:], Tm[:], bank8(2), ALU.subtract)
                    dve.tensor_tensor(Ut[:], Ut[:], bank8(6), ALU.subtract).then_inc(s["t_ready"], 1)
                    dve.wait_ge(s["t_ready"], l - 1)
                dve.wait_ge(s["tok_made"], 1)
                dve.tensor_copy(bt[:], ps[:, 4, 0:256].rearrange("p (m c) -> p m c", m=2))
                dve.tensor_copy(kt[:], ps[:, 4, 256:512].rearrange("p (m c) -> p m c", m=2)).then_inc(s["tok_out"], 1)
                for c in range(2):
                    dve.wait_ge(s["r_made"], c + 1)
                    dve.tensor_copy(R[:], ps[:, 0, 0:256].rearrange("p (m c) -> p m c", m=2)).then_inc(s["r_out"], 1)
                    dve.wait_ge(s["u_made"], c + 1)
                    dve.tensor_scalar(U[:], ps[:, 1, 0:256].rearrange("p (m c) -> p m c", m=2), -1.0, None,
                                      ALU.mult).then_inc(s["u_out"], 1)
                    if c == 0:
                        dve.wait_ge(s["s_made"], 1)
                        for m in range(2):
                            ins = dve.scalar_tensor_tensor(s0[:, m, :], ps[:, 5, m * P:(m + 1) * P],
                                                           e1[:, m, P - 1:P], blockones[:], ALU.mult, ALU.mult)
                        step(ins)
                        for m in range(2):
                            ins = dve.tensor_scalar(s0[:, m, :], s0[:, m, :], emid[:, m, 1:2], None, ALU.mult)
                        ins.then_inc(s["s_out"], 1)
                dve.wait_ge(s["y_made"], 2)
                y = YT[:, :, BW:BW + 256]
                yh = lambda v: v.rearrange("p (h c) -> p h c", c=HD64)
                step(dve.tensor_copy(y, ps[:, 2:4, 0:256]))
                for a in range(TT):
                    ins = dve.tensor_reduce(mean[:, 4 * a:4 * a + 4], yh(YT[:, a, BW:BW + 256]), AX.X, ALU.add)
                step(ins)
                step(dve.tensor_scalar(mean[:], mean[:], 1.0 / HD64, None, ALU.mult))
                for a in range(TT):
                    v = yh(YT[:, a, BW:BW + 256])
                    ins = dve.tensor_tensor(v, v, mean[:, 4 * a:4 * a + 4].unsqueeze(2).to_broadcast([P, 4, HD64]), ALU.subtract)
                step(ins)
                sqt = bm[:].rearrange("p a b t -> p (a b t)")[:, 0:512].rearrange("p (a c) -> p a c", a=2)
                step(dve.tensor_tensor(sqt, y, y, ALU.mult))
                for a in range(TT):
                    ins = dve.tensor_reduce(mean[:, 4 * a:4 * a + 4], yh(sqt[:, a, :]), AX.X, ALU.add)
                step(ins)
                dve.tensor_scalar(mean[:], mean[:], 1.0 / HD64, 64e-5, ALU.mult, ALU.add).then_inc(s["mean_ready"], 1)
                dve.wait_ge(s["sd_ready"], 1)
                step(dve.reciprocal(mean[:], mean[:]))
                for a in range(TT):
                    v = yh(YT[:, a, BW:BW + 256])
                    ins = dve.tensor_tensor(v, v, mean[:, 4 * a:4 * a + 4].unsqueeze(2).to_broadcast([P, 4, HD64]), ALU.mult)
                step(ins)
                row = lambda at: RB[:, at:at + 256].unsqueeze(1).to_broadcast([P, TT, 256])
                step(dve.tensor_tensor(y, y, row(RB_LNG), ALU.mult))
                step(dve.tensor_tensor(y, y, row(RB_LNB), ALU.add))
                dve.wait_ge(s["bonus_made"], 1)
                step(dve.tensor_tensor(bonus[:], ps[:, 6:8, 0:256], vt[:], ALU.mult))
                step(dve.tensor_tensor(y, y, bonus[:], ALU.add))
                dve.tensor_tensor(y, y, gt[:], ALU.mult)

            @block.scalar
            def _(act):
                act.wait_ge(s["mixed"], 1)
                act.activation(lact[0:32, :], p[0:32, 6, :], ACT.Tanh)
                act.activation(lact[32:64, :], p[32:64, 6, :], ACT.Copy)
                act.activation(lact[64:128, :], p[64:128, 6, :], ACT.Sigmoid).then_inc(s["low_ready"], 1)
                act.wait_ge(s["low_made"], 1)
                for m in range(2):
                    act.activation(gl[:, m, :], ps[:, 0, m * T:(m + 1) * T], ACT.Sigmoid, bias=VL[:, VL_W0 + m:VL_W0 + m + 1])
                    act.activation(av[:, m, :], ps[:, 1, m * T:(m + 1) * T], ACT.Sigmoid,
                                   bias=VL[:, VL_A0 + m:VL_A0 + m + 1]).then_inc(s["sig_ready"], 1)
                act.activation(gt[:], ps[:, 2, :].rearrange("p (a c) -> p a c", a=2), ACT.Copy)
                act.wait_ge(s["cum_ready"], 1)
                act.activation(e1[:], cum[:], ACT.Exp)
                act.activation(e3[:], cum[:], ACT.Exp, scale=-1.0)
                act.activation(ce[:], ce[:], ACT.Exp)
                act.activation(emid[:], emid[:], ACT.Exp).then_inc(s["exp_ready"], 1)
                act.wait_ge(s["root_req"], 1)
                act.activation(sq[:], sq[:], ACT.Sqrt).then_inc(s["root_ready"], 1)
                for l in range(2, LEVELS + 1):
                    act.wait_ge(s["x_made"], l - 1)
                    act.activation(X, bank8(0), ACT.Copy).then_inc(s["x_out"], 1)
                act.wait_ge(s["mean_ready"], 1)
                act.activation(mean[:], mean[:], ACT.Sqrt).then_inc(s["sd_ready"], 1)

            @block.tensor
            def _(pe):
                pe.wait_ge(s["low_ready"], 1)
                for m in range(2):
                    pe.matmul(ps[:, 0, m * T:(m + 1) * T], LR[:, 0, m * P:(m + 1) * P], lact[:], start=True, stop=True)
                    pe.matmul(ps[:, 1, m * T:(m + 1) * T], LR[:, 1, m * P:(m + 1) * P], lact[:], start=True, stop=True)
                for a in range(TT):
                    ins = pe.matmul(ps[:, 2, a * T:(a + 1) * T], lact[:, a * P:(a + 1) * P], LR[:, 2, :], start=True, stop=True)
                ins.then_inc(s["low_made"], 1)
                pe.wait_ge(s["mixed"], 2)
                for a in range(TT):
                    for m in range(2):
                        ins = pe.transpose(ps[:, 4 + a, m * P:(m + 1) * P], p[:, 4 + m, a * P:(a + 1) * P], ident[:])
                ins.then_inc(s["vt_made"], 1)
                pe.wait_ge(s["ssq_ready"], 1)
                pe.matmul(ps[:, 3, :], blockones[:], sq[:].rearrange("p m t -> p (m t)"), start=True,
                          stop=True).then_inc(s["ssq_made"], 1)
                pe.wait_ge(s["ops_ready"], 1)
                for x, (c, m, h) in enumerate(ITEMS):
                    pe.matmul(at8(0, x), bm[:, h, m, cols(c)], kk[:, m, cols(c)], start=True, stop=True)
                    ins = pe.matmul(at8(2, x), kk[:, m, cols(c)], bm[:, h, m, cols(c)], start=True, stop=True)
                ins.then_inc(s["mats_a"], 1)
                for x, (c, m, h) in enumerate(ITEMS):
                    pe.matmul(at8(4, x), km[:, h, m, cols(c)], kk[:, m, cols(c)], start=True, stop=True)
                    ins = pe.matmul(at8(6, x), bm[:, h, m, cols(c)], p[:, m, cols(c)], start=True, stop=True)
                ins.then_inc(s["mats_b"], 1)
                pe.wait_ge(s["mats_b_out"], 1)
                for x, (c, m, h) in enumerate(ITEMS):
                    ins = pe.matmul(at8(4, x), km[:, h, m, cols(c)], p[:, m, cols(c)], start=True, stop=True)
                ins.then_inc(s["mats_d"], 1)
                for l in range(2, LEVELS + 1):
                    pe.wait_ge(s["ct_ready"], l - 1)
                    for x in range(8):
                        ins = pe.matmul(at8(0, x), CT[:, x, :], Tm[:, x, :], start=True, stop=True)
                    ins.then_inc(s["x_made"], 1)
                    pe.wait_ge(s["x_out"], l - 1)
                    for x in range(8):
                        pe.matmul(at8(2, x), Ut[:, x, :], X[:, x, :], start=True, stop=True)
                        ins = pe.matmul(at8(6, x), X[:, x, :], Ut[:, x, :], start=True, stop=True)
                    ins.then_inc(s["tx_made"], 1)
                pe.wait_ge(s["t_ready"], LEVELS - 1)
                pe.wait_ge(s["mats_d_out"], 1)
                for m in range(2):
                    pe.transpose(ps[:, 4, m * P:(m + 1) * P], av[:, m, 0:P], ident[:])
                    ins = pe.transpose(ps[:, 4, 256 + m * P:256 + (m + 1) * P], p[:, 2 + m, 0:P], ident[:])
                ins.then_inc(s["tok_made"], 1)
                for a in range(TT):
                    for m in range(2):
                        ins = pe.matmul(ps[:, 6 + a, m * P:(m + 1) * P], sq[:, m, a * P:(a + 1) * P], blockones[:],
                                        start=True, stop=True)
                ins.then_inc(s["bonus_made"], 1)
                hc = lambda m, h: slice(m * P + h * HD64, m * P + (h + 1) * HD64)
                for c in range(2):
                    if c:
                        pe.wait_ge(s["s_out"], 1)
                    for m in range(2):
                        if c:
                            pe.matmul(ps[:, 0, m * P:(m + 1) * P], kk[:, m, cols(1)], s0[:, m, :], start=(m == 0), stop=False,
                                      skip_group_check=True)
                        for h in range(2):
                            ins = pe.matmul(ps[:, 0, hc(m, h)], BT[:, 4 * c + 2 * m + h, :], vt[:, c, hc(m, h)],
                                            start=(c == 0), stop=True, skip_group_check=True)
                    ins.then_inc(s["r_made"], 1)
                    pe.wait_ge(s["r_out"], c + 1)
                    for m in range(2):
                        for h in range(2):
                            ins = pe.matmul(ps[:, 1, hc(m, h)], Ut[:, 4 * c + 2 * m + h, :], R[:, m, h * HD64:(h + 1) * HD64],
                                            start=True, stop=True)
                    ins.then_inc(s["u_made"], 1)
                    pe.wait_ge(s["u_out"], c + 1)
                    if c == 0:
                        pe.wait_ge(s["tok_out"], 1)
                        for m in range(2):
                            pe.matmul(ps[:, 5, m * P:(m + 1) * P], bt[:, m, :], U[:, m, :], start=True, stop=False)
                            ins = pe.matmul(ps[:, 5, m * P:(m + 1) * P], kt[:, m, :], vt[:, 0, m * P:(m + 1) * P],
                                            start=False, stop=True)
                        ins.then_inc(s["s_made"], 1)
                    for m in range(2):
                        if c:
                            pe.matmul(ps[:, 3, m * P:(m + 1) * P], p[:, m, cols(1)], s0[:, m, :], start=(m == 0), stop=False,
                                      skip_group_check=True)
                        for h in range(2):
                            x = 4 * c + 2 * m + h
                            pe.matmul(ps[:, 2 + c, hc(m, h)], DTm[:, x, :], U[:, m, h * HD64:(h + 1) * HD64],
                                      start=(c == 0), stop=False, skip_group_check=True)
                            ins = pe.matmul(ps[:, 2 + c, hc(m, h)], ET[:, x, :], vt[:, c, hc(m, h)], start=False, stop=True,
                                            skip_group_check=True)
                    ins.then_inc(s["y_made"], 1)
        return sems


def output_projection(nc, S, ring, l):
    ps, ident, YT, YF, t = S["ps"], S["ident"], S["YT"], S["YF"], S["t"]
    with ExitStack() as ctx:
        turned, yf_ready, used = sems = semaphores(ctx, nc, "op_turned op_yf_ready op_used")
        with nc.Block() as block:

            @block.tensor
            def _(pe):
                for a in range(TT):
                    for d in range(DT):
                        ins = pe.transpose(ps[:, 4 + 2 * a + d // 4, (d % 4) * P:(d % 4 + 1) * P],
                                           YT[:, a, d * P:(d + 1) * P], ident[:])
                    ins.then_inc(turned, 1)
                pe.wait_ge(yf_ready, TT)
                for h in range(2):
                    ring.arrived(pe, C2_WOUT + h)
                    w = ring.view(C2_WOUT + h, DT, CH)
                    for a in range(TT):
                        for k in range(DT):
                            ins = pe.matmul(ps[:, 2 * a + h, :], YF[:, k, a * P:(a + 1) * P], w[:, k, :],
                                            start=(k == 0), stop=(k == DT - 1))
                    ins.then_inc(ring.used, 1)

            @block.scalar
            def _(act):
                for a in range(TT):
                    act.wait_ge(turned, a + 1)
                    act.activation(YF[:, :, a * P:(a + 1) * P],
                                   ps[:, 4 + 2 * a:6 + 2 * a, :].rearrange("p a (d t) -> p (a d) t", d=4),
                                   ACT.Copy).then_inc(yf_ready, 1)
        return sems


def route(nc, S):
    ps, XT, WR, BR, gates, rank = S["ps"], S["XT"], S["WR"], S["BR"], S["gates"], S["rank"]
    with ExitStack() as ctx:
        sb = lambda n, s: ctx.enter_context(nc.sbuf_tensor(f"rt_{n}", s, F32))
        lg = sb("lg", [P, TT, 36])
        keep = sb("keep", [P, 8])
        gmax, gsum, m1, m2, ws = (sb(n, [P, TT]) for n in ("gmax", "gsum", "m1", "m2", "ws"))
        eg, ohg, cg = (sb(n, [P, TT, 4]) for n in ("eg", "ohg", "cg"))
        tmp = sb("tmp", [P, TT, 32])
        el, oh1, oh2, c8 = (sb(n, [P, TT, 8]) for n in ("el", "oh1", "oh2", "c8"))
        chosen = sb("chosen", [P, TT, N_EXP])
        most, more = sb("most", [P, 1]), sb("more", [P, 1])
        total = sb("total", [P, 1])
        logits, group_diff, group_exp, pair_diff, pair_exp, chosen_ready, ranked, dve_step = semaphores(
            ctx, nc, "rt_logits rt_group_diff rt_group_exp rt_pair_diff rt_pair_exp rt_chosen_ready rt_ranked rt_dve_step")
        block = ctx.enter_context(nc.Block())

        @block.tensor
        def _(pe):
            for a in range(TT):
                for k in range(DT):
                    ins = pe.matmul(ps[:, 4, a * 64:a * 64 + 36], XT[:, k, a * P:(a + 1) * P], WR[:, k, :],
                                    start=(k == 0), stop=(k == DT - 1))
            ins.then_inc(logits, 1)
            pe.wait_ge(chosen_ready, 1)
            strict, ones = S["triu_strict"], S["ones"]
            pe.matmul(ps[:, 5, 0:32], strict[:], chosen[:, 0, :], start=True, stop=True)
            pe.matmul(ps[:, 5, 32:64], strict[:], chosen[:, 1, :], start=True, stop=False)
            pe.matmul(ps[:, 5, 32:64], ones[:], chosen[:, 0, :], start=False, stop=True)
            pe.matmul(ps[:, 5, 64:96], ones[:], chosen[:, 0, :], start=True, stop=False)
            pe.matmul(ps[:, 5, 64:96], ones[:], chosen[:, 1, :], start=False, stop=True).then_inc(ranked, 1)

        @block.scalar
        def _(act):
            act.wait_ge(group_diff, 1)
            act.activation(eg[:], eg[:], ACT.Exp).then_inc(group_exp, 1)
            act.wait_ge(pair_diff, 1)
            act.activation(ws[:], ws[:], ACT.Exp).then_inc(pair_exp, 1)

        @block.vector
        def _(dve):
            step = Chain(dve, dve_step)
            wide = lambda v, n: v.unsqueeze(2).to_broadcast([P, TT, n])

            def first_of(out, count, values, best, n):
                step(dve.tensor_tensor(out[:], values, wide(best[:], n), ALU.is_ge))
                for a in range(TT):
                    ins = dve.tensor_tensor_scan(count[:, a, :], keep[:, 0:n], out[:, a, :], 0.0, ALU.mult, ALU.add)
                step(ins)
                step(dve.tensor_scalar(count[:], count[:], 1.0, None, ALU.is_equal))
                step(dve.tensor_tensor(out[:], out[:], count[:], ALU.mult))

            dve.memset(keep[:], 1.0)
            dve.wait_ge(logits, 1)
            step(dve.tensor_tensor(lg[:], ps[:, 4, 0:128].rearrange("p (a n) -> p a n", a=TT)[:, :, 0:36],
                                   BR[:].unsqueeze(1).to_broadcast([P, TT, 36]), ALU.add))
            step(dve.tensor_reduce(gmax[:], lg[:, :, 0:4], AX.X, ALU.max))
            dve.tensor_tensor(eg[:], lg[:, :, 0:4], wide(gmax[:], 4), ALU.subtract).then_inc(group_diff, 1)
            first_of(ohg, cg, lg[:, :, 0:4], gmax, 4)
            for a in range(TT):
                ins = dve.tensor_tensor(tmp[:, a, :].rearrange("p (g e) -> p g e", g=4),
                                        lg[:, a, 4:36].rearrange("p (g e) -> p g e", g=4),
                                        ohg[:, a, :].unsqueeze(2).to_broadcast([P, 4, 8]), ALU.mult)
            step(ins)
            step(dve.tensor_reduce(el[:], tmp[:].rearrange("p a (g e) -> p a e g", g=4), AX.X, ALU.add))
            step(dve.tensor_reduce(m1[:], el[:], AX.X, ALU.max))
            first_of(oh1, c8, el[:], m1, 8)
            step(dve.scalar_tensor_tensor(el[:], oh1[:], -1.0e30, el[:], ALU.mult, ALU.add))
            step(dve.tensor_reduce(m2[:], el[:], AX.X, ALU.max))
            dve.tensor_tensor(ws[:], m2[:], m1[:], ALU.subtract).then_inc(pair_diff, 1)
            first_of(oh2, c8, el[:], m2, 8)
            dve.wait_ge(group_exp, 1)
            step(dve.tensor_reduce(gsum[:], eg[:], AX.X, ALU.add))
            dve.wait_ge(pair_exp, 1)
            step(dve.tensor_scalar(m1[:], ws[:], 1.0, None, ALU.add))
            step(dve.tensor_tensor(m1[:], m1[:], gsum[:], ALU.mult))
            step(dve.reciprocal(m1[:], m1[:]))
            step(dve.tensor_tensor(m2[:], ws[:], m1[:], ALU.mult))
            dve.tensor_tensor(oh1[:], oh1[:], wide(m1[:], 8), ALU.mult)
            step(dve.tensor_tensor(oh2[:], oh2[:], wide(m2[:], 8), ALU.mult))
            step(dve.tensor_tensor(oh1[:], oh1[:], oh2[:], ALU.add))
            dve.memset(gates[:, :, N_EXP:], 0.0)
            dve.memset(rank[:, :, N_EXP:], -1.0)
            for a in range(TT):
                ins = dve.tensor_tensor(gates[:, a, 0:N_EXP].rearrange("p (g e) -> p g e", g=4),
                                        ohg[:, a, :].unsqueeze(2).to_broadcast([P, 4, 8]),
                                        oh1[:, a, :].unsqueeze(1).to_broadcast([P, 4, 8]), ALU.mult)
            step(ins)
            dve.tensor_scalar(chosen[:], gates[:, :, 0:N_EXP], 0.0, None, ALU.is_gt).then_inc(chosen_ready, 1)
            dve.wait_ge(ranked, 1)
            v = rank[:, :, 0:N_EXP]
            step(dve.scalar_tensor_tensor(v, ps[:, 5, 0:64].rearrange("p (a e) -> p a e", a=TT), 1.0, chosen[:],
                                          ALU.add, ALU.mult))
            dve.tensor_scalar(v, v, 1.0, None, ALU.subtract)
            step(dve.tensor_reduce(most[:], ps[:, 5, 64:96], AX.X, ALU.max))
            step(dve.tensor_scalar(total[:], most[:], float(CAP), 1.0, ALU.is_gt, ALU.add))
            for n in range(2, T // CAP):
                step(dve.tensor_scalar(more[:], most[:], float(CAP * n), None, ALU.is_gt))
                step(dve.tensor_tensor(total[:], total[:], more[:], ALU.add))
            dve.tensor_copy(S["rounds"][:], total[:])


EPB = 4
PAIRS = EPB // 2
CPB = 3 * EPB
NB = N_EXP // EPB
CAP = 64


def experts(nc, S, l):
    ps, zeros = S["ps"], S["zeros"]
    with ExitStack() as ctx:
        zero_ready, = semaphores(ctx, nc, "ex_zero_ready")
        block = ctx.enter_context(nc.Block())

        @block.vector
        def _(dve):
            dve.memset(zeros[:], 0.0).then_inc(zero_ready, 1)

        @block.tensor
        def _(pe):
            pe.wait_ge(zero_ready, 1)
            for b in range(4):
                pe.matmul(ps[:, b, :], zeros[:, 0:P], zeros[:], start=True, stop=False, skip_group_check=True)

    rounds = nc.values_load(S["rounds"][0:1, 0:1], min_val=1, max_val=T // CAP)
    with nc.Fori(0, rounds) as _:
        expert_round(nc, S, l)


def expert_round(nc, S, l):
    ps, ident, X, gates, rank, iota, t = (S[n] for n in ("ps", "ident", "X", "gates", "rank", "iota", "t"))
    xc = S["XT"]
    ye = S["YT"]
    with ExitStack() as ctx:
        sb = lambda n, s: ctx.enter_context(nc.sbuf_tensor(f"ex_{n}", s, F32))
        more = sb("more", [P, EXTRA_SLOTS, SLOT])
        slots = [S["weights"][:, i, :] for i in range(SLOTS)] + [more[:, i, :] for i in range(EXTRA_SLOTS)]
        NS = len(slots)
        sel = sb("sel", [P, TT, EPB, CAP])
        selg = sb("selg", [P, TT, EPB, CAP])
        GT = sb("GT", [P, PAIRS, T])
        sg, hs = sb("sg", [P, E_FF]), sb("hs", [P, E_FF])
        hT = sb("hT", [P, 4, P])
        names = [f"landed{i}" for i in range(NS)] + """used sel_ready selg_ready gathered xc_low_ready xc_high_ready
            gt_turned gt_ready silu_ready h_ready turned ht_ready ye_low_ready ye_high_ready dve_step""".split()
        sems = semaphores(ctx, nc, " ".join(f"ex_{s}" for s in names))
        landed = sems[:NS]
        (used, sel_ready, selg_ready, gathered, xc_low_ready, xc_high_ready, gt_turned, gt_ready, silu_ready, h_ready,
         turned, ht_ready, ye_low_ready, ye_high_ready, dve_step) = sems[NS:]
        block = ctx.enter_context(nc.Block())
        bank_pair = lambda b: ps[:, b:b + 2, :].rearrange("p a (k c) -> p (a k) c", c=EPB * CAP)

        def view(j, a, b):
            return slots[j % NS].rearrange("p (a b) -> p a b", a=a) if a * b == SLOT else slots[j % NS][:, 0:a * b]

        def chunk_of(j):
            return 2 * (j // 6) + j % 2, (j % 6) // 2

        @block.sync
        def _(sp):
            def load(i, j):
                e, part = chunk_of(j)
                a, b = (DT, CH) if part < 2 else (4, D)
                sp.dma_start(view(j, a, b), expert_chunk(t, l * N_EXP + EPB * i + e, part)).then_inc(landed[j % NS], 16)

            for j in range(CPB):
                if j >= NS:
                    sp.wait_ge(used, j - NS + 1)
                load(0, j)
            with sp.Fori(1, NB) as i:
                for j in range(CPB):
                    sp.wait_ge(used, CPB * i + (j - NS + 1))
                    load(i, j)

        @block.tensor
        def _(pe):
            def arrived(i, j):
                pe.wait_ge(landed[j % NS], (16 * CPB // NS) * i + 16 * (j // NS + 1))

            def gather(i):
                pe.wait_ge(sel_ready, i + 1)
                for part in range(2):
                    for k in range(4 * part, 4 * part + 4):
                        out = bank_pair(4 + 2 * part)[:, k % 4, :]
                        for a in range(TT):
                            ins = pe.matmul(out, X[:, a, k * P:(k + 1) * P], sel[:, a].rearrange("p e c -> p (e c)"),
                                            start=(a == 0), stop=(a == TT - 1))
                    ins.then_inc(gathered, 1)

            def expert_products(i, p, part):
                j = 6 * p + 2 * part
                a, b = (DT, CH)
                w = [view(j + h, a, b) for h in range(2)]
                for h in range(2):
                    arrived(i, j + h)
                for k in range(DT):
                    if p == 0 and part == 0 and k % 4 == 0:
                        pe.wait_ge((xc_low_ready, xc_high_ready)[k // 4], i + 1)
                    for h in range(2):
                        e = 2 * p + h
                        ins = pe.matmul(ps[h * CAP:(h + 1) * CAP, 4 + part, :], xc[:, k, e * CAP:(e + 1) * CAP],
                                        w[h][:, k, :], start=(k == 0), stop=(k == DT - 1))
                        if k == DT - 1:
                            ins.then_inc(used, 1)

            def turn_gates(i, p):
                pe.wait_ge(selg_ready, PAIRS * i + p + 1)
                if p:
                    pe.wait_ge(ye_low_ready, PAIRS * i + p)
                    pe.wait_ge(ye_high_ready, PAIRS * i + p)
                for a in range(TT):
                    ins = pe.transpose(ps[:, 6, a * P:(a + 1) * P],
                                       selg[:, a, 2 * p:2 * p + 2, :].rearrange("p e c -> p (e c)"), ident[:])
                ins.then_inc(gt_turned, 1)

            def down(i, p):
                j = 6 * p + 4
                w = [view(j + h, 4, D) for h in range(2)]
                for h in range(2):
                    arrived(i, j + h)
                pe.wait_ge(gt_ready, PAIRS * i + p + 1)
                pe.wait_ge(ht_ready, PAIRS * i + p + 1)
                for half in range(2):
                    for f in range(4):
                        for h in range(2):
                            ins = pe.matmul(ps[h * CAP:(h + 1) * CAP, 6 + half, :], hT[:, f, h * CAP:(h + 1) * CAP],
                                            w[h][:, f, half * CH:(half + 1) * CH], start=(f == 0), stop=(f == 3))
                            if half == 1 and f == 3:
                                ins.then_inc(used, 1)

            def turn_hidden(i, p):
                pe.wait_ge(h_ready, PAIRS * i + p + 1)
                for f in range(4):
                    ins = pe.transpose(ps[:, 4, f * P:(f + 1) * P], hs[:, f * P:(f + 1) * P], ident[:])
                ins.then_inc(turned, 1)

            def scatter(i, p):
                pe.wait_ge(ye_low_ready, PAIRS * i + p + 1)
                pe.wait_ge(ye_high_ready, PAIRS * i + p + 1)
                for a in range(TT):
                    for half in range(2):
                        pe.matmul(ps[:, 2 * a + half, :], GT[:, p, a * P:(a + 1) * P], ye[:, p, half * CH:(half + 1) * CH],
                                  start=False, stop=False, skip_group_check=True)

            with pe.Fori(0, NB) as i:
                gather(i)
                for p in range(PAIRS):
                    if p == 0:
                        expert_products(i, p, 0)
                        turn_gates(i, p)
                    else:
                        turn_gates(i, p)
                        expert_products(i, p, 0)
                    expert_products(i, p, 1)
                    if p:
                        scatter(i, p - 1)
                    turn_hidden(i, p)
                    down(i, p)
                scatter(i, PAIRS - 1)

        @block.scalar
        def _(act):
            with act.Fori(0, NB) as i:
                act.wait_ge(gathered, 2 * i + 1)
                act.activation(xc[:, 0:4, :], bank_pair(4), ACT.Copy).then_inc(xc_low_ready, 1)
                for p in range(PAIRS):
                    act.wait_ge(gt_turned, PAIRS * i + p + 1)
                    act.activation(GT[:, p, :], ps[:, 6, 0:T], ACT.Copy).then_inc(gt_ready, 1)
                    act.wait_ge(used, CPB * i + (6 * p + 2))
                    act.activation(sg[:], ps[:, 4, :], ACT.Silu).then_inc(silu_ready, 1)
                    act.wait_ge(turned, PAIRS * i + p + 1)
                    act.activation(hT[:], ps[:, 4, :].rearrange("p (f t) -> p f t", f=4), ACT.Copy).then_inc(ht_ready, 1)
                    act.wait_ge(used, CPB * i + (6 * p + 6))
                    act.activation(ye[:, p, 0:CH], ps[:, 6, :], ACT.Copy).then_inc(ye_low_ready, 1)

        @block.vector
        def _(dve):
            def select(i, out, gated, sem):
                for e in range(EPB):
                    for a in range(TT):
                        r = rank[:, a, bass.ds(EPB * i + e, 1)]
                        if gated:
                            ins = dve.tensor_scalar(out[:, a, e, :], iota[:], r, gates[:, a, bass.ds(EPB * i + e, 1)],
                                                    ALU.is_equal, ALU.mult)
                        else:
                            ins = dve.tensor_scalar(out[:, a, e, :], iota[:], r, None, ALU.is_equal)
                    if not gated and e == EPB - 1 or gated and e % 2 == 1:
                        ins.then_inc(sem, 1)

            select(0, sel, False, sel_ready)
            select(0, selg, True, selg_ready)
            with dve.Fori(0, NB) as i:
                dve.wait_ge(gathered, 2 * i + 2)
                dve.tensor_copy(xc[:, 4:8, :], bank_pair(6)).then_inc(xc_high_ready, 1)
                select(i + 1, sel, False, sel_ready)
                for p in range(PAIRS):
                    dve.wait_ge(silu_ready, PAIRS * i + p + 1)
                    dve.wait_ge(used, CPB * i + (6 * p + 4))
                    dve.tensor_tensor(hs[:], sg[:], ps[:, 5, :], ALU.mult).then_inc(h_ready, 1)
                    dve.wait_ge(used, CPB * i + (6 * p + 6))
                    dve.tensor_copy(ye[:, p, CH:D], ps[:, 7, :]).then_inc(ye_high_ready, 1)
                dve.wait_ge(gt_turned, PAIRS * (i + 1))
                select(i + 1, selg, True, selg_ready)
            dve.wait_ge(selg_ready, PAIRS * (NB + 1))
            dve.tensor_scalar(rank[:], rank[:], float(CAP), None, ALU.subtract)


def program(nc, t, out):
    t = dict(t)
    with ExitStack() as ctx:
        sb = lambda n, s, c=ctx: c.enter_context(nc.sbuf_tensor(n, s, F32))
        S = {"t": t, "ps": ctx.enter_context(nc.psum_tensor("ps", [P, 8, 512], F32))}
        buf = S["weights"] = sb("weights", [P, SLOTS, SLOT])
        for name, shape in (("ident", [P, P]), ("ones", [P, P]), ("masks", [P, 2, LEVELS + 1, P]), ("X", [P, TT, D])):
            S[name] = sb(name, shape)
        with ExitStack() as one:
            first_block(nc, t, S, Ring(one, nc, "ring", buf), lambda n, s: sb(n, s, one))
        with ExitStack() as two:
            second_block(nc, t, S, Ring(two, nc, "ring2", buf), lambda n, s: sb(n, s, two),
                         lambda n, s: two.enter_context(nc.sbuf_tensor(n, s, mybir.dt.int32)))
        with ExitStack() as last:
            (stored,) = semaphores(last, nc, "stored")
            block = last.enter_context(nc.Block())

            @block.sync
            def _(sp):
                sp.dma_start(out[0].rearrange("(a p) d -> p a d", p=P), S["X"][:]).then_inc(stored, 16)
                sp.wait_ge(stored, 16)


def first_block(nc, t, S, ring, sb):
    for name, shape in (("H", [P, DT, 2 * T]), ("modv", [P, 2, N_MOD * DT]), ("VA", [P, VA_ROWS]),
                        ("VB", [P, VB_ROWS]), ("VC", [64, 4])):
        S[name] = sb(name, shape)
    chunks = first_block_chunks(t)
    with ExitStack() as ctx:
        (set_ones,) = semaphores(ctx, nc, "set_ones")
        block = ctx.enter_context(nc.Block())

        @block.gpsimd
        def _(pool):
            pool.memset(S["ones"][:], 1.0).then_inc(set_ones, 1)

    modulation(nc, t, S, ring, chunks)

    def split_norm(c, W, part, name, room=None):
        for x in ("NH", "NL"):
            S[x] = c.enter_context(nc.sbuf_tensor(f"{name}_{x}", [P, DT, W], F32R))
        norm_modulate(nc, S, W, part, name, room)
        for x in ("w_high", "w_low"):
            S[x] = c.enter_context(nc.sbuf_tensor(f"{name}_{x}", [P, SplitTiles.DEPTH * CH], F32R))

    with ExitStack() as half:
        split_norm(half, 2 * T, 0, "n0")
        feed_forward(nc, S, ring, chunks, 2 * T, 2, C_FFN0, "f0")
    with ExitStack() as mix:
        for name, shape in (("V", [P, 2 * TT, 512]), ("SG", [P, 2, HEADS_A, 2 * T]), ("MG", [P, 2 * DT, T]),
                            ("Q", [P, HEADS_A, T]), ("G", [P, HEADS_A, T]), ("HY", [P, 12, T + 2])):
            S[name] = mix.enter_context(nc.sbuf_tensor(name, shape, F32))
        with ExitStack() as half:
            split_norm(half, 2 * T, 3, "n1", S["SG"][:].rearrange("p r h t -> p (r h) t"))
            input_projection(nc, S, ring, chunks)
        S["N"] = mix.enter_context(nc.sbuf_tensor("N", [P, DT, 2 * T], F32))
        hgrn2(nc, S)
        S["KS"], S["OB"] = S["SG"], S["Q"]
        with ExitStack() as hy:
            S["CF"] = hy.enter_context(nc.sbuf_tensor("CF", [P, TT, 2 * T], F32))
            S["CI"] = hy.enter_context(nc.sbuf_tensor("CI", [P, 4, T], F32))
            hyena_filters(nc, S)
            hyena_mix(nc, S)
        merge_heads(nc, S, ring, chunks)
    with ExitStack() as half:
        split_norm(half, T, 6, "n2")
        feed_forward(nc, S, ring, chunks, T, 8, C_FFN1, "f1")
    to_tokens(nc, t, S)
    ring.clear(nc)


def second_block(nc, t, S, ring, sb, sb_int):
    for name, shape in (("XT", [P, DT, T]), ("YT", [P, TT, D]), ("RW", [P, 7, T + 1]), ("DTR", [P, TT, 8]),
                        ("VL", [P, VL_ROWS]), ("RB", [P, RB_END]), ("LR", [P, 3, 256]), ("WA2", [16, P]),
                        ("WR", [P, DT, 36]), ("BR", [P, 36]), ("triu", [P, P]), ("triu_strict", [P, P]),
                        ("blockones", [P, P]), ("hm2", [P, 2]), ("hm4", [P, 4]), ("gates", [P, TT, N_EXP + EPB]), ("rank", [P, TT, N_EXP + EPB]), ("iota", [P, CAP]),
                        ("arena", [P, 4400])):
        S[name] = sb(name, shape)
    at = 0
    for name, shape in (("Z", [TT, BW]), ("XBC", [6, T + 3]), ("GV", [TT, 256]), ("GG", [TT, 256])):
        n = shape[0] * shape[1]
        S[name] = S["arena"][:, at:at + n].rearrange("p (a b) -> p a b", a=shape[0])
        at += n
    S["GQ"], S["GK"] = S["arena"][:, at:at + T], S["arena"][:, at + T:at + 2 * T]
    S["GA"] = S["arena"][0:16, at + 2 * T:at + 3 * T]
    S["YF"] = S["arena"][:, 0:DT * T].rearrange("p (k t) -> p k t", k=DT)
    S["rounds"] = sb_int("rounds", [P, 1])
    S["zeros"] = S["arena"][:, 2048:2048 + CH]
    with ExitStack() as ctx:
        const_in, lr_zero = semaphores(ctx, nc, "const_in lr_zero")
        block = ctx.enter_context(nc.Block())

        @block.sync
        def _(sp):
            for name in ("triu", "triu_strict", "blockones", "hm2", "hm4", "iota"):
                sp.dma_start(S[name][:], t["c_" + name]).then_inc(const_in, 16)
            sp.wait_ge(const_in, 96)

        @block.gpsimd
        def _(pool):
            pool.memset(S["LR"][:], 0.0).then_inc(lr_zero, 1)

    residual_norm(nc, S, "l0", t["ln_in_g_2"], t["ln_in_b_2"], False)
    with nc.Fori(0, 2) as l:
        row = lambda name: t[name][bass.ds(l, 1)].rearrange("a n -> (a n)")
        input_projection2(nc, S, ring, l)
        ssd_mixer(nc, S)
        gla_mixer(nc, S)
        rwkv_mixer(nc, S)
        output_projection(nc, S, ring, l)
        residual_norm(nc, S, "l1", row("ln1_g_2"), row("ln1_b_2"), True)
        route(nc, S)
        experts(nc, S, l)
        residual_norm(nc, S, "l2", row("ln2_g_2"), row("ln2_b_2"), True)
        ring.clear(nc)


def constants():
    c = {"c_ident": np.eye(P, dtype=np.float32)}
    c["c_fold"] = (np.arange(P)[:, None] % 32 == np.arange(2)[None]).astype(np.float32)
    quarter, grid_w = D // 4, 64
    omega = 1.0 / (10000.0 ** (np.arange(quarter, dtype=np.float32) / np.float32(quarter)))
    ar = np.arange(T // grid_w, dtype=np.float32)[:, None] * omega
    ac = np.arange(grid_w, dtype=np.float32)[:, None] * omega
    er = np.concatenate([np.sin(ar), np.cos(ar)], -1)
    ec = np.concatenate([np.sin(ac), np.cos(ac)], -1)
    c["c_pos"] = np.concatenate([np.broadcast_to(er[:, None], (T // grid_w, grid_w, D // 2)),
                                 np.broadcast_to(ec[None], (T // grid_w, grid_w, D // 2))], -1)\
        .reshape(T, D).astype(np.float32)
    i = np.arange(P)
    fw = [np.eye(P, dtype=bool)]
    for l in range(LEVELS):
        size = 2 << l
        same = (i[:, None] // size) == (i[None] // size)
        fw.append(same & (i[:, None] % size < size // 2) & (i[None] % size >= size // 2))
    fw = np.stack(fw, 1)
    c["c_masks"] = np.stack([fw, fw.transpose(2, 1, 0)], 1).reshape(P, -1).astype(np.float32)
    p = np.arange(T, dtype=np.float64)
    tn = p / (T - 1)
    ang = (2.0 * math.pi * p / T)[:, None] * np.linspace(1e-4, 15, 16)[None]
    c["c_feat"] = np.concatenate([tn[:, None], np.cos(ang), -np.sin(ang)], -1).T.astype(np.float32)
    deltas = np.abs(np.linspace(math.log(1e-2) / 1.5, math.log(1e-2) / 0.3, BW))
    c["c_window"] = (np.exp(-tn[:, None] * deltas[None]) + 0.05).astype(np.float32)
    theta = math.pi * (2 * np.arange(T) + 1) / (2 * T)
    at = theta[None] * p[:, None]
    c["c_cf"] = np.concatenate([np.cos(at), -np.sin(at)], 1).astype(np.float32)
    at1 = theta[None] * (p[:, None] + 1)
    cg = np.concatenate([np.cos(at1), np.sin(at1)], 1)
    cg[T - 1] = 0.0
    c["c_cg"] = cg.astype(np.float32)
    c["c_ci"] = (np.concatenate([np.cos(at.T), -np.sin(at.T)], 0) / T).astype(np.float32)
    c["c_triu"] = (i[:, None] <= i[None]).astype(np.float32)
    c["c_triu_strict"] = (i[:, None] < i[None]).astype(np.float32)
    c["c_blockones"] = (i[:, None] // 64 == i[None] // 64).astype(np.float32)
    c["c_hm2"] = (i[:, None] // 64 == np.arange(2)[None]).astype(np.float32)
    c["c_hm4"] = (i[:, None] // 32 == np.arange(4)[None]).astype(np.float32)
    c["c_iota"] = np.broadcast_to(np.arange(CAP, dtype=np.float32), (P, CAP)).copy()
    return c


def kernel(**inputs):
    import concourse.bacc as bacc
    from concourse.bass_utils import run_bass_kernel_spmd

    nc = bacc.Bacc("TRN2", target_bir_lowering=False, num_devices=1)
    arrays, t = {}, {}
    for name, a in list(inputs.items()) + list(constants().items()):
        a = np.ascontiguousarray(a)
        arrays[f"in_{name}"] = a
        t[name] = nc.dram_tensor(f"in_{name}", a.shape, mybir.dt.from_np(a.dtype), kind="ExternalInput").ap()
    out = nc.dram_tensor("out", (1, T, D), F32, kind="ExternalOutput").ap()
    program(nc, t, out)
    r = run_bass_kernel_spmd(nc, [arrays], core_ids=[0])
    return r.results[0]["out"]
```

```python
from contextlib import ExitStack
import math

import numpy as np

import concourse.bass as bass
from concourse import mybir

ALU = mybir.AluOpType
ACT = mybir.ActivationFunctionType
AX = mybir.AxisListType
F32 = mybir.dt.float32
F32R = mybir.dt.float32r

P = 128
T = 256
TT = T // P
D = 1024
DT = D // P
CH = 512
SLOT = DT * CH
D_FF = 2816
FT = D_FF // P
N_MOD = 9
HEADS_A = 4
BW = 512
BT = BW // P
RMS_EPS = 1e-6
LN_EPS = 1e-5
HYENA_L1_EPS = 1e-6
LEVELS = 7
STAGE_SEMAPHORES = 160
SLOTS = 4
EXTRA_SLOTS = 2
EXPERT_LANDED = STAGE_SEMAPHORES - SLOTS - EXTRA_SLOTS
LOG_FLOOR = 2.0 ** -63

VA_MODB, VA_C, VA_CCTX, VA_FNORM, VA_CONVB, VA_HYB, VA_HNORM = 0, 72, 80, 88, 96, 108, 116
VA_ROWS = 117
VB_CONVW, VB_LB = 0, 36
VB_ROWS = 52


class Chain:

    def __init__(self, eng, sem):
        self.eng, self.sem, self.n = eng, sem, 0

    def __call__(self, ins):
        self.n += 1
        ins.then_inc(self.sem, 1)
        self.eng.wait_ge(self.sem, self.n)


class Ring:

    def __init__(self, ctx, nc, name, buf):
        self.slots, self.buf = buf.shape[1], buf
        self.landed = [ctx.enter_context(nc.semaphore(f"{name}_landed{s}")) for s in range(self.slots)]
        self.used = ctx.enter_context(nc.semaphore(f"{name}_used"))

    def clear(self, nc):
        nc.all_engine_barrier(sems_to_clear=range(self.landed[0].num, self.used.num + 1))

    def view(self, n, a, b):
        return self.buf[:, n % self.slots, 0:a * b].rearrange("p (a b) -> p a b", a=a)

    def load(self, sp, n, src):
        if n >= self.slots:
            sp.wait_ge(self.used, n - self.slots + 1)
        sp.dma_start(self.view(n, src.shape[1], src.shape[2]), src).then_inc(self.landed[n % self.slots], 16)

    def arrived(self, pe, n):
        pe.wait_ge(self.landed[n % self.slots], 16 * (n // self.slots + 1))


class SplitTiles:

    DEPTH = 4

    def __init__(self, ring, first, shapes, high, low, high_ready, low_ready, tile_used):
        self.ring, self.high_part, self.low_part = ring, high, low
        self.high_ready, self.low_ready, self.tile_used = high_ready, low_ready, tile_used
        self.tiles = [(first + c, k, K, cols) for c, (K, cols) in enumerate(shapes) for k in range(K)]

    def __len__(self):
        return len(self.tiles)

    def source(self, q):
        n, k, K, cols = self.tiles[q]
        return self.ring.view(n, K, cols)[:, k, :]

    def parts(self, q):
        cols = self.tiles[q][3]
        return [x[:, (q % self.DEPTH) * CH:(q % self.DEPTH) * CH + cols] for x in (self.high_part, self.low_part)]

    def upper(self, act, q):
        n, k = self.tiles[q][:2]
        if k == 0:
            self.ring.arrived(act, n)
        if q >= self.DEPTH:
            act.wait_ge(self.tile_used, q - self.DEPTH + 1)
        act.activation(self.parts(q)[0], self.source(q), ACT.Copy).then_inc(self.high_ready, 1)

    def lower(self, dve, q):
        dve.wait_ge(self.high_ready, q + 1)
        high, low = self.parts(q)
        dve.tensor_tensor(low, self.source(q), high.bitcast(F32), ALU.subtract).then_inc(self.low_ready, 1)

    def products(self, pe, q, outs, first, last, tokens_out=False):
        n, k, K, cols = self.tiles[q]
        pe.wait_ge(self.low_ready, q + 1)
        high, low = self.parts(q)
        for j, (out, x_high, x_low) in enumerate(outs):
            c = slice(0, cols) if tokens_out else slice(j * P, (j + 1) * P)
            for i, (w, x) in enumerate(((high, x_high), (high, x_low), (low, x_high))):
                w = w[:, c]
                a, b = (x, w) if tokens_out else (w, x)
                ins = pe.matmul(out, a, b, start=(first and i == 0), stop=(last and i == 2))
            if j == 0 and k == K - 1:
                ins.then_inc(self.ring.used, 1)
        ins.then_inc(self.tile_used, 1)


def semaphores(ctx, nc, names, clear_from=STAGE_SEMAPHORES):
    sems = [ctx.enter_context(nc.semaphore(n, num=STAGE_SEMAPHORES + i)) for i, n in enumerate(names.split())]
    ctx.callback(lambda: nc.all_engine_barrier(
        sems_to_clear=range(clear_from, STAGE_SEMAPHORES + len(sems))))
    return sems


def column_chunks(w, bounds):
    v = w.rearrange("(k p) n -> p k n", p=P)
    return [v[:, :, a:b] for a, b in bounds]


def down_chunks(w):
    v = w.rearrange("(k p) n -> p k n", p=P)
    return [v[:, a:b, h * CH:(h + 1) * CH] for h in range(2) for a, b in ((0, 8), (8, 16), (16, 22))]


def ffn_chunks(wg, wu, wd):
    bounds = [(a, min(a + CH, D_FF)) for a in range(0, D_FF, CH)]
    out = []
    for g, u in zip(column_chunks(wg, bounds), column_chunks(wu, bounds)):
        out += [g, u]
    return out + down_chunks(wd)


FFN_CHUNKS = 18
WIN_ORDER = [0, 1, 2, 8, 9, 10, 11, 3, 4, 5, 6, 7]


def first_block_chunks(t):
    mod = t["mod_w"][0]
    out = column_chunks(mod, [(a, a + CH) for a in range(0, N_MOD * D, CH)])
    out += ffn_chunks(t["ffn_w_gate"][0, 0], t["ffn_w_up"][0, 0], t["ffn_w_down"][0, 0])
    out += column_chunks(t["w_in"][0], [(CH * c, CH * c + CH) for c in WIN_ORDER])
    out += [t["w_proj_a"][0].rearrange("(k p) n -> p k n", p=P), t["w_proj_b"][0].rearrange("(k p) n -> p k n", p=P)]
    out += column_chunks(t["w_out"][0], [(0, CH), (CH, D)])
    out += ffn_chunks(t["ffn_w_gate"][0, 1], t["ffn_w_up"][0, 1], t["ffn_w_down"][0, 1])
    return out


C_MOD = 0
C_FFN0 = 18
C_WIN = C_FFN0 + FFN_CHUNKS
C_PROJ = C_WIN + 12
C_WOUT = C_PROJ + 2
C_FFN1 = C_WOUT + 2
C_END = C_FFN1 + FFN_CHUNKS


def refill(sp, ring, chunks, first, count):
    for n in range(first + ring.slots, min(first + count + ring.slots, len(chunks))):
        ring.load(sp, n, chunks[n])


def modulation(nc, t, S, ring, chunks):
    ps, ident = S["ps"], S["ident"]
    H, modv, VA, VB, VC = S["H"], S["modv"], S["VA"], S["VB"], S["VC"]
    with ExitStack() as ctx:
        rowsA = ctx.enter_context(nc.sbuf_tensor("rowsA", [P, P], F32))
        rowsB = ctx.enter_context(nc.sbuf_tensor("rowsB", [P, P], F32))
        rowsC = ctx.enter_context(nc.sbuf_tensor("rowsC", [4, 64], F32))
        xin = ctx.enter_context(nc.sbuf_tensor("xin", [P, 2 * TT, D], F32))
        pos = ctx.enter_context(nc.sbuf_tensor("pos", [P, TT, D], F32))
        silc = ctx.enter_context(nc.sbuf_tensor("silc", [P, DT, 32], F32))
        rows = ctx.enter_context(nc.sbuf_tensor("mod_rows", [P, 2, CH], F32))
        fold = ctx.enter_context(nc.sbuf_tensor("fold", [P, 2], F32))
        (ident_in, vec_in, x_in, x_ready, vec_turned, vec_out, silc_zero, c_ready, turned, turned_out, rows_out,
         folded, dve_step, *filter_sems) = semaphores(
            ctx, nc, """ident_in vec_in x_in x_ready vec_turned vec_out silc_zero c_ready turned turned_out
            mod_rows_out mod_folded mod_dve_step """ + " ".join(f"hf_{s}" for s in HyenaFilters.SEMAPHORES.split()))
        block = ctx.enter_context(nc.Block())
        step = Chain(nc.vector, dve_step)
        filters = HyenaFilters(ctx, nc, S, filter_sems, step)
        FILTER_FROM = 18 - 1 - filters.STEPS

        @block.sync
        def _(sp):
            sp.dma_start(ident[:], t["c_ident"]).then_inc(ident_in, 16)
            sp.dma_start(fold[:], t["c_fold"]).then_inc(ident_in, 16)
            row = lambda a, n: a.rearrange("(r c) -> r c", c=n)
            for at, src in ((VA_MODB, row(t["mod_b"][0], P)), (VA_C, row(t["c"][0], P)),
                            (VA_CCTX, row(t["c_ctx"], P)), (VA_FNORM, row(t["final_norm_w"], P)),
                            (VA_CONVB, row(t["hyena_conv_b"][0], P)),
                            (VA_HYB, t["hyena_bias"][0].rearrange("o (r c) -> (o r) c", c=P)),
                            (VA_HNORM, t["hgrn_norm_w"])):
                sp.dma_start(rowsA[at:at + src.shape[0], :], src).then_inc(vec_in, 16)
            for at, src in ((VB_CONVW, t["hyena_conv_w"][0].rearrange("j (r c) -> (j r) c", c=P)),
                            (VB_LB, t["hgrn_lb_logits"].rearrange("l d (r c) -> (l d r) c", c=P))):
                sp.dma_start(rowsB[at:at + src.shape[0], :], src).then_inc(vec_in, 16)
            for i, name in enumerate(("hyena_b1", "hyena_freq1", "hyena_b2", "hyena_freq2")):
                sp.dma_start(rowsC[i:i + 1, :], t[name]).then_inc(vec_in, 16)
            sp.dma_start(xin[:, 0:TT, :], t["x"][0].rearrange("(a p) d -> p a d", p=P)).then_inc(x_in, 16)
            sp.dma_start(xin[:, TT:2 * TT, :], t["ctx"][0].rearrange("(a p) d -> p a d", p=P)).then_inc(x_in, 16)
            sp.dma_start(pos[:], t["c_pos"].rearrange("(a p) d -> p a d", p=P)).then_inc(x_in, 16)
            for n in range(ring.slots):
                ring.load(sp, n, chunks[n])
            filters.load(sp)
            refill(sp, ring, chunks, C_MOD, 18)
            sp.wait_ge(filters.stored, 32)

        @block.vector
        def _(dve):
            dve.memset(silc[:], 0.0).then_inc(silc_zero, 1)
            dve.wait_ge(x_in, 48)
            dve.tensor_tensor(xin[:, 0:TT, :], xin[:, 0:TT, :], pos[:], ALU.add).then_inc(x_ready, 1)
            dve.wait_ge(vec_turned, 1)
            dve.tensor_copy(VA[:], ps[:, 7, 0:VA_ROWS]).then_inc(vec_out, 1)
            dve.tensor_copy(VB[:], ps[:, 7, 128:128 + VB_ROWS]).then_inc(vec_out, 1)
            dve.tensor_copy(VC[:], ps[0:64, 7, 256:260]).then_inc(vec_out, 1)
            for i in range(2 * TT * DT // 4):
                a, d = i // 2, 4 * (i % 2)
                dve.wait_ge(turned, i + 1)
                dve.tensor_copy(H[:, d:d + 4, a * P:(a + 1) * P],
                                ps[:, 1 + i % 4, :].rearrange("p (d t) -> p d t", d=4)).then_inc(turned_out, 1)
            for n in range(18):
                dve.wait_ge(ring.used, n + 1)
                if n >= 2:
                    dve.wait_ge(folded, n - 1)
                dve.tensor_copy(rows[:, n % 2, :], ps[:, 5 + n % 2, :]).then_inc(rows_out, 1)
                if n == 0:
                    dve.wait_ge(vec_out, 3)
                if 0 <= n - FILTER_FROM < filters.STEPS:
                    filters.arithmetic(dve, n - FILTER_FROM)
            dve.wait_ge(folded, 18)
            raw = ps[:, 0, 0:2 * N_MOD * DT].rearrange("p (m s) -> p m s", s=2)
            for s in range(2):
                ins = dve.tensor_tensor(modv[:, s, :], raw[:, :, s], VA[:, VA_MODB:VA_MODB + 72], ALU.add)
            step(ins)
            for part in (1, 4, 7):
                v = modv[:, :, part * DT:(part + 1) * DT]
                dve.tensor_scalar(v, v, 1.0, None, ALU.add)
            for part in (2, 8):
                v = modv[:, :, part * DT:(part + 1) * DT]
                ins = dve.tensor_scalar(v, v, 0.5, None, ALU.mult)
            step(ins)

        @block.scalar
        def _(act):
            act.wait_ge(vec_out, 1)
            act.wait_ge(silc_zero, 1)
            act.activation(silc[:, :, 0:2], VA[:, VA_C:VA_C + 2 * DT].rearrange("p (s k) -> p k s", s=2),
                           ACT.Silu).then_inc(c_ready, 1)
            filters.activations(act)

        @block.tensor
        def _(pe):
            pe.wait_ge(ident_in, 32)
            pe.wait_ge(vec_in, 16 * 13)
            pe.transpose(ps[:, 7, 0:VA_ROWS], rowsA[0:VA_ROWS, :], ident[0:VA_ROWS, 0:VA_ROWS])
            pe.transpose(ps[:, 7, 128:128 + VB_ROWS], rowsB[0:VB_ROWS, :], ident[0:VB_ROWS, 0:VB_ROWS])
            pe.transpose(ps[0:64, 7, 256:260], rowsC[:, :], ident[0:4, 0:4]).then_inc(vec_turned, 1)
            pe.wait_ge(x_ready, 1)
            for i in range(2 * TT * DT // 4):
                a, d = i // 2, 4 * (i % 2)
                if i >= 4:
                    pe.wait_ge(turned_out, i - 3)
                for j in range(4):
                    ins = pe.transpose(ps[:, 1 + i % 4, j * P:(j + 1) * P], xin[:, a, (d + j) * P:(d + j + 1) * P],
                                       ident[:])
                ins.then_inc(turned, 1)
            pe.wait_ge(c_ready, 1)

            def fold_rows(n):
                pe.wait_ge(rows_out, n + 1)
                for m in range(4 * n, 4 * n + 4):
                    ins = pe.matmul(ps[:, 0, 2 * m:2 * m + 2], rows[:, n % 2, (m % 4) * P:(m % 4 + 1) * P], fold[:],
                                    start=True, stop=True)
                ins.then_inc(folded, 1)

            for n in range(18):
                ring.arrived(pe, n)
                if n >= 2:
                    pe.wait_ge(rows_out, n - 1)
                w = ring.view(n, DT, CH)
                for k in range(DT):
                    g = k % 4
                    ins = pe.matmul(ps[32 * g:32 * g + 32, 5 + n % 2, :], silc[:, k, :], w[:, k, :],
                                    start=(k < 4), stop=(k >= 4))
                ins.then_inc(ring.used, 1)
                if n:
                    fold_rows(n - 1)
                if 0 <= n - FILTER_FROM < filters.STEPS:
                    filters.products(pe, n - FILTER_FROM)
            fold_rows(17)


def norm_modulate(nc, S, W, part, name, room=None):
    ps, ones, H, modv, NH, NL = S["ps"], S["ones"], S["H"], S["modv"], S["NH"], S["NL"]
    with ExitStack() as ctx:
        rstd = ctx.enter_context(nc.sbuf_tensor(f"{name}_rstd", [P, W], F32))
        N = room if room is not None else ctx.enter_context(nc.sbuf_tensor(f"{name}_n", [P, DT, W], F32))
        squares, summed, mean_ready, root_ready, dve_step, scaled, act_step, high_ready = semaphores(
            ctx, nc, " ".join(f"{name}_{s}" for s in
                              "squares summed mean_ready root_ready dve_step scaled act_step high_ready".split()))
        block = ctx.enter_context(nc.Block())

        @block.scalar
        def _(act):
            for d in range(DT):
                act.activation(N[:, d, 0:W], H[:, d, 0:W], ACT.Square).then_inc(squares, 1)
            act.wait_ge(mean_ready, 1)
            act.activation(rstd[:], rstd[:], ACT.Sqrt).then_inc(root_ready, 1)
            for d in range(DT):
                act.wait_ge(scaled, d + 1)
                for s in range(W // T):
                    v = N[:, d, s * T:(s + 1) * T]
                    ins = act.activation(v, v, ACT.Identity, scale=modv[:, s, (part + 1) * DT + d:(part + 1) * DT + d + 1],
                                         bias=modv[:, s, part * DT + d:part * DT + d + 1])
                ins.then_inc(act_step, 1)
                if d:
                    act.wait_ge(act_step, d)
                    act.activation(NH[:, d - 1, 0:W], N[:, d - 1, 0:W], ACT.Copy).then_inc(high_ready, 1)
            act.wait_ge(act_step, DT)
            act.activation(NH[:, DT - 1, 0:W], N[:, DT - 1, 0:W], ACT.Copy).then_inc(high_ready, 1)

        @block.tensor
        def _(pe):
            for d in range(DT):
                pe.wait_ge(squares, d + 1)
                ins = pe.matmul(ps[:, 0, 0:W], ones[:], N[:, d, 0:W], start=(d == 0), stop=(d == DT - 1))
            ins.then_inc(summed, 1)

        @block.vector
        def _(dve):
            step = Chain(dve, dve_step)
            dve.wait_ge(summed, 1)
            dve.tensor_scalar(rstd[:], ps[:, 0, 0:W], 1.0 / D, RMS_EPS, ALU.mult, ALU.add).then_inc(mean_ready, 1)
            dve.wait_ge(root_ready, 1)
            step(dve.reciprocal(rstd[:], rstd[:]))
            for d in range(DT):
                dve.tensor_tensor(N[:, d, 0:W], H[:, d, 0:W], rstd[:], ALU.mult).then_inc(scaled, 1)
            for d in range(DT):
                dve.wait_ge(high_ready, d + 1)
                dve.tensor_tensor(NL[:, d, 0:W], N[:, d, :], NH[:, d, 0:W].bitcast(F32), ALU.subtract)


def feed_forward(nc, S, ring, chunks, W, part, base, name):
    ps, H, NH, NL, modv = S["ps"], S["H"], S["NH"], S["NL"], S["modv"]
    GROUPS = -(-FT // 4)
    tiles_of = lambda g: range(4 * g, min(4 * g + 4, FT))
    GATED = 2 * GROUPS * DT
    with ExitStack() as ctx:
        hid = ctx.enter_context(nc.sbuf_tensor(f"{name}_hid", [P, FT, W], F32))
        sg = S["X"][:].rearrange("p a (b n) -> p (a b) n", b=2)[:, :, 0:W]
        hid_high = ctx.enter_context(nc.sbuf_tensor(f"{name}_hid_high", [P, 4, W], F32R))
        hid_low = ctx.enter_context(nc.sbuf_tensor(f"{name}_hid_low", [P, 4, W], F32R))
        high_ready, low_ready, tile_used, silu_ready, hid_ready, hid_high_ready, hid_low_ready = semaphores(
            ctx, nc, " ".join(f"{name}_{s}" for s in """high_ready low_ready tile_used silu_ready hid_ready
            hid_high_ready hid_low_ready""".split()))
        block = ctx.enter_context(nc.Block())
        shapes = [(DT, P * len(tiles_of(g))) for g in range(GROUPS) for _ in range(2)] + [(8, CH), (8, CH), (6, CH)] * 2
        W_ = SplitTiles(ring, base, shapes, S["w_high"], S["w_low"], high_ready, low_ready, tile_used)

        @block.sync
        def _(sp):
            refill(sp, ring, chunks, base, FFN_CHUNKS)

        @block.tensor
        def _(pe):
            for g in range(GROUPS):
                for u in range(2):
                    if g:
                        pe.wait_ge((silu_ready, hid_ready)[u], 4 * g)
                    for k in range(DT):
                        outs = [(ps[:, 4 * u + j, 0:W], NH[:, k, 0:W], NL[:, k, 0:W]) for j in range(len(tiles_of(g)))]
                        W_.products(pe, (2 * g + u) * DT + k, outs, k == 0, k == DT - 1)
            for half in range(2):
                pe.wait_ge((silu_ready, hid_ready)[half], FT)
                for k in range(FT):
                    r = half * FT + k
                    pe.wait_ge(hid_low_ready, r + 1)
                    outs = [(ps[:, 4 * half + d, 0:W], hid_high[:, r % 4, :], hid_low[:, r % 4, :]) for d in range(4)]
                    W_.products(pe, GATED + r, outs, k == 0, k == FT - 1)

        @block.scalar
        def _(act):
            for q in range(len(W_)):
                W_.upper(act, q)
                g, at = divmod(q, 2 * DT)
                if q < GATED and at == DT + 4:
                    act.wait_ge(tile_used, (2 * g + 1) * DT)
                    if g:
                        act.wait_ge(hid_ready, 4 * g)
                    for i in tiles_of(g):
                        act.activation(sg[:, i % 4, :], ps[:, i % 4, 0:W], ACT.Silu).then_inc(silu_ready, 1)
                if q >= GATED:
                    r = q - GATED
                    act.wait_ge(hid_ready, r % FT + 1)
                    act.activation(hid_high[:, r % 4, :], hid[:, r % FT, :], ACT.Copy).then_inc(hid_high_ready, 1)

        @block.vector
        def _(dve):
            def add_output(half):
                dve.wait_ge(tile_used, GATED + (half + 1) * FT)
                for d in range(4):
                    m = 4 * half + d
                    for s in range(W // T):
                        v = H[:, m, s * T:(s + 1) * T]
                        dve.scalar_tensor_tensor(v, ps[:, m, s * T:(s + 1) * T],
                                                 modv[:, s, part * DT + m:part * DT + m + 1], v, ALU.mult, ALU.add)

            for q in range(len(W_)):
                W_.lower(dve, q)
                if q >= GATED:
                    r = q - GATED
                    dve.wait_ge(hid_high_ready, r + 1)
                    dve.tensor_tensor(hid_low[:, r % 4, :], hid[:, r % FT, :], hid_high[:, r % 4, :].bitcast(F32),
                                      ALU.subtract).then_inc(hid_low_ready, 1)
                g, at = divmod(q - 2 * DT, 2 * DT)
                if 0 <= g < GROUPS and at == 4:
                    dve.wait_ge(tile_used, (2 * g + 2) * DT)
                    for i in tiles_of(g):
                        dve.wait_ge(silu_ready, i + 1)
                        dve.tensor_tensor(hid[:, i, :], sg[:, i % 4, :], ps[:, 4 + i % 4, 0:W],
                                          ALU.mult).then_inc(hid_ready, 1)
                if q == GATED + FT + 4:
                    add_output(0)
            add_output(1)


WIN_KINDS = [("v", 0), ("f0", 0), ("f1", 0), ("merge", 0), ("merge", 4), ("merge", 8), ("merge", 12), ("q", 0), ("g", 0),
             ("hy", 0), ("hy", 4), ("hy", 8)]
DVE_KINDS = ("v", "hy")


def input_projection(nc, S, ring, chunks):
    ps, NH, NL = S["ps"], S["NH"], S["NL"]
    V, SG, MG, Q, G, HY = S["V"], S["SG"], S["MG"], S["Q"], S["G"], S["HY"]
    with ExitStack() as ctx:
        high_ready, low_ready, tile_used, act_out, dve_out = semaphores(
            ctx, nc, "win_high_ready win_low_ready win_tile_used win_act_out win_dve_out")
        block = ctx.enter_context(nc.Block())
        W_ = SplitTiles(ring, C_WIN, [(DT, CH)] * len(WIN_KINDS), S["w_high"], S["w_low"], high_ready, low_ready, tile_used)
        by_dve = [kind in DVE_KINDS for kind, _ in WIN_KINDS]
        bank = lambda c, j: 4 * (c % 2) + j

        @block.sync
        def _(sp):
            refill(sp, ring, chunks, C_WIN, 12)

        @block.tensor
        def _(pe):
            for c, (kind, _) in enumerate(WIN_KINDS):
                if c >= 2:
                    pe.wait_ge(dve_out if by_dve[c - 2] else act_out, by_dve[:c - 1].count(by_dve[c - 2]))
                W = 2 * T if kind in ("f0", "f1") else T
                for k in range(DT):
                    if kind == "v":
                        outs = [(ps[:, bank(c, j), :], NH[:, k, j * P:(j + 1) * P], NL[:, k, j * P:(j + 1) * P])
                                for j in range(2 * TT)]
                    else:
                        outs = [(ps[:, bank(c, j), 0:W], NH[:, k, 0:W], NL[:, k, 0:W]) for j in range(4)]
                    W_.products(pe, c * DT + k, outs, k == 0, k == DT - 1, tokens_out=(kind == "v"))

        @block.scalar
        def _(act):
            def take(c):
                kind, first = WIN_KINDS[c]
                act.wait_ge(tile_used, (c + 1) * DT)
                for j in range(4):
                    src = ps[:, bank(c, j), :]
                    if kind in ("f0", "f1"):
                        ins = act.activation(SG[:, int(kind[1]), j, :], src, ACT.Sigmoid)
                    elif kind == "merge":
                        ins = act.activation(MG[:, first + j, :], src[:, 0:T], ACT.Sigmoid)
                    else:
                        ins = act.activation((Q if kind == "q" else G)[:, j, :], src[:, 0:T], ACT.Silu)
                ins.then_inc(act_out, 1)

            for q in range(len(W_)):
                W_.upper(act, q)
                c, at = divmod(q, DT)
                if at == 4 and c and not by_dve[c - 1]:
                    take(c - 1)

        @block.vector
        def _(dve):
            def take(c):
                kind, first = WIN_KINDS[c]
                dve.wait_ge(tile_used, (c + 1) * DT)
                for j in range(4):
                    if kind == "v":
                        ins = dve.tensor_copy(V[:, j, :], ps[:, bank(c, j), :])
                    else:
                        ins = dve.tensor_copy(HY[:, first + j, 1:T + 1], ps[:, bank(c, j), 0:T])
                ins.then_inc(dve_out, 1)

            dve.memset(HY[:, :, 0:1], 0.0)
            dve.memset(HY[:, :, T + 1:T + 2], 0.0)
            for q in range(len(W_)):
                W_.lower(dve, q)
                c, at = divmod(q, DT)
                if at == 4 and c and by_dve[c - 1]:
                    take(c - 1)
            take(len(WIN_KINDS) - 1)


def block_differences(eng, out, cum, size, backward):
    half = size // 2
    v = cum.rearrange("p (n s) -> p n s", s=size)
    o = out.rearrange("p (n s) -> p n s", s=size)
    m = half if backward else half - 1
    ref = v[:, :, m:m + 1].to_broadcast([P, v.shape[1], half])
    late, early = (slice(0, half), slice(half, size)) if backward else (slice(half, size), slice(0, half))
    eng.tensor_tensor(o[:, :, late], v[:, :, late], ref, ALU.subtract)
    return eng.tensor_tensor(o[:, :, early], ref, v[:, :, early], ALU.subtract)


def hgrn2(nc, S):
    ps, ident, ones, VA, VB = S["ps"], S["ident"], S["ones"], S["VA"], S["VB"]
    V, SG, Q, G = S["V"], S["SG"], S["Q"], S["G"]
    NL = LEVELS + 1
    with ExitStack() as ctx:
        sb = lambda n, s: ctx.enter_context(nc.sbuf_tensor(f"hg_{n}", s, F32))
        lbv = sb("lb", [P, 8])
        lb1 = sb("lb1", [P, 8])
        cum = S["N"][:].rearrange("p (r h) t -> p r h t", r=2)         
        keep = sb("keep", [P, T])
        EB = sb("EB", [P, 2, NL, T])
        prod = sb("prod", [P, 2, NL * P])
        cross = sb("cross", [P, 2, P])
        spare = S["X"][:].rearrange("p a d -> p (a d)")
        kd, kdt, qc = (spare[:, 512 * i:512 * (i + 1)].rearrange("p (a t) -> p a t", a=2) for i in range(3))
        sq, rs = spare[:, 1536:1792], spare[:, 1792:2048]
        s0 = sb("s0", [P, 2, P])
        on = sb("on", [P, T])
        masks = S["masks"]
        (lb_diff, lb_ready, masks_in, f_ready, log_ready, cum_ready, diff_ready, e_ready, ctx_decay, eb_ready, kd_ready,
         q_decay, kd_turned, kdt_ready, s0_made, s0_out, scores, prod_ready, cross_done, o_done, sq_ready,
         summed, mean_ready, root_ready, head_done, act_step, dve_step, pool_step) = semaphores(
            ctx, nc, " ".join(f"hg_{s}" for s in """lb_diff lb_ready masks_in f_ready log_ready cum_ready diff_ready
            e_ready ctx_decay eb_ready kd_ready q_decay kd_turned kdt_ready s0_made s0_out scores prod_ready
            cross_done o_done sq_ready summed mean_ready root_ready head_done act_step dve_step pool_step""".split()))
        block = ctx.enter_context(nc.Block())
        HD = [(h, r) for h in range(HEADS_A) for r in range(2)]

        @block.sync
        def _(sp):
            sp.dma_start(masks[:], S["t"]["c_masks"].rearrange("p (r l c) -> p r l c", r=2, l=NL)).then_inc(masks_in, 16)

        @block.vector
        def _(dve):
            step = Chain(dve, dve_step)
            dve.memset(keep[:], 1.0)
            dve.tensor_tensor(lbv[:], VB[:, VB_LB:VB_LB + 8], VB[:, VB_LB + 8:VB_LB + 16],
                              ALU.subtract).then_inc(lb_diff, 1)
            dve.wait_ge(lb_ready, 1)
            step(dve.tensor_scalar(lb1[:], lbv[:], -1.0, 1.0, ALU.mult, ALU.add))
            for h, r in HD:
                c = 4 * r + h
                ins = dve.tensor_scalar(SG[:, r, h, :], SG[:, r, h, :], lb1[:, c:c + 1], lbv[:, c:c + 1], ALU.mult, ALU.add)
            step(ins)
            for r in range(2):
                ins = dve.tensor_scalar(cum[:, r], SG[:, r], LOG_FLOOR, None, ALU.max)
                ins.then_inc(f_ready, 1)
            for r in range(2):
                dve.tensor_scalar(SG[:, r], SG[:, r], -1.0, 1.0, ALU.mult, ALU.add)
            for r in range(2):
                dve.wait_ge(log_ready, r + 1)
                for h in range(HEADS_A):
                    v = cum[:, r, h, :]
                    for s in range(2):
                        w = v[:, s * T:(s + 1) * T]
                        w = w[:, ::-1] if r else w
                        ins = dve.tensor_tensor_scan(w, keep[:], w, 0.0, ALU.mult, ALU.add)
            ins.then_inc(cum_ready, 1)

            def merge_kq(x):
                h, r = HD[x]
                dve.wait_ge(e_ready, x + 1)
                for l in range(NL):
                    s = 1 << l
                    e = EB[:, x % 2, l, :].rearrange("p (n two s) -> p n two s", two=2, s=s)
                    kv = SG[:, r, h, 0:T].rearrange("p (n two s) -> p n two s", two=2, s=s)
                    qv = Q[:, h, :].rearrange("p (n two s) -> p n two s", two=2, s=s)
                    dve.tensor_tensor(e[:, :, r, :], e[:, :, r, :], kv[:, :, r, :], ALU.mult)
                    ins = dve.tensor_tensor(e[:, :, 1 - r, :], e[:, :, 1 - r, :], qv[:, :, 1 - r, :], ALU.mult)
                ins.then_inc(eb_ready, 1)
                dve.wait_ge(ctx_decay, x + 1)
                dve.tensor_tensor(kd[:, x % 2, :], kd[:, x % 2, :], SG[:, r, h, T:2 * T], ALU.mult).then_inc(kd_ready, 1)
                dve.tensor_tensor(qc[:, x % 2, :], qc[:, x % 2, :], Q[:, h, :], ALU.mult).then_inc(q_decay, 1)

            def context_state(x):
                dve.wait_ge(kd_turned, x + 1)
                if x >= 2:
                    dve.wait_ge(s0_made, x - 1)
                dve.tensor_copy(kdt[:, x % 2, :], ps[:, 4, 0:T]).then_inc(kdt_ready, 1)
                dve.wait_ge(s0_made, x + 1)
                if x >= 2:
                    dve.wait_ge(cross_done, 3 * (x - 2) + 1)
                dve.tensor_copy(s0[:, x % 2, :], ps[:, 4, T:T + P]).then_inc(s0_out, 1)

            def mask(x):
                h, r = HD[x]
                for tt in range(TT):
                    y = 2 * x + tt
                    dve.wait_ge(scores, 3 * x + tt + 1)
                    if y >= 2:
                        dve.wait_ge(prod_ready, y - 1)
                        dve.wait_ge(cross_done, 3 * ((y - 2) // 2) + (y - 2) % 2 + 1)
                    dve.tensor_tensor(prod[:, y % 2, :], ps[:, 2 * (y % 2):2 * (y % 2) + 2, :].rearrange("p a b -> p (a b)"),
                                      masks[:, r].rearrange("p l c -> p (l c)"), ALU.mult).then_inc(prod_ready, 1)
                dve.wait_ge(scores, 3 * x + 3)
                if x >= 2:
                    dve.wait_ge(cross_done, 3 * (x - 1))
                dve.tensor_copy(cross[:, x % 2, :], ps[:, 4, T + P:T + 2 * P]).then_inc(s0_out, 1)

            def normalise(h):
                dve.wait_ge(summed, h + 1)
                dve.tensor_scalar(rs, ps[:, 7, 0:T], 1.0 / P, RMS_EPS, ALU.mult, ALU.add).then_inc(mean_ready, 1)
                dve.wait_ge(root_ready, h + 1)
                step(dve.reciprocal(rs, rs))
                step(dve.tensor_tensor(on[:], ps[:, 5 + h % 2, 0:T], rs, ALU.mult))
                dve.scalar_tensor_tensor(G[:, h, :], on[:], VA[:, VA_HNORM:VA_HNORM + 1], G[:, h, :],
                                         ALU.mult, ALU.mult).then_inc(head_done, 1)

            for x in range(8):
                merge_kq(x)
                context_state(x)
                mask(x)
                if x % 2 == 1 and x >= 3:
                    normalise(x // 2 - 1)
            normalise(3)

        @block.gpsimd
        def _(pool):
            pool.wait_ge(cum_ready, 1)
            for x, (h, r) in enumerate(HD):
                if x >= 2:
                    pool.wait_ge(scores, 3 * (x - 1))
                for l in range(NL):
                    ins = block_differences(pool, EB[:, x % 2, l, :], cum[:, r, h, 0:T], 2 << l, r)
                ins.then_inc(diff_ready, 1)

        @block.scalar
        def _(act):
            def norm_act(h):
                act.wait_ge(cross_done, 3 * (2 * h + 2))
                act.activation(sq, ps[:, 5 + h % 2, 0:T], ACT.Square).then_inc(sq_ready, 1)
                act.wait_ge(mean_ready, h + 1)
                act.activation(rs, rs, ACT.Sqrt).then_inc(root_ready, 1)

            act.wait_ge(lb_diff, 1)
            act.activation(lbv[:], lbv[:], ACT.Sigmoid).then_inc(lb_ready, 1)
            for r in range(2):
                act.wait_ge(f_ready, r + 1)
                act.activation(cum[:, r], cum[:, r], ACT.Ln).then_inc(log_ready, 1)
            act.wait_ge(cum_ready, 1)
            for x, (h, r) in enumerate(HD):
                act.wait_ge(diff_ready, x + 1)
                act.activation(EB[:, x % 2], EB[:, x % 2], ACT.Exp).then_inc(e_ready, 1)
                if x >= 2:
                    act.wait_ge(kd_turned, x - 1)
                    act.wait_ge(cross_done, 3 * (x - 1))
                end = T if r else 2 * T - 1
                act.activation(kd[:, x % 2, :], cum[:, r, h, T:2 * T], ACT.Exp, scale=-1.0, bias=cum[:, r, h, end:end + 1])
                act.activation(qc[:, x % 2, :], cum[:, r, h, 0:T], ACT.Exp).then_inc(ctx_decay, 1)
                if x % 2 == 1 and x >= 3:
                    norm_act(x // 2 - 1)
            norm_act(3)

        @block.tensor
        def _(pe):
            def state_part(x):
                h, r = HD[x]
                pe.wait_ge(kd_ready, x + 1)
                if x >= 1:
                    pe.wait_ge(s0_out, 2 * x)
                for s in range(TT):
                    ins = pe.transpose(ps[:, 4, s * P:(s + 1) * P], kd[:, x % 2, s * P:(s + 1) * P], ident[:])
                ins.then_inc(kd_turned, 1)
                pe.wait_ge(kdt_ready, x + 1)
                for s in range(TT):
                    ins = pe.matmul(ps[:, 4, T:T + P], kdt[:, x % 2, s * P:(s + 1) * P],
                                    V[:, TT + s, h * P:(h + 1) * P], start=(s == 0), stop=(s == TT - 1))
                ins.then_inc(s0_made, 1)

            def score_part(x):
                h, r = HD[x]
                pe.wait_ge(eb_ready, x + 1)
                for tt in range(TT):
                    y = 2 * x + tt
                    if y >= 2:
                        pe.wait_ge(prod_ready, y - 1)
                    c = slice(tt * P, (tt + 1) * P)
                    for l in range(NL):
                        a, b = (SG[:, r, h, c], Q[:, h, c]) if l == 0 else (EB[:, x % 2, l - 1, c],) * 2
                        ins = pe.matmul(ps[:, 2 * (y % 2) + l // 4, (l % 4) * P:(l % 4 + 1) * P], a, b,
                                        start=True, stop=True)
                    ins.then_inc(scores, 1)
                early, late = (slice(P, T), slice(0, P)) if r else (slice(0, P), slice(P, T))
                pe.wait_ge(s0_out, 2 * x + 1)
                pe.matmul(ps[:, 4, T + P:T + 2 * P], EB[:, x % 2, NL - 1, early], EB[:, x % 2, NL - 1, late],
                          start=True, stop=True).then_inc(scores, 1)

            def out_part(x):
                h, r = HD[x]
                bank = 5 + h % 2
                if r == 0 and h >= 2:
                    pe.wait_ge(head_done, h - 1)
                pe.wait_ge(q_decay, x + 1)
                pe.matmul(ps[:, bank, 0:T], s0[:, x % 2, :], qc[:, x % 2, :], start=(r == 0), stop=False,
                          skip_group_check=True)
                for tt in range(TT):
                    y = 2 * x + tt
                    pe.wait_ge(prod_ready, y + 1)
                    for l in range(NL):
                        ins = pe.matmul(ps[:, bank, tt * P:(tt + 1) * P], V[:, tt, h * P:(h + 1) * P],
                                        prod[:, y % 2, l * P:(l + 1) * P], start=False, stop=False, skip_group_check=True)
                    ins.then_inc(cross_done, 1)
                early, late = (1, 0) if r else (0, 1)
                pe.wait_ge(s0_out, 2 * x + 2)
                pe.matmul(ps[:, bank, late * P:(late + 1) * P], V[:, early, h * P:(h + 1) * P], cross[:, x % 2, :],
                          start=False, stop=(r == 1), skip_group_check=True).then_inc(cross_done, 1)

            def norm_part(h):
                pe.wait_ge(sq_ready, h + 1)
                if h >= 1:
                    pe.wait_ge(mean_ready, h)
                pe.matmul(ps[:, 7, 0:T], ones[:], sq, start=True, stop=True).then_inc(summed, 1)

            pe.wait_ge(masks_in, 16)
            for x in range(8):
                state_part(x)
                score_part(x)
                out_part(x)
                if x % 2 == 1 and x >= 3:
                    norm_part(x // 2 - 1)
            norm_part(3)


TWO_PI_PARTS = (6.28125, 0.0019353071693331003, 2 * math.pi - 6.28125 - 0.0019353071693331003)
ROUND = 1.5 * 2.0 ** 23
PI_INSIDE = 3.1415925


class HyenaFilters:

    SEMAPHORES = "consts lin arg_ready sin_ready taps_lin taps_ready mag_ready mag_read scaled spectrum spectrum_out stored"
    STEPS = 14

    def __init__(self, ctx, nc, S, sems, dve_step):
        sb = lambda n, s: ctx.enter_context(nc.sbuf_tensor(f"hf_{n}", s, F32))
        self.S, self.dve_step = S, dve_step
        (self.consts, self.lin, self.arg_ready, self.sin_ready, self.taps_lin, self.taps_ready, self.mag_ready,
         self.mag_read, self.scaled, self.spectrum, self.spectrum_out, self.stored) = sems
        self.KS = sb("KS", [P, 2, 4, BW])
        self.CF, self.CG, self.window = (sb(n, [P, TT, CH]) for n in ("CF", "CG", "window"))
        self.feat = sb("feat", [33, T])
        self.w1, self.w2, self.w3 = sb("w1", [33, 64]), sb("w2", [64, 64]), sb("w3", [64, 4 * BW])
        self.arg, self.rnd, self.hid = sb("arg", [64, T]), sb("rnd", [64, T]), sb("hid", [64, T])
        self.hk = S["X"][:].rearrange("p a (b n) -> p (a b) n", b=2)
        self.mag, self.rn = sb("mag", [P, 2, BW]), sb("rn", [P, BW])

    def load(self, sp):
        t = self.S["t"]
        tiled = lambda a: a.rearrange("(a p) n -> p a n", p=P)
        for dst, src in ((self.feat, t["c_feat"]), (self.w1, t["hyena_w1"][0]), (self.w2, t["hyena_w2"][0]),
                         (self.w3, t["hyena_w3"][0]), (self.window, tiled(t["c_window"])), (self.CF, tiled(t["c_cf"])),
                         (self.CG, tiled(t["c_cg"]))):
            sp.dma_start(dst[:], src).then_inc(self.consts, 16)

    def products(self, pe, i):
        ps, hid = self.S["ps"], self.hid
        if i < 2:
            if i == 0:
                pe.wait_ge(self.consts, 16 * 7)
            else:
                pe.wait_ge(self.sin_ready, 1)
            w, x = ((self.w1, self.feat), (self.w2, hid))[i]
            pe.matmul(ps[0:64, 7, 0:T], w[:], x[:], start=True, stop=True).then_inc(self.lin, 1)
            return
        o, k = divmod(i - 2, 6)
        if k == 0:
            pe.wait_ge(self.sin_ready, 2)
            if o:
                pe.wait_ge(self.spectrum_out, 4)
            for j in range(4):
                r, tt = j // 2, j % 2
                pe.matmul(ps[:, 1 + j, :], hid[:, tt * P:(tt + 1) * P], self.w3[:, (2 * o + r) * BW:(2 * o + r + 1) * BW],
                          start=True, stop=True).then_inc(self.taps_lin, 1)
        elif k == 1:
            if o:
                pe.wait_ge(self.scaled, 1)
            for j in range(4):
                pe.wait_ge(self.mag_ready, 4 * o + j + 1)
                pe.matmul(ps[:, 7, :], self.S["ones"][:], self.mag[:, j % 2, :], start=(j == 0),
                          stop=(j == 3)).then_inc(self.mag_read, 1)
        else:
            m = k - 2
            pe.wait_ge(self.scaled, o + 1)
            for j in range(4):
                basis = (self.CF, self.CG)[j // 2]
                ins = pe.matmul(ps[:, 1 + m, :], basis[:, j % 2, m * P:(m + 1) * P], self.hk[:, j, :],
                                start=(j == 0), stop=(j == 3))
            ins.then_inc(self.spectrum, 1)

    def arithmetic(self, dve, i):
        ps, VC, hk, arg, rnd, rn = self.S["ps"], self.S["VC"], self.hk, self.arg, self.rnd, self.rn
        if i < 2:
            dve.wait_ge(self.lin, i + 1)
            b, fr = VC[:, 2 * i:2 * i + 1], VC[:, 2 * i + 1:2 * i + 2]
            self.dve_step(dve.tensor_scalar(arg[:], ps[0:64, 7, 0:T], b, fr, ALU.add, ALU.mult))
            self.dve_step(dve.tensor_scalar(rnd[:], arg[:], 1.0 / (2 * math.pi), ROUND, ALU.mult, ALU.add))
            self.dve_step(dve.tensor_scalar(rnd[:], rnd[:], ROUND, None, ALU.subtract))
            for part in TWO_PI_PARTS:
                self.dve_step(dve.scalar_tensor_tensor(arg[:], rnd[:], -part, arg[:], ALU.mult, ALU.add))
            dve.tensor_scalar(arg[:], arg[:], PI_INSIDE, -PI_INSIDE, ALU.min, ALU.max).then_inc(self.arg_ready, 1)
            return
        o, k = divmod(i - 2, 6)
        if k == 0:
            for j in range(4):
                dve.wait_ge(self.taps_lin, 4 * o + j + 1)
                if o:
                    dve.wait_ge(self.spectrum, 4)
                dve.tensor_tensor(hk[:, j, :], ps[:, 1 + j, :], self.window[:, j % 2, :], ALU.mult).then_inc(self.taps_ready, 1)
        elif k == 1:
            dve.wait_ge(self.mag_read, 4 * o + 4)
            self.dve_step(dve.tensor_scalar(rn[:], ps[:, 7, :], HYENA_L1_EPS, None, ALU.add))
            self.dve_step(dve.reciprocal(rn[:], rn[:]))
            dve.wait_ge(self.taps_ready, 4 * o + 4)
            dve.tensor_tensor(hk, hk, rn[:].unsqueeze(1).to_broadcast([P, 4, BW]), ALU.mult).then_inc(self.scaled, 1)

    def activations(self, act):
        ps, KS, hk = self.S["ps"], self.KS, self.hk
        for layer in range(2):
            act.wait_ge(self.arg_ready, layer + 1)
            act.activation(self.hid[:], self.arg[:], ACT.Sin).then_inc(self.sin_ready, 1)
        for o in range(2):
            for j in range(4):
                act.wait_ge(self.taps_ready, 4 * o + j + 1)
                if 4 * o + j >= 2:
                    act.wait_ge(self.mag_read, 4 * o + j - 1)
                act.activation(self.mag[:, j % 2, :], hk[:, j, :], ACT.Abs).then_inc(self.mag_ready, 1)
            for m in range(4):
                act.wait_ge(self.spectrum, 4 * o + m + 1)
                act.activation(KS[:, o, m, :], ps[:, 1 + m, :], ACT.Copy).then_inc(self.spectrum_out, 1)
            act.wait_ge(self.spectrum_out, 4 * (o + 1))
            act.dma_start(self.S["spectra"][:, o], KS[:, o]).then_inc(self.stored, 16)


def hyena_mix(nc, S):
    ps, ident, VA, VB, HY = S["ps"], S["ident"], S["VA"], S["VB"], S["HY"]
    KS, OB, t = S["SG"][:], S["Q"], S["t"]
    with ExitStack() as ctx:
        sb = lambda n, s: ctx.enter_context(nc.sbuf_tensor(f"hm_{n}", s, F32))
        u3 = S["N"][:].rearrange("p d t -> p (d t)")[:, 0:12 * T].rearrange("p (c t) -> p c t", c=12)
        zt = sb("zt", [P, TT, BW])
        Y = S["X"][:].rearrange("p a (b n) -> p (a b) n", b=2)
        ta, tb = sb("ta", [P, 2, BW]), sb("tb", [P, 2, BW])
        CF, CI = sb("CF", [P, TT, 2 * T]), sb("CI", [P, 4, T])
        bases_in, spectra_in, z_ready, turned, zt_ready, spectrum, y_ready, conv_done, dve_step = semaphores(
            ctx, nc, " ".join(f"hm_{s}" for s in "bases_in spectra_in z_ready turned zt_ready spectrum y_ready conv_done dve_step".split()))
        block = ctx.enter_context(nc.Block())

        @block.sync
        def _(sp):
            sp.dma_start(CF[:], t["c_cf"].rearrange("(a p) n -> p a n", p=P)).then_inc(bases_in, 16)
            for o in range(2):
                sp.dma_start(KS[:, o], S["spectra"][:, o]).then_inc(spectra_in, 16)
            sp.dma_start(CI[:], t["c_ci"].rearrange("(a p) n -> p a n", p=P)).then_inc(bases_in, 16)

        @block.vector
        def _(dve):
            step = Chain(dve, dve_step)
            conv_w = lambda j, c: VB[:, VB_CONVW + 12 * j + c:VB_CONVW + 12 * j + c + 1]
            for c in range(12):
                ins = dve.tensor_scalar(u3[:, c, :], HY[:, c, 0:T], conv_w(0, c),
                                        VA[:, VA_CONVB + c:VA_CONVB + c + 1], ALU.mult, ALU.add)
            step(ins)
            for j in (1, 2):
                for c in range(12):
                    ins = dve.scalar_tensor_tensor(u3[:, c, :], HY[:, c, j:j + T], conv_w(j, c), u3[:, c, :],
                                                   ALU.mult, ALU.add)
                if j == 1:
                    step(ins)
            ins.then_inc(z_ready, 1)
            for o in range(2):
                z = u3[:, 0:4, :]
                for tt in range(TT):
                    dve.wait_ge(turned, TT * o + tt + 1)
                    dve.tensor_copy(zt[:, tt, :], ps[:, tt, :]).then_inc(zt_ready, 1)
                if o == 0:
                    dve.wait_ge(spectra_in, 32)
                dve.wait_ge(spectrum, o + 1)
                ur, ui = ps[:, 2:4, :], ps[:, 4:6, :]
                kr, ki = KS[:, o, 0:2, :], KS[:, o, 2:4, :]
                dve.tensor_tensor(ta[:], ur, kr, ALU.mult)
                step(dve.tensor_tensor(tb[:], ui, ki, ALU.mult))
                step(dve.tensor_tensor(Y[:, 0:2, :], ta[:], tb[:], ALU.subtract))
                dve.tensor_tensor(ta[:], ur, ki, ALU.mult)
                step(dve.tensor_tensor(tb[:], ui, kr, ALU.mult))
                dve.tensor_tensor(Y[:, 2:4, :], ta[:], tb[:], ALU.add).then_inc(y_ready, 1)
                dve.wait_ge(conv_done, o + 1)
                if o:
                    dve.wait_ge(z_ready, 2)
                for c in range(4):
                    b = VA[:, VA_HYB + 4 * o + c:VA_HYB + 4 * o + c + 1]
                    ins = dve.scalar_tensor_tensor(ta[:, c // 2, (c % 2) * T:(c % 2 + 1) * T], z[:, c, :], b,
                                                   ps[:, 6 + c // 2, (c % 2) * T:(c % 2 + 1) * T], ALU.mult, ALU.add)
                step(ins)
                dst = OB[:] if o else z
                dve.tensor_tensor(dst, ta[:].rearrange("p a (b t) -> p (a b) t", b=2), u3[:, 4 + 4 * o:8 + 4 * o, :],
                                  ALU.mult).then_inc(z_ready, 1)

        @block.tensor
        def _(pe):
            for o in range(2):
                if o == 0:
                    pe.wait_ge(bases_in, 32)
                pe.wait_ge(z_ready, o + 1)
                for tt in range(TT):
                    for c in range(4):
                        ins = pe.transpose(ps[:, tt, c * P:(c + 1) * P], u3[:, c, tt * P:(tt + 1) * P], ident[:])
                    ins.then_inc(turned, 1)
                pe.wait_ge(zt_ready, TT * (o + 1))
                for m in range(4):
                    for tt in range(TT):
                        ins = pe.matmul(ps[:, 2 + m, :], CF[:, tt, m * P:(m + 1) * P], zt[:, tt, :],
                                        start=(tt == 0), stop=(tt == TT - 1))
                ins.then_inc(spectrum, 1)
                pe.wait_ge(y_ready, o + 1)
                for c in range(4):
                    for m in range(4):
                        ins = pe.matmul(ps[:, 6 + c // 2, (c % 2) * T:(c % 2 + 1) * T], Y[:, m, c * P:(c + 1) * P],
                                        CI[:, m, :], start=(m == 0), stop=(m == 3))
                ins.then_inc(conv_done, 1)


def merge_heads(nc, S, ring, chunks):
    ps, H, MG, modv = S["ps"], S["H"], S["MG"], S["modv"]
    OA, OB, Y = S["G"], S["Q"], S["N"]
    with ExitStack() as ctx:
        ta = ctx.enter_context(nc.sbuf_tensor("mh_ta", [P, 2, 2, T], F32))
        pair_ready, ta_done, y_ready, out_ready, h_done, dve_step = semaphores(
            ctx, nc, " ".join(f"mh_{s}" for s in "pair_ready ta_done y_ready out_ready h_done dve_step".split()))
        block = ctx.enter_context(nc.Block())

        @block.sync
        def _(sp):
            refill(sp, ring, chunks, C_PROJ, 4)

        @block.tensor
        def _(pe):
            for i in range(2):
                ring.arrived(pe, C_PROJ + i)
            for d in range(DT):
                if d >= 4:
                    pe.wait_ge(ta_done, d - 3)
                for i, src in enumerate((OA, OB)):
                    w = ring.view(C_PROJ + i, 4, D)
                    for k in range(4):
                        ins = pe.matmul(ps[:, 2 * (d % 4) + i, 0:T], w[:, k, d * P:(d + 1) * P], src[:, k, :],
                                        start=(k == 0), stop=(k == 3))
                    if d == DT - 1:
                        ins.then_inc(ring.used, 1)
                    elif i == 1:
                        ins.then_inc(pair_ready, 1)
            pe.wait_ge(y_ready, DT)
            for d in range(DT):
                w = ring.view(C_WOUT + d // 4, DT, CH)
                if d % 4 == 0:
                    ring.arrived(pe, C_WOUT + d // 4)
                for k in range(DT):
                    ins = pe.matmul(ps[:, d, 0:T], w[:, k, (d % 4) * P:(d % 4 + 1) * P], Y[:, k, 0:T],
                                    start=(k == 0), stop=(k == DT - 1))
                ins.then_inc(ring.used if d % 4 == 3 else out_ready, 1)

        @block.vector
        def _(dve):
            step = Chain(dve, dve_step)
            for d in range(DT):
                if d == DT - 1:
                    dve.wait_ge(ring.used, C_PROJ + 2)
                else:
                    dve.wait_ge(pair_ready, d + 1)
                dve.tensor_tensor(ta[:, d % 2, 0, :], MG[:, d, :], ps[:, 2 * (d % 4), 0:T], ALU.mult)
                dve.tensor_tensor(ta[:, d % 2, 1, :], MG[:, DT + d, :], ps[:, 2 * (d % 4) + 1, 0:T],
                                  ALU.mult).then_inc(ta_done, 1)
                dve.wait_ge(ta_done, d + 1)
                dve.tensor_tensor(Y[:, d, 0:T], ta[:, d % 2, 0, :], ta[:, d % 2, 1, :], ALU.add).then_inc(y_ready, 1)
            for d in range(DT):
                if d % 4 == 3:
                    dve.wait_ge(ring.used, C_WOUT + d // 4 + 1)
                else:
                    dve.wait_ge(out_ready, d - d // 4 + 1)
                v = H[:, d, 0:T]
                dve.scalar_tensor_tensor(v, ps[:, d, 0:T], modv[:, 0, 5 * DT + d:5 * DT + d + 1], v, ALU.mult, ALU.add)


ALPHA = (2 * 2) ** 0.25
E_FF = 512
N_EXP = 32
RB_SSDN, RB_LNG, RB_LNB, RB_GLAN, RB_DTB, RB_ALOG, RB_DSKIP, RB_END = 0, 512, 768, 1024, 1280, 1288, 1296, 1304
VL_CONVW, VL_CONVB, VL_MU, VL_W0, VL_A0, VL_KK, VL_KA, VL_RK, VL_GBA, VL_ROWS = 0, 24, 30, 37, 39, 41, 43, 45, 47, 48
WIN2_BOUNDS = [(0, 512), (512, 1024), (1024, 1288), (2184, 2696), (2696, 2968), (1288, 1800), (1800, 2184)]
WIN2_OUTPUTS = [
    [("z", 0, 512, 0), ("z", 0, 512, 1)],
    [("xbc", P * j, P, j) for j in range(4)],
    [("xbc", 0, P, 4), ("xbc", P, P, 5), ("dt", 256, 8, 0), ("dt", 256, 8, 1)],
    [("gq", 0, P, 0), ("gk", P, P, 0), ("gv", 256, 256, 0), ("gv", 256, 256, 1)],
    [("gg", 0, 256, 0), ("gg", 0, 256, 1), ("ga", 256, 16, 0)],
    [("rw", P * j, P, j) for j in range(4)],
    [("rw", P * j, P, 4 + j) for j in range(3)],
]
C2_WIN, C2_WOUT, C2_END = 0, len(WIN2_BOUNDS), len(WIN2_BOUNDS) + 2
TOKEN_MAJOR = ("z", "dt", "gv", "gg")
BY_ACT = ("z", "gg")


def to_tokens(nc, t, S):
    ps, ident, ones, H, VA, X = S["ps"], S["ident"], S["ones"], S["H"], S["VA"], S["X"]
    with ExitStack() as ctx:
        rstd = ctx.enter_context(nc.sbuf_tensor("tk_rstd", [P, T], F32))
        N = ctx.enter_context(nc.sbuf_tensor("tk_n", [P, DT, T], F32))
        squares, summed, mean_ready, root_ready, dve_step, scaled, turned = semaphores(
            ctx, nc, " ".join(f"tk_{s}" for s in "squares summed mean_ready root_ready dve_step scaled turned".split()))
        block = ctx.enter_context(nc.Block())

        @block.scalar
        def _(act):
            for d in range(DT):
                act.activation(N[:, d, 0:T], H[:, d, 0:T], ACT.Square).then_inc(squares, 1)
            act.wait_ge(mean_ready, 1)
            act.activation(rstd[:], rstd[:], ACT.Sqrt).then_inc(root_ready, 1)

        @block.tensor
        def _(pe):
            for d in range(DT):
                pe.wait_ge(squares, d + 1)
                ins = pe.matmul(ps[:, 0, 0:T], ones[:], N[:, d, 0:T], start=(d == 0), stop=(d == DT - 1))
            ins.then_inc(summed, 1)
            for d in range(DT):
                pe.wait_ge(scaled, d + 1)
                for a in range(TT):
                    ins = pe.transpose(ps[:, 2 + 2 * a + d // 4, (d % 4) * P:(d % 4 + 1) * P],
                                       N[:, d, a * P:(a + 1) * P], ident[:])
            ins.then_inc(turned, 1)

        @block.vector
        def _(dve):
            step = Chain(dve, dve_step)
            dve.wait_ge(summed, 1)
            dve.tensor_scalar(rstd[:], ps[:, 0, 0:T], 1.0 / D, RMS_EPS, ALU.mult, ALU.add).then_inc(mean_ready, 1)
            dve.wait_ge(root_ready, 1)
            step(dve.reciprocal(rstd[:], rstd[:]))
            for d in range(DT):
                dve.scalar_tensor_tensor(N[:, d, 0:T], H[:, d, 0:T], VA[:, VA_FNORM + d:VA_FNORM + d + 1], rstd[:],
                                         ALU.mult, ALU.mult).then_inc(scaled, 1)
            dve.wait_ge(turned, 1)
            for a in range(TT):
                dve.tensor_copy(X[:, a, :], ps[:, 2 + 2 * a:4 + 2 * a, :].rearrange("p a n -> p (a n)"))


def residual_norm(nc, S, name, g_row, b_row, add, out=None):
    ps, ident, X, XT = S["ps"], S["ident"], S["X"], S["XT"]
    with ExitStack() as ctx:
        g = ctx.enter_context(nc.sbuf_tensor(f"{name}_g", [P, D], F32))
        b = ctx.enter_context(nc.sbuf_tensor(f"{name}_b", [P, D], F32))
        stats = ctx.enter_context(nc.sbuf_tensor(f"{name}_stats", [P, TT, 2, 6], F32))
        mv = ctx.enter_context(nc.sbuf_tensor(f"{name}_mv", [P, TT, 2], F32))
        sd = ctx.enter_context(nc.sbuf_tensor(f"{name}_sd", [P, TT], F32))
        rows_in, var_ready, sd_ready, x_ready, turned, xt_ready, dve_step, stored = sems = semaphores(
            ctx, nc, " ".join(f"{name}_{s}" for s in
                              "rows_in var_ready sd_ready x_ready turned xt_ready dve_step stored".split()))
        with nc.Block() as block:

            @block.sync
            def _(sp):
                sp.dma_start(g[:], g_row.partition_broadcast(P)).then_inc(rows_in, 16)
                sp.dma_start(b[:], b_row.partition_broadcast(P)).then_inc(rows_in, 16)
                sp.wait_ge(rows_in, 32)
                if out is not None:
                    for a in range(TT):
                        sp.wait_ge(x_ready, a + 1)
                        sp.dma_start(out[0, a * P:(a + 1) * P, :], X[:, a, :]).then_inc(stored, 16)
                    sp.wait_ge(stored, 16 * TT)

            @block.vector
            def _(dve):
                step = Chain(dve, dve_step)
                if add:
                    for a in range(TT):
                        v = X[:, a, :]
                        ins = dve.scalar_tensor_tensor(v, v, ALPHA, ps[:, 2 * a:2 * a + 2, :].rearrange("p a n -> p (a n)"),
                                                       ALU.mult, ALU.add)
                    step(ins)
                for a in range(TT):
                    for h in range(2):
                        ins = dve.bn_stats(stats[:, a, h, :], X[:, a, h * CH:(h + 1) * CH])
                step(ins)
                for a in range(TT):
                    ins = dve.bn_aggr(mv[:, a, :], stats[:, a, :, :].rearrange("p a b -> p (a b)"))
                step(ins)
                dve.tensor_scalar(sd[:], mv[:, :, 1], LN_EPS, None, ALU.add).then_inc(var_ready, 1)
                dve.wait_ge(sd_ready, 1)
                step(dve.reciprocal(sd[:], sd[:]))
                dve.wait_ge(rows_in, 32)
                for a in range(TT):
                    v = X[:, a, :]
                    step(dve.tensor_scalar(v, v, mv[:, a, 0:1], sd[:, a:a + 1], ALU.subtract, ALU.mult))
                    step(dve.tensor_tensor(v, v, g[:], ALU.mult))
                    dve.tensor_tensor(v, v, b[:], ALU.add).then_inc(x_ready, 1)

            @block.tensor
            def _(pe):
                for a in range(TT):
                    pe.wait_ge(x_ready, a + 1)
                    for d in range(DT):
                        ins = pe.transpose(ps[:, 4 + 2 * a + d // 4, (d % 4) * P:(d % 4 + 1) * P],
                                           X[:, a, d * P:(d + 1) * P], ident[:])
                    ins.then_inc(turned, 1)

            @block.scalar
            def _(act):
                act.wait_ge(var_ready, 1)
                act.activation(sd[:], sd[:], ACT.Sqrt).then_inc(sd_ready, 1)
                for a in range(TT):
                    act.wait_ge(turned, a + 1)
                    act.activation(XT[:, :, a * P:(a + 1) * P],
                                   ps[:, 4 + 2 * a:6 + 2 * a, :].rearrange("p a (d t) -> p (a d) t", d=4), ACT.Copy)
        return sems


SSD_H, HD64 = 8, 64
CB_W = T + P


class SsdMixer:

    SEMAPHORES = """conv_ready silu_ready turned m_ready exp_ready ln_ready adt_ready acs_made acs_out rows_made cb_made
        diff_ready decay_ready sd_ready y_made mean_ready root_ready bm_ready y_taken"""

    def __init__(self, ctx, nc, S, sems, step):
        sb = lambda n, s: ctx.enter_context(nc.sbuf_tensor(f"sd_{n}", s, F32))
        self.S, self.step = S, step
        (self.conv_ready, self.silu_ready, self.turned, self.m_ready, self.exp_ready, self.ln_ready, self.adt_ready,
         self.acs_made, self.acs_out, self.rows_made, self.cb_made, self.diff_ready, self.decay_ready, self.sd_ready,
         self.y_made, self.mean_ready, self.root_ready, self.bm_ready, self.y_taken) = sems
        self.xc = sb("xc", [P, 6, T])
        self.xh, self.xdt, self.sq = (sb(n, [P, TT, BW]) for n in ("xh", "xdt", "sq"))
        self.dt, self.m, self.e, self.adt, self.acs = (sb(n, [P, TT, 8]) for n in ("dt", "m", "e", "adt", "acs"))
        self.aexp = sb("aexp", [P, 8])
        self.adtb = sb("adtb", [P, TT, 8, P])
        self.bm = sb("bm", [P, 2, T])
        self.cbm = sb("cbm", [P, 2, CB_W])
        self.SD = sb("SD", [P, 8, CB_W])
        self.rs = sb("rs", [P, 2 * TT])

    def begin(self, dve):
        S, step, dt, m = self.S, self.step, self.dt, self.m
        step(dve.tensor_tensor(dt[:], S["DTR"][:], S["RB"][:, RB_DTB:RB_DTB + 8].unsqueeze(1).to_broadcast([P, TT, 8]), ALU.add))
        step(dve.tensor_scalar(m[:], dt[:], -1.0, None, ALU.mult))
        dve.tensor_tensor(m[:], m[:], dt[:], ALU.min).then_inc(self.m_ready, 1)
        step(dve.tensor_scalar(dt[:], dt[:], 0.0, None, ALU.max))
        self.tap(dve, 0)

    def tap(self, dve, j):
        VL, XBC, xc = self.S["VL"], self.S["XBC"], self.xc
        for c in range(6):
            w = VL[:, VL_CONVW + 6 * j + c:VL_CONVW + 6 * j + c + 1]
            if j == 0:
                ins = dve.tensor_scalar(xc[:, c, :], XBC[:, c, 0:T], w, VL[:, VL_CONVB + c:VL_CONVB + c + 1], ALU.mult, ALU.add)
            else:
                ins = dve.scalar_tensor_tensor(xc[:, c, :], XBC[:, c, j:j + T], w, xc[:, c, :], ALU.mult, ALU.add)
        if j < 3:
            self.step(ins)
        else:
            ins.then_inc(self.conv_ready, 1)

    def time_steps(self, dve):
        dt, adt = self.dt, self.adt
        dve.wait_ge(self.ln_ready, 1)
        self.step(dve.tensor_tensor(dt[:], dt[:], self.m[:], ALU.add))
        dve.scalar_tensor_tensor(adt[:], dt[:], -1.0, self.aexp[:].unsqueeze(1).to_broadcast([P, TT, 8]),
                                 ALU.mult, ALU.mult).then_inc(self.adt_ready, 1)
        dve.wait_ge(self.adt_ready, 1)
        for a in range(TT):
            ins = dve.tensor_copy(self.adtb[:, a], adt[:, a, :].unsqueeze(2).to_broadcast([P, 8, P]))
        ins.then_inc(self.adt_ready, 1)

    def running_sums(self, dve):
        dve.wait_ge(self.acs_made, 1)
        dve.tensor_copy(self.acs[:], self.S["ps"][:, 4, 0:16].rearrange("p (a h) -> p a h", a=TT)).then_inc(self.acs_out, 1)
        dve.wait_ge(self.silu_ready, 1)
        for g in range(2):
            ins = dve.tensor_scalar(self.bm[:, g, :], self.xc[:, 4, :], self.S["hm2"][:, g:g + 1], None, ALU.mult)
        ins.then_inc(self.bm_ready, 1)

    def token_major(self, dve):
        heads = lambda v: v.rearrange("p a (h c) -> p (a h) c", c=HD64)
        dve.wait_ge(self.turned, 1)
        self.step(dve.tensor_copy(self.xh[:], self.S["ps"][:, 4:6, :]))
        per_head = self.dt[:].rearrange("p a h -> p (a h)").unsqueeze(2).to_broadcast([P, TT * SSD_H, HD64])
        dve.tensor_tensor(heads(self.xdt[:]), heads(self.xh[:]), per_head, ALU.mult)

    def differences(self, dve):
        ps, acs, SD = self.S["ps"], self.acs, self.SD
        dve.wait_ge(self.acs_out, 1)
        dve.wait_ge(self.rows_made, 1)
        for h in range(SSD_H):
            row = ps[:, h // 2, (h % 2) * T:(h % 2 + 1) * T]
            dve.tensor_scalar(SD[:, h, 0:T], row, acs[:, 0, h:h + 1], 0.0, ALU.subtract, ALU.min)
            ins = dve.tensor_scalar(SD[:, h, T:], row[:, P:T], acs[:, 1, h:h + 1], 0.0, ALU.subtract, ALU.min)
        ins.then_inc(self.diff_ready, 1)

    def weights(self, dve):
        ps, cbm, triu = self.S["ps"], self.cbm, self.S["triu"]
        dve.wait_ge(self.cb_made, 1)
        for g in range(2):
            dve.tensor_tensor(cbm[:, g, 0:P], ps[:, g, 0:P], triu[:], ALU.mult)
            dve.tensor_copy(cbm[:, g, P:T], ps[:, g, P:T])
            ins = dve.tensor_tensor(cbm[:, g, T:], ps[:, g, T:CB_W], triu[:], ALU.mult)
        self.step(ins)
        dve.wait_ge(self.decay_ready, 1)
        for g in range(2):
            v = self.SD[:, 4 * g:4 * g + 4, :]
            dve.tensor_tensor(v, v, cbm[:, g, :].unsqueeze(1).to_broadcast([P, 4, CB_W]), ALU.mult).then_inc(self.sd_ready, 1)
        for a in range(TT):
            v = self.xh[:, a, :].rearrange("p (h c) -> p h c", c=HD64)
            skip = self.S["RB"][:, RB_DSKIP:RB_DSKIP + 8].unsqueeze(2).to_broadcast([P, 8, HD64])
            ins = dve.tensor_tensor(v, v, skip, ALU.mult)
        self.step(ins)

    def take_outputs(self, dve):
        dve.wait_ge(self.y_made, 1)
        dve.tensor_tensor(self.S["YT"][:, :, 0:BW], self.S["ps"][:, 4:6, :], self.xh[:], ALU.add).then_inc(self.y_taken, 1)

    def finish(self, dve):
        YT, RB, rs, sq, step = self.S["YT"], self.S["RB"], self.rs, self.sq, self.step
        y = YT[:, :, 0:BW]
        dve.wait_ge(self.y_taken, 1)
        step(dve.tensor_tensor(y, y, self.S["Z"][:], ALU.mult))
        step(dve.tensor_tensor(sq[:], y, y, ALU.mult))
        step(dve.tensor_reduce(rs[:], sq[:].rearrange("p a (g c) -> p (a g) c", g=2), AX.X, ALU.add))
        dve.tensor_scalar(rs[:], rs[:], 1.0 / 256, RMS_EPS, ALU.mult, ALU.add).then_inc(self.mean_ready, 1)
        dve.wait_ge(self.root_ready, 1)
        step(dve.reciprocal(rs[:], rs[:]))
        for a in range(TT):
            for g in range(2):
                c = slice(256 * g, 256 * g + 256)
                dve.scalar_tensor_tensor(YT[:, a, c], YT[:, a, c], rs[:, 2 * a + g:2 * a + g + 1],
                                         RB[:, RB_SSDN + 256 * g:RB_SSDN + 256 * g + 256], ALU.mult, ALU.mult)

    def activations(self, act):
        act.wait_ge(self.m_ready, 1)
        act.activation(self.aexp[:], self.S["RB"][:, RB_ALOG:RB_ALOG + 8], ACT.Exp)
        act.activation(self.e[:], self.m[:], ACT.Exp).then_inc(self.exp_ready, 1)
        act.wait_ge(self.exp_ready, 1)
        act.activation(self.m[:], self.e[:], ACT.Ln, bias=1.0).then_inc(self.ln_ready, 1)
        act.wait_ge(self.conv_ready, 1)
        act.activation(self.xc[:], self.xc[:], ACT.Silu).then_inc(self.silu_ready, 1)

    def decays(self, act):
        act.wait_ge(self.diff_ready, 1)
        act.activation(self.SD[:], self.SD[:], ACT.Exp).then_inc(self.decay_ready, 1)

    def root(self, act):
        act.wait_ge(self.mean_ready, 1)
        act.activation(self.rs[:], self.rs[:], ACT.Sqrt).then_inc(self.root_ready, 1)

    def sum_steps(self, pe):
        ps, triu, ones, adt = self.S["ps"], self.S["triu"], self.S["ones"], self.adt
        pe.wait_ge(self.adt_ready, 1)
        pe.matmul(ps[:, 4, 0:8], triu[:], adt[:, 0, :], start=True, stop=True)
        pe.matmul(ps[:, 4, 8:16], triu[:], adt[:, 1, :], start=True, stop=False)
        pe.matmul(ps[:, 4, 8:16], ones[:], adt[:, 0, :], start=False, stop=True).then_inc(self.acs_made, 1)

    def sum_rows(self, pe):
        ps, triu, ones, adtb = self.S["ps"], self.S["triu"], self.S["ones"], self.adtb
        pe.wait_ge(self.adt_ready, 2)
        for h in range(SSD_H):
            bank, c = h // 2, (h % 2) * T
            pe.matmul(ps[:, bank, c:c + P], adtb[:, 0, h, :], triu[:], start=True, stop=True)
            pe.matmul(ps[:, bank, c + P:c + T], adtb[:, 0, h, :], ones[:], start=True, stop=False)
            ins = pe.matmul(ps[:, bank, c + P:c + T], adtb[:, 1, h, :], triu[:], start=False, stop=True)
        ins.then_inc(self.rows_made, 1)

    def turn(self, pe):
        pe.wait_ge(self.silu_ready, 1)
        pe.wait_ge(self.acs_out, 1)
        for a in range(TT):
            for c in range(4):
                ins = pe.transpose(self.S["ps"][:, 4 + a, c * P:(c + 1) * P], self.xc[:, c, a * P:(a + 1) * P], self.S["ident"][:])
        ins.then_inc(self.turned, 1)

    def scores(self, pe):
        ps, bm, xc = self.S["ps"], self.bm, self.xc
        pe.wait_ge(self.bm_ready, 1)
        pe.wait_ge(self.diff_ready, 1)
        for g in range(2):
            pe.matmul(ps[:, g, 0:T], bm[:, g, 0:P], xc[:, 5, :], start=True, stop=True)
            ins = pe.matmul(ps[:, g, T:CB_W], bm[:, g, P:T], xc[:, 5, P:T], start=True, stop=True)
        ins.then_inc(self.cb_made, 1)

    def outputs(self, pe, g):
        ps, SD, xdt = self.S["ps"], self.SD, self.xdt
        pe.wait_ge(self.sd_ready, g + 1)
        for h in range(4 * g, 4 * g + 4):
            c = slice(h * HD64, (h + 1) * HD64)
            pe.matmul(ps[:, 4, c], SD[:, h, 0:P], xdt[:, 0, c], start=True, stop=True)
            pe.matmul(ps[:, 5, c], SD[:, h, P:T], xdt[:, 0, c], start=True, stop=False)
            ins = pe.matmul(ps[:, 5, c], SD[:, h, T:], xdt[:, 1, c], start=False, stop=True)
        if g:
            ins.then_inc(self.y_made, 1)


class GlaMixer:

    SEMAPHORES = """gate_made m_ready e_ready ln_ready diff_ready decay_ready km_ready scored prod_ready cross_ready
        o_made mean_ready root_ready"""
    NL = LEVELS + 1

    def __init__(self, ctx, nc, S, sems, step, ssd):
        sb = lambda n, s: ctx.enter_context(nc.sbuf_tensor(f"gl_{n}", s, F32))
        self.S, self.step = S, step
        (self.gate_made, self.m_ready, self.e_ready, self.ln_ready, self.diff_ready, self.decay_ready, self.km_ready,
         self.scored, self.prod_ready, self.cross_ready, self.o_made, self.mean_ready, self.root_ready) = sems
        self.x, self.m, self.e, self.keep = (sb(n, [P, T]) for n in ("x", "m", "e", "keep"))
        self.EB = sb("EB", [P, self.NL, T])
        self.KM = sb("KM", [P, 2, self.NL + 1, T])
        self.prod = ssd.adtb[:].rearrange("p a h t -> p a (h t)")
        self.cross = ssd.xc[:, 0:2, :].rearrange("p a (b t) -> p (a b) t", b=2)
        self.sq = ssd.bm
        self.rs = sb("rs", [P, TT * 4])

    def gate(self, pe):
        pe.matmul(self.S["ps"][:, 3, 0:T], self.S["WA2"][:], self.S["GA"][:], start=True, stop=True).then_inc(self.gate_made, 1)

    def head_products(self, pe, h, cross_free):
        ps, KM, EB, prod, NL = self.S["ps"], self.KM, self.EB, self.prod, self.NL
        pe.wait_ge(self.km_ready, h + 1)
        for tt in range(TT):
            y = 2 * h + tt
            if y >= 2:
                pe.wait_ge(self.prod_ready, y - 1)
            c = slice(tt * P, (tt + 1) * P)
            for l in range(NL):
                ins = pe.matmul(ps[:, 2 * (y % 2) + l // 4, (l % 4) * P:(l % 4 + 1) * P],
                                KM[:, h % 2, l, c], self.S["GQ"][:, c] if l == 0 else EB[:, l - 1, c], start=True, stop=True)
            ins.then_inc(self.scored, 1)
        if h == 0:
            pe.wait_ge(cross_free, 1)
        pe.matmul(ps[:, 4, h * P:(h + 1) * P], KM[:, h % 2, NL, 0:P], EB[:, NL - 1, P:T],
                  start=True, stop=True).then_inc(self.scored, 1)
        out = lambda tt: ps[:, 5, tt * 256 + h * HD64:tt * 256 + (h + 1) * HD64]
        for tt in range(TT):
            y = 2 * h + tt
            pe.wait_ge(self.prod_ready, y + 1)
            v = self.S["GV"][:, tt, h * HD64:(h + 1) * HD64]
            for l in range(NL):
                ins = pe.matmul(out(tt), prod[:, y % 2, l * P:(l + 1) * P], v,
                                start=(l == 0), stop=(l == NL - 1 and tt == 0))
            if tt == 0:
                ins.then_inc(self.o_made, 1)
        pe.wait_ge(self.cross_ready, h + 1)
        pe.matmul(out(1), self.cross[:, h, :], self.S["GV"][:, 0, h * HD64:(h + 1) * HD64],
                  start=False, stop=True).then_inc(self.o_made, 1)

    def activations(self, act):
        act.wait_ge(self.m_ready, 1)
        act.activation(self.e[:], self.m[:], ACT.Exp).then_inc(self.e_ready, 1)
        act.wait_ge(self.e_ready, 1)
        act.activation(self.m[:], self.e[:], ACT.Ln, bias=1.0).then_inc(self.ln_ready, 1)
        act.wait_ge(self.diff_ready, 1)
        act.activation(self.EB[:], self.EB[:], ACT.Exp).then_inc(self.decay_ready, 1)

    def root(self, act):
        act.wait_ge(self.mean_ready, 1)
        act.activation(self.rs[:], self.rs[:], ACT.Sqrt).then_inc(self.root_ready, 1)

    def gate_argument(self, dve):
        S, x, m, step = self.S, self.x, self.m, self.step
        dve.memset(self.keep[:], 1.0)
        dve.tensor_scalar(S["GQ"][:], S["GQ"][:], 32 ** -0.5, None, ALU.mult)
        dve.wait_ge(self.gate_made, 1)
        step(dve.tensor_scalar(x[:], S["ps"][:, 3, 0:T], S["VL"][:, VL_GBA:VL_GBA + 1], None, ALU.add))
        step(dve.tensor_scalar(m[:], x[:], -1.0, None, ALU.mult))
        dve.tensor_tensor(m[:], m[:], x[:], ALU.min).then_inc(self.m_ready, 1)

    def differences(self, dve):
        x, m, e, step = self.x, self.m, self.e, self.step
        dve.wait_ge(self.ln_ready, 1)
        step(dve.scalar_tensor_tensor(x[:], x[:], 0.0, m[:], ALU.min, ALU.subtract))
        step(dve.tensor_scalar(x[:], x[:], 1.0 / 16.0, None, ALU.mult))
        step(dve.tensor_tensor_scan(e[:], self.keep[:], x[:], 0.0, ALU.mult, ALU.add))
        for l in range(self.NL):
            ins = block_differences(dve, self.EB[:, l, :], e[:], 2 << l, False)
        ins.then_inc(self.diff_ready, 1)

    def merge_keys_queries(self, dve):
        dve.wait_ge(self.decay_ready, 1)
        for l in range(self.NL):
            v = self.EB[:, l, :].rearrange("p (n two s) -> p n two s", two=2, s=1 << l)
            for side, src in ((0, self.S["GK"]), (1, self.S["GQ"])):
                w = src[:].rearrange("p (n two s) -> p n two s", two=2, s=1 << l)
                ins = dve.tensor_tensor(v[:, :, side, :], v[:, :, side, :], w[:, :, side, :], ALU.mult)
        self.step(ins)

    def one_head(self, dve, h):
        hm4 = self.S["hm4"]
        if h >= 2:
            dve.wait_ge(self.scored, 3 * (h - 1))
        dve.tensor_scalar(self.KM[:, h % 2, 0, :], self.S["GK"][:], hm4[:, h:h + 1], None, ALU.mult)
        dve.tensor_scalar(self.KM[:, h % 2, 1:, :], self.EB[:], hm4[:, h:h + 1], None, ALU.mult).then_inc(self.km_ready, 1)

    def mask(self, dve, h):
        ps, prod = self.S["ps"], self.prod
        for tt in range(TT):
            y = 2 * h + tt
            dve.wait_ge(self.scored, 3 * h + tt + 1)
            if y >= 2:
                dve.wait_ge(self.o_made, y - 1)
            dve.tensor_tensor(prod[:, y % 2, :], ps[:, 2 * (y % 2):2 * (y % 2) + 2, :].rearrange("p a b -> p (a b)"),
                              self.S["masks"][:, 0].rearrange("p l c -> p (l c)"), ALU.mult).then_inc(self.prod_ready, 1)
        dve.wait_ge(self.scored, 3 * h + 3)
        dve.tensor_copy(self.cross[:, h, :], ps[:, 4, h * P:(h + 1) * P]).then_inc(self.cross_ready, 1)

    def finish(self, dve):
        S, sq, rs, step = self.S, self.sq, self.rs, self.step
        GG, y = S["GG"], S["YT"][:, :, 768:1024]
        dve.wait_ge(self.o_made, 8)
        step(dve.tensor_copy(y, S["ps"][:, 5, :].rearrange("p (a c) -> p a c", a=TT)))
        step(dve.tensor_tensor(sq[:], y, y, ALU.mult))
        step(dve.tensor_reduce(rs[:], sq[:].rearrange("p a (h c) -> p (a h) c", c=HD64), AX.X, ALU.add))
        dve.tensor_scalar(rs[:], rs[:], 1.0 / HD64, RMS_EPS, ALU.mult, ALU.add).then_inc(self.mean_ready, 1)
        step(dve.tensor_tensor(GG[:], GG[:], S["RB"][:, RB_GLAN:RB_GLAN + 256].unsqueeze(1).to_broadcast([P, TT, 256]), ALU.mult))
        dve.wait_ge(self.root_ready, 1)
        step(dve.reciprocal(rs[:], rs[:]))
        step(dve.tensor_tensor(y, y, GG[:], ALU.mult))
        for a in range(TT):
            v = S["YT"][:, a, 768:1024].rearrange("p (h c) -> p h c", c=HD64)
            dve.tensor_tensor(v, v, rs[:, 4 * a:4 * a + 4].unsqueeze(2).to_broadcast([P, 4, HD64]), ALU.mult)


def project_and_mix(nc, S, ring, l):
    ps, ident, XT, t = S["ps"], S["ident"], S["XT"], S["t"]
    VL, RB, LR, WA2 = S["VL"], S["RB"], S["LR"], S["WA2"]
    with ExitStack() as ctx:
        rows = ctx.enter_context(nc.sbuf_tensor("rows2", [VL_ROWS, P], F32))
        vec_in, vec_turned, vec_out, tile_ready, act_out, dve_out, dve_step, *mixer_sems = semaphores(
            ctx, nc, "w2_vec_in w2_vec_turned w2_vec_out w2_tile_ready w2_act_out w2_dve_out w2_dve_step "
            + " ".join([f"sd_{s}" for s in SsdMixer.SEMAPHORES.split()] + [f"gl_{s}" for s in GlaMixer.SEMAPHORES.split()]))
        step = Chain(nc.vector, dve_step)
        ssd_sems = len(SsdMixer.SEMAPHORES.split())
        ssd = SsdMixer(ctx, nc, S, mixer_sems[:ssd_sems], step)
        gla = GlaMixer(ctx, nc, S, mixer_sems[ssd_sems:], step, ssd)
        flat = [(n, kind, col, w, j, m == len(outs) - 1) for n, outs in enumerate(WIN2_OUTPUTS)
                for m, (kind, col, w, j) in enumerate(outs)]
        dest = {"z": lambda j: S["Z"][:, j, :], "gg": lambda j: S["GG"][:, j, :], "gv": lambda j: S["GV"][:, j, :],
                "dt": lambda j: S["DTR"][:, j, :], "xbc": lambda j: S["XBC"][:, j, 3:T + 3],
                "rw": lambda j: S["RW"][:, j, 1:T + 1], "gq": lambda j: S["GQ"][:], "gk": lambda j: S["GK"][:],
                "ga": lambda j: S["GA"][:]}
        OWN = sum(len(outs) for outs in WIN2_OUTPUTS[:3])
        bank = lambda i: i % 6 if i < OWN else 7 - (i - OWN) % 2
        layer = lambda name: t[name + "_2"][bass.ds(l, 1)]
        with nc.Block() as block:

            def copied(eng, i):
                mine = flat[i][1] in BY_ACT
                eng.wait_ge(act_out if mine else dve_out, sum((f[1] in BY_ACT) == mine for f in flat[:i + 1]))

            def ready(eng, i):
                if flat[i][5]:
                    eng.wait_ge(ring.used, C2_WIN + flat[i][0] + 1)
                else:
                    eng.wait_ge(tile_ready, sum(not f[5] for f in flat[:i + 1]))

            @block.sync
            def _(sp):
                for n in range(ring.slots):
                    ring.load(sp, n, layer_chunk(t, n, l))
                for at, name in ((VL_CONVB, "ssd_conv_b"), (VL_MU, "rwkv_mu"), (VL_W0, "rwkv_w0"), (VL_A0, "rwkv_a0"),
                                 (VL_KK, "rwkv_k_k"), (VL_KA, "rwkv_k_a"), (VL_GBA, "gla_b_a")):
                    src = layer(name).rearrange("a (r c) -> (a r) c", c=P)
                    sp.dma_start(rows[at:at + src.shape[0], :], src).then_inc(vec_in, 16)
                sp.dma_start(rows[VL_CONVW:VL_CONVW + 24, :],
                             layer("ssd_conv_w").rearrange("a j (r c) -> (a j r) c", c=P)).then_inc(vec_in, 16)
                sp.dma_start(rows[VL_RK:VL_RK + 2, :],
                             layer("rwkv_r_k").rearrange("a (r h) c -> (a r) (h c)", h=2)).then_inc(vec_in, 16)
                for at, name in ((RB_SSDN, "ssd_norm_g"), (RB_LNG, "rwkv_ln_g"), (RB_LNB, "rwkv_ln_b"),
                                 (RB_GLAN, "gla_norm_g"), (RB_DTB, "ssd_dt_bias"), (RB_ALOG, "ssd_a_log"),
                                 (RB_DSKIP, "ssd_d")):
                    src = layer(name).rearrange("a n -> (a n)")
                    sp.dma_start(RB[:, at:at + src.shape[0]], src.partition_broadcast(P)).then_inc(vec_in, 16)
                for i, (name, a, b) in enumerate((("rwkv_w2", 0, 32), ("rwkv_a2", 32, 64), ("rwkv_g2", 64, 128))):
                    sp.dma_start(LR[a:b, i, :], layer(name).rearrange("a r n -> (a r) n")).then_inc(vec_in, 16)
                sp.dma_start(WA2[:], layer("gla_w_a2").rearrange("a r n -> (a r) n")).then_inc(vec_in, 16)
                sp.dma_start(S["WR"][:, :, 0:4], layer("moe_w_rg").rearrange("a (k p) n -> p (a k) n", p=P)).then_inc(vec_in, 16)
                sp.dma_start(S["WR"][:, :, 4:36], layer("moe_w_re").rearrange("a (k p) n -> p (a k) n", p=P)).then_inc(vec_in, 16)
                sp.dma_start(S["BR"][:, 0:4], layer("moe_b_rg").rearrange("a n -> (a n)").partition_broadcast(P)).then_inc(vec_in, 16)
                sp.dma_start(S["BR"][:, 4:36], layer("moe_b_re").rearrange("a n -> (a n)").partition_broadcast(P)).then_inc(vec_in, 16)
                for n in range(ring.slots, C2_END):
                    ring.load(sp, n, layer_chunk(t, n, l))

            @block.tensor
            def _(pe):
                for i, (n, kind, col, w, j, last) in enumerate(flat):
                    if i == 0 or flat[i - 1][0] != n:
                        ring.arrived(pe, C2_WIN + n)
                    if i == OWN:
                        pe.wait_ge(vec_in, 16 * 24)
                        pe.transpose(ps[:, 6, 0:VL_ROWS], rows[:], ident[0:VL_ROWS, 0:VL_ROWS]).then_inc(vec_turned, 1)
                    if i == OWN + 1:
                        pe.wait_ge(vec_out, 1)
                    if 6 <= i < OWN:
                        copied(pe, i - 6)
                    elif i >= OWN + 2:
                        copied(pe, i - 2)
                    a, b = WIN2_BOUNDS[n]
                    wv = ring.view(C2_WIN + n, DT, b - a)
                    for k in range(DT):
                        if kind in TOKEN_MAJOR:
                            ins = pe.matmul(ps[:, bank(i), 0:w], XT[:, k, j * P:(j + 1) * P], wv[:, k, col:col + w],
                                            start=(k == 0), stop=(k == DT - 1))
                        else:
                            ins = pe.matmul(ps[0:w, bank(i), 0:T], wv[:, k, col:col + w], XT[:, k, :],
                                            start=(k == 0), stop=(k == DT - 1))
                    ins.then_inc(ring.used if last else tile_ready, 1)
                    if i - OWN == 3:
                        ssd.sum_steps(pe)
                    elif i - OWN == 4:
                        ssd.sum_rows(pe)
                    elif i - OWN == 5:
                        ssd.turn(pe)
                    elif i - OWN == 8:
                        ssd.scores(pe)
                        gla.gate(pe)
                    elif i - OWN in (10, 11):
                        ssd.outputs(pe, i - OWN - 10)
                for h in range(4):
                    gla.head_products(pe, h, ssd.y_taken)

            @block.scalar
            def _(act):
                for i, (n, kind, col, w, j, last) in enumerate(flat):
                    if i == OWN:
                        ssd.activations(act)
                    if kind in BY_ACT:
                        ready(act, i)
                        act.activation(dest[kind](j), ps[:, bank(i), 0:w], ACT.Silu).then_inc(act_out, 1)
                ssd.decays(act)
                gla.activations(act)
                ssd.root(act)
                gla.root(act)

            @block.vector
            def _(dve):
                dve.memset(S["XBC"][:, :, 0:3], 0.0)
                dve.memset(S["RW"][:, :, 0:1], 0.0)
                for i, (n, kind, col, w, j, last) in enumerate(flat):
                    if i == OWN:
                        dve.wait_ge(vec_turned, 1)
                        dve.tensor_copy(VL[:], ps[:, 6, 0:VL_ROWS]).then_inc(vec_out, 1)
                        dve.wait_ge(vec_out, 1)
                        dve.wait_ge(dve_out, sum(f[1] not in BY_ACT for f in flat[:OWN]))
                        ssd.begin(dve)
                    if kind not in BY_ACT:
                        ready(dve, i)
                        src = ps[:, bank(i), 0:w] if kind in TOKEN_MAJOR else ps[0:w, bank(i), 0:T]
                        dve.tensor_copy(dest[kind](j), src).then_inc(dve_out, 1)
                    if i - OWN in (0, 1, 2):
                        ssd.tap(dve, i - OWN + 1)
                    if i - OWN == 2:
                        ssd.time_steps(dve)
                    elif i - OWN == 4:
                        ssd.running_sums(dve)
                    elif i - OWN == 6:
                        ssd.token_major(dve)
                    elif i - OWN == 7:
                        ssd.differences(dve)
                    elif i - OWN == 9:
                        ssd.weights(dve)
                        gla.gate_argument(dve)
                    elif i - OWN == 10:
                        gla.differences(dve)
                    elif i - OWN == 11:
                        gla.merge_keys_queries(dve)
                        gla.one_head(dve, 0)
                ssd.take_outputs(dve)
                for h in range(4):
                    if h < 3:
                        gla.one_head(dve, h + 1)
                    gla.mask(dve, h)
                    if h == 0:
                        ssd.finish(dve)
                gla.finish(dve)


def layer_chunk(t, n, l):
    at = bass.ds(l, 1)
    if n < C2_WOUT:
        a, b = WIN2_BOUNDS[n]
        return t["w_in_2"][at].rearrange("a (k p) n -> p (a k) n", p=P)[:, :, a:b]
    a = CH * (n - C2_WOUT)
    return t["w_out_2"][at].rearrange("a (k p) n -> p (a k) n", p=P)[:, :, a:a + CH]


def expert_chunk(t, le, part):
    w = t[("moe_w_gate_2", "moe_w_up_2", "moe_w_down_2")[part]].rearrange("l e a b -> (l e) a b")
    return w[bass.ds(le, 1)].rearrange("o (k p) n -> p (o k) n", p=P)


def rwkv_mixer(nc, S):
    ps, ident, blockones = S["ps"], S["ident"], S["blockones"]
    masks, triu, VL, RB, LR, RW, YT, hm2 = S["masks"], S["triu"], S["VL"], S["RB"], S["LR"], S["RW"], S["YT"], S["hm2"]
    with ExitStack() as ctx:
        sb = lambda n, s: ctx.enter_context(nc.sbuf_tensor(f"rk_{n}", s, F32))
        p = sb("p", [P, 7, T])
        lact = sb("lact", [P, T])
        gl, av = sb("gl", [P, 2, T]), sb("av", [P, 2, T])
        cum, ce = sb("cum", [P, 2, T]), sb("ce", [P, 2, T])
        e1, e3 = sb("e1", [P, 2, T]), sb("e3", [P, 2, T])
        kk, sq = sb("kk", [P, 2, T]), sb("sq", [P, 2, T])
        keep = sb("keep", [P, P])
        emid = sb("emid", [P, 2, 2])
        bm, km = sb("bm", [P, 2, 2, T]), sb("km", [P, 2, 2, T])
        gt = sb("gt", [P, TT, 256])
        vt = sb("vt", [P, TT, 256])
        bonus = sb("bonus", [P, TT, 256])
        A8 = lambda n: sb(n, [P, 8, P])
        Tm, Ut, DTm, ET = (A8(n) for n in ("Tm", "Ut", "DT", "ET"))
        AT, BT, X, CT0 = (S["arena"][:, 1024 * i:1024 * (i + 1)].rearrange("p (x c) -> p x c", x=8)
                          for i in range(4))
        CT = [CT0, A8("CT1")[:]]
        bt, kt = sb("bt", [P, 2, P]), sb("kt", [P, 2, P])
        s0 = sb("s0", [P, 2, P])
        R, U = sb("R", [P, 2, P]), sb("U", [P, 2, P])
        mean = sb("mean", [P, TT * 4])
        names = """mixed low_ready low_made sig_ready glog_ready cum_ready ssq_ready ssq_made exp_ready root_req root_ready
            ops_ready vt_made vt_ready bonus_made mats_a mats_a_out mats_b mats_b_out mats_d mats_d_out first_ready ct_ready
            x_made x_out tx_made t_ready tok_made tok_out r_made r_out u_made u_out y_made s_made s_out mean_ready
            sd_ready dve_step act_step pool_step""".split()
        sems = semaphores(ctx, nc, " ".join(f"rk_{s}" for s in names))
        s = dict(zip(names, sems))
        bank8 = lambda b: ps[:, b:b + 2, :].rearrange("p a (x c) -> p (a x) c", x=4)
        at8 = lambda b, x: ps[:, b + x // 4, (x % 4) * P:(x % 4 + 1) * P]
        ITEMS = [(c, m, h) for c in range(2) for m in range(2) for h in range(2)]
        cols = lambda c: slice(c * P, (c + 1) * P)
        half = lambda c: slice(4 * c, 4 * c + 4)
        wide = lambda v: v.unsqueeze(1).to_broadcast([P, 8, P])
        with nc.Block() as block:

            @block.vector
            def _(dve):
                step = Chain(dve, dve_step := s["dve_step"])
                dve.memset(keep[:], 1.0)
                step(dve.tensor_tensor(p[:], RW[:, :, 0:T], RW[:, :, 1:T + 1], ALU.subtract))
                for i in (6, 0, 1, 2, 3, 4, 5):
                    ins = dve.scalar_tensor_tensor(p[:, i, :], p[:, i, :], VL[:, VL_MU + i:VL_MU + i + 1], RW[:, i, 1:T + 1],
                                                   ALU.mult, ALU.add)
                    if i in (6, 5):
                        ins.then_inc(s["mixed"], 1)
                dve.wait_ge(s["mixed"], 2)
                for m in range(2):
                    ins = dve.tensor_scalar(kk[:, m, :], p[:, 2 + m, :], VL[:, VL_KK + m:VL_KK + m + 1], None, ALU.mult)
                step(ins)
                dve.tensor_tensor(sq[:], kk[:], kk[:], ALU.mult).then_inc(s["ssq_ready"], 1)
                dve.wait_ge(s["vt_made"], 1)
                dve.tensor_copy(vt[:], ps[:, 4:6, 0:256])
                dve.wait_ge(s["sig_ready"], 2)
                step(dve.tensor_scalar(gl[:], gl[:], -math.exp(-0.5), None, ALU.mult))
                for m in range(2):
                    for c in range(2):
                        ins = dve.tensor_tensor_scan(cum[:, m, cols(c)], keep[:], gl[:, m, cols(c)], 0.0, ALU.mult, ALU.add)
                step(ins)
                dve.tensor_copy(emid[:], cum[:].rearrange("p m (c t) -> p m c t", c=2)[:, :, :, P // 2 - 1])
                step(dve.tensor_tensor(ce[:], cum[:], gl[:], ALU.subtract))
                for m in range(2):
                    for c in range(2):
                        mid = emid[:, m, c:c + 1]
                        dve.tensor_scalar(cum[:, m, cols(c)], cum[:, m, cols(c)], mid, None, ALU.subtract)
                        ins = dve.tensor_scalar(ce[:, m, cols(c)], ce[:, m, cols(c)], mid, None, ALU.subtract)
                ins.then_inc(s["cum_ready"], 1)
                dve.wait_ge(s["ssq_made"], 1)
                for m in range(2):
                    ins = dve.tensor_scalar(sq[:, m, :], av[:, m, :], 1.0, VL[:, VL_KA + m:VL_KA + m + 1],
                                            ALU.subtract, ALU.mult)
                step(ins)
                step(dve.scalar_tensor_tensor(p[:, 2:4, :], sq[:], 1.0, p[:, 2:4, :], ALU.add, ALU.mult))
                dve.tensor_scalar(sq[:], ps[:, 3, :].rearrange("p (m t) -> p m t", m=2), 1e-12, None,
                                  ALU.add).then_inc(s["root_req"], 1)
                dve.wait_ge(s["root_ready"], 1)
                step(dve.reciprocal(sq[:], sq[:]))
                step(dve.tensor_tensor(kk[:], kk[:], sq[:], ALU.mult))
                step(dve.tensor_tensor(av[:], av[:], kk[:], ALU.mult))
                for m in range(2):
                    ins = dve.scalar_tensor_tensor(sq[:, m, :], p[:, m, :], VL[:, VL_RK + m:VL_RK + m + 1], p[:, 2 + m, :],
                                                   ALU.mult, ALU.mult)
                step(ins)
                dve.wait_ge(s["exp_ready"], 1)
                dve.tensor_tensor(kk[:], kk[:], ce[:], ALU.mult)
                dve.tensor_tensor(av[:], av[:], e3[:], ALU.mult)
                dve.tensor_tensor(p[:, 2:4, :], p[:, 2:4, :], e3[:], ALU.mult)
                step(dve.tensor_tensor(p[:, 0:2, :], p[:, 0:2, :], e1[:], ALU.mult))
                for h in range(2):
                    dve.tensor_scalar(bm[:, h], av[:], hm2[:, h:h + 1], None, ALU.mult)
                    ins = dve.tensor_scalar(km[:, h], p[:, 2:4, :], hm2[:, h:h + 1], None, ALU.mult)
                ins.then_inc(s["ops_ready"], 1)
                dve.wait_ge(s["mats_a"], 1)
                step(dve.tensor_copy(AT, bank8(0)))
                step(dve.tensor_tensor(Tm[:], bank8(2), wide(masks[:, 1, 1, :]), ALU.mult))
                step(dve.tensor_tensor(Tm[:], wide(ident[:]), Tm[:], ALU.subtract))
                step(dve.tensor_tensor(Ut[:], AT, wide(masks[:, 0, 1, :]), ALU.mult))
                dve.tensor_tensor(Ut[:], wide(ident[:]), Ut[:], ALU.subtract).then_inc(s["first_ready"], 1)

                def couplings(l):
                    for c in range(2):
                        dve.tensor_tensor(CT[l % 2][:, half(c), :], AT[:, half(c), :],
                                          masks[:, 0, l, :].unsqueeze(1).to_broadcast([P, 4, P]),
                                          ALU.mult).then_inc(s["ct_ready"], 1)

                couplings(2)
                dve.wait_ge(s["mats_b"], 1)
                dve.tensor_tensor(BT, bank8(4), wide(S["triu_strict"][:]), ALU.mult)
                dve.tensor_tensor(DTm[:], bank8(6), wide(triu[:]), ALU.mult).then_inc(s["mats_b_out"], 1)
                couplings(3)
                dve.wait_ge(s["mats_d"], 1)
                dve.tensor_tensor(ET[:], bank8(4), wide(triu[:]), ALU.mult).then_inc(s["mats_d_out"], 1)
                for l in range(2, LEVELS + 1):
                    for c in range(2):
                        dve.wait_ge(s["tx_made"], 2 * (l - 2) + c + 1)
                        dve.tensor_tensor(Tm[:, half(c), :], Tm[:, half(c), :], bank8(2)[:, half(c), :], ALU.subtract)
                        dve.tensor_tensor(Ut[:, half(c), :], Ut[:, half(c), :], bank8(6)[:, half(c), :],
                                          ALU.subtract).then_inc(s["t_ready"], 1)
                    if l + 2 <= LEVELS:
                        couplings(l + 2)
                dve.wait_ge(s["tok_made"], 1)
                dve.tensor_copy(bt[:], ps[:, 4, 0:256].rearrange("p (m c) -> p m c", m=2))
                dve.tensor_copy(kt[:], ps[:, 4, 256:512].rearrange("p (m c) -> p m c", m=2)).then_inc(s["tok_out"], 1)
                for c in range(2):
                    dve.wait_ge(s["r_made"], c + 1)
                    dve.tensor_copy(R[:], ps[:, 0, 0:256].rearrange("p (m c) -> p m c", m=2)).then_inc(s["r_out"], 1)
                    dve.wait_ge(s["u_made"], c + 1)
                    dve.tensor_scalar(U[:], ps[:, 1, 0:256].rearrange("p (m c) -> p m c", m=2), -1.0, None,
                                      ALU.mult).then_inc(s["u_out"], 1)
                    if c == 0:
                        dve.wait_ge(s["s_made"], 1)
                        for m in range(2):
                            ins = dve.scalar_tensor_tensor(s0[:, m, :], ps[:, 5, m * P:(m + 1) * P],
                                                           e1[:, m, P - 1:P], blockones[:], ALU.mult, ALU.mult)
                        step(ins)
                        for m in range(2):
                            ins = dve.tensor_scalar(s0[:, m, :], s0[:, m, :], emid[:, m, 1:2], None, ALU.mult)
                        ins.then_inc(s["s_out"], 1)
                dve.wait_ge(s["y_made"], 2)
                y = YT[:, :, BW:BW + 256]
                yh = lambda v: v.rearrange("p (h c) -> p h c", c=HD64)
                step(dve.tensor_copy(y, ps[:, 2:4, 0:256]))
                for a in range(TT):
                    ins = dve.tensor_reduce(mean[:, 4 * a:4 * a + 4], yh(YT[:, a, BW:BW + 256]), AX.X, ALU.add)
                step(ins)
                step(dve.tensor_scalar(mean[:], mean[:], 1.0 / HD64, None, ALU.mult))
                for a in range(TT):
                    v = yh(YT[:, a, BW:BW + 256])
                    ins = dve.tensor_tensor(v, v, mean[:, 4 * a:4 * a + 4].unsqueeze(2).to_broadcast([P, 4, HD64]), ALU.subtract)
                step(ins)
                sqt = bm[:].rearrange("p a b t -> p (a b t)")[:, 0:512].rearrange("p (a c) -> p a c", a=2)
                step(dve.tensor_tensor(sqt, y, y, ALU.mult))
                for a in range(TT):
                    ins = dve.tensor_reduce(mean[:, 4 * a:4 * a + 4], yh(sqt[:, a, :]), AX.X, ALU.add)
                step(ins)
                dve.tensor_scalar(mean[:], mean[:], 1.0 / HD64, 64e-5, ALU.mult, ALU.add).then_inc(s["mean_ready"], 1)
                dve.wait_ge(s["sd_ready"], 1)
                step(dve.reciprocal(mean[:], mean[:]))
                for a in range(TT):
                    v = yh(YT[:, a, BW:BW + 256])
                    ins = dve.tensor_tensor(v, v, mean[:, 4 * a:4 * a + 4].unsqueeze(2).to_broadcast([P, 4, HD64]), ALU.mult)
                step(ins)
                row = lambda at: RB[:, at:at + 256].unsqueeze(1).to_broadcast([P, TT, 256])
                step(dve.tensor_tensor(y, y, row(RB_LNG), ALU.mult))
                step(dve.tensor_tensor(y, y, row(RB_LNB), ALU.add))
                dve.wait_ge(s["bonus_made"], 1)
                step(dve.tensor_tensor(bonus[:], ps[:, 6:8, 0:256], vt[:], ALU.mult))
                step(dve.tensor_tensor(y, y, bonus[:], ALU.add))
                dve.tensor_tensor(y, y, gt[:], ALU.mult)

            @block.scalar
            def _(act):
                act.wait_ge(s["mixed"], 1)
                act.activation(lact[0:32, :], p[0:32, 6, :], ACT.Tanh)
                act.activation(lact[32:64, :], p[32:64, 6, :], ACT.Copy)
                act.activation(lact[64:128, :], p[64:128, 6, :], ACT.Sigmoid).then_inc(s["low_ready"], 1)
                act.wait_ge(s["low_made"], 1)
                for m in range(2):
                    act.activation(gl[:, m, :], ps[:, 0, m * T:(m + 1) * T], ACT.Sigmoid, bias=VL[:, VL_W0 + m:VL_W0 + m + 1])
                    act.activation(av[:, m, :], ps[:, 1, m * T:(m + 1) * T], ACT.Sigmoid,
                                   bias=VL[:, VL_A0 + m:VL_A0 + m + 1]).then_inc(s["sig_ready"], 1)
                act.activation(gt[:], ps[:, 2, :].rearrange("p (a c) -> p a c", a=2), ACT.Copy)
                act.wait_ge(s["cum_ready"], 1)
                act.activation(e1[:], cum[:], ACT.Exp)
                act.activation(e3[:], cum[:], ACT.Exp, scale=-1.0)
                act.activation(ce[:], ce[:], ACT.Exp)
                act.activation(emid[:], emid[:], ACT.Exp).then_inc(s["exp_ready"], 1)
                act.wait_ge(s["root_req"], 1)
                act.activation(sq[:], sq[:], ACT.Sqrt).then_inc(s["root_ready"], 1)
                for l in range(2, LEVELS + 1):
                    for c in range(2):
                        act.wait_ge(s["x_made"], 2 * (l - 2) + c + 1)
                        act.activation(X[:, half(c), :], bank8(0)[:, half(c), :], ACT.Copy).then_inc(s["x_out"], 1)
                act.wait_ge(s["mean_ready"], 1)
                act.activation(mean[:], mean[:], ACT.Sqrt).then_inc(s["sd_ready"], 1)

            @block.tensor
            def _(pe):
                pe.wait_ge(s["low_ready"], 1)
                for m in range(2):
                    pe.matmul(ps[:, 0, m * T:(m + 1) * T], LR[:, 0, m * P:(m + 1) * P], lact[:], start=True, stop=True)
                    pe.matmul(ps[:, 1, m * T:(m + 1) * T], LR[:, 1, m * P:(m + 1) * P], lact[:], start=True, stop=True)
                for a in range(TT):
                    ins = pe.matmul(ps[:, 2, a * T:(a + 1) * T], lact[:, a * P:(a + 1) * P], LR[:, 2, :], start=True, stop=True)
                ins.then_inc(s["low_made"], 1)
                pe.wait_ge(s["mixed"], 2)
                for a in range(TT):
                    for m in range(2):
                        ins = pe.transpose(ps[:, 4 + a, m * P:(m + 1) * P], p[:, 4 + m, a * P:(a + 1) * P], ident[:])
                ins.then_inc(s["vt_made"], 1)
                pe.wait_ge(s["ssq_ready"], 1)
                pe.matmul(ps[:, 3, :], blockones[:], sq[:].rearrange("p m t -> p (m t)"), start=True,
                          stop=True).then_inc(s["ssq_made"], 1)
                pe.wait_ge(s["ops_ready"], 1)
                for x, (c, m, h) in enumerate(ITEMS):
                    pe.matmul(at8(0, x), bm[:, h, m, cols(c)], kk[:, m, cols(c)], start=True, stop=True)
                    ins = pe.matmul(at8(2, x), kk[:, m, cols(c)], bm[:, h, m, cols(c)], start=True, stop=True)
                ins.then_inc(s["mats_a"], 1)
                for x, (c, m, h) in enumerate(ITEMS):
                    pe.matmul(at8(4, x), km[:, h, m, cols(c)], kk[:, m, cols(c)], start=True, stop=True)
                    ins = pe.matmul(at8(6, x), bm[:, h, m, cols(c)], p[:, m, cols(c)], start=True, stop=True)
                ins.then_inc(s["mats_b"], 1)
                pe.wait_ge(s["mats_b_out"], 1)
                for x, (c, m, h) in enumerate(ITEMS):
                    ins = pe.matmul(at8(4, x), km[:, h, m, cols(c)], p[:, m, cols(c)], start=True, stop=True)
                ins.then_inc(s["mats_d"], 1)
                pe.wait_ge(s["first_ready"], 1)
                for l in range(2, LEVELS + 1):
                    for c in range(2):
                        pe.wait_ge(s["ct_ready"], 2 * (l - 2) + c + 1)
                        if l > 2:
                            pe.wait_ge(s["t_ready"], 2 * (l - 3) + c + 1)
                        for x in range(4 * c, 4 * c + 4):
                            ins = pe.matmul(at8(0, x), CT[l % 2][:, x, :], Tm[:, x, :], start=True, stop=True)
                        ins.then_inc(s["x_made"], 1)
                    for c in range(2):
                        pe.wait_ge(s["x_out"], 2 * (l - 2) + c + 1)
                        for x in range(4 * c, 4 * c + 4):
                            pe.matmul(at8(2, x), Ut[:, x, :], X[:, x, :], start=True, stop=True)
                            ins = pe.matmul(at8(6, x), X[:, x, :], Ut[:, x, :], start=True, stop=True)
                        ins.then_inc(s["tx_made"], 1)
                pe.wait_ge(s["t_ready"], 2 * (LEVELS - 1))
                pe.wait_ge(s["mats_d_out"], 1)
                for m in range(2):
                    pe.transpose(ps[:, 4, m * P:(m + 1) * P], av[:, m, 0:P], ident[:])
                    ins = pe.transpose(ps[:, 4, 256 + m * P:256 + (m + 1) * P], p[:, 2 + m, 0:P], ident[:])
                ins.then_inc(s["tok_made"], 1)
                for a in range(TT):
                    for m in range(2):
                        ins = pe.matmul(ps[:, 6 + a, m * P:(m + 1) * P], sq[:, m, a * P:(a + 1) * P], blockones[:],
                                        start=True, stop=True)
                ins.then_inc(s["bonus_made"], 1)
                hc = lambda m, h: slice(m * P + h * HD64, m * P + (h + 1) * HD64)
                for c in range(2):
                    if c:
                        pe.wait_ge(s["s_out"], 1)
                    for m in range(2):
                        if c:
                            pe.matmul(ps[:, 0, m * P:(m + 1) * P], kk[:, m, cols(1)], s0[:, m, :], start=(m == 0), stop=False,
                                      skip_group_check=True)
                        for h in range(2):
                            ins = pe.matmul(ps[:, 0, hc(m, h)], BT[:, 4 * c + 2 * m + h, :], vt[:, c, hc(m, h)],
                                            start=(c == 0), stop=True, skip_group_check=True)
                    ins.then_inc(s["r_made"], 1)
                    pe.wait_ge(s["r_out"], c + 1)
                    for m in range(2):
                        for h in range(2):
                            ins = pe.matmul(ps[:, 1, hc(m, h)], Ut[:, 4 * c + 2 * m + h, :], R[:, m, h * HD64:(h + 1) * HD64],
                                            start=True, stop=True)
                    ins.then_inc(s["u_made"], 1)
                    pe.wait_ge(s["u_out"], c + 1)
                    if c == 0:
                        pe.wait_ge(s["tok_out"], 1)
                        for m in range(2):
                            pe.matmul(ps[:, 5, m * P:(m + 1) * P], bt[:, m, :], U[:, m, :], start=True, stop=False)
                            ins = pe.matmul(ps[:, 5, m * P:(m + 1) * P], kt[:, m, :], vt[:, 0, m * P:(m + 1) * P],
                                            start=False, stop=True)
                        ins.then_inc(s["s_made"], 1)
                    for m in range(2):
                        if c:
                            pe.matmul(ps[:, 3, m * P:(m + 1) * P], p[:, m, cols(1)], s0[:, m, :], start=(m == 0), stop=False,
                                      skip_group_check=True)
                        for h in range(2):
                            x = 4 * c + 2 * m + h
                            pe.matmul(ps[:, 2 + c, hc(m, h)], DTm[:, x, :], U[:, m, h * HD64:(h + 1) * HD64],
                                      start=(c == 0), stop=False, skip_group_check=True)
                            ins = pe.matmul(ps[:, 2 + c, hc(m, h)], ET[:, x, :], vt[:, c, hc(m, h)], start=False, stop=True,
                                            skip_group_check=True)
                    ins.then_inc(s["y_made"], 1)
        return sems


def output_projection(nc, S, ring, l):
    ps, ident, YT, YF, t = S["ps"], S["ident"], S["YT"], S["YF"], S["t"]
    with ExitStack() as ctx:
        turned, yf_ready, used = sems = semaphores(ctx, nc, "op_turned op_yf_ready op_used")
        with nc.Block() as block:

            @block.sync
            def _(sp):
                for j in range(4):
                    load_expert_chunk(sp, S, l, 0, j)

            @block.tensor
            def _(pe):
                for a in range(TT):
                    for d in range(DT):
                        ins = pe.transpose(ps[:, 4 + 2 * a + d // 4, (d % 4) * P:(d % 4 + 1) * P],
                                           YT[:, a, d * P:(d + 1) * P], ident[:])
                    ins.then_inc(turned, 1)
                pe.wait_ge(yf_ready, TT)
                for h in range(2):
                    ring.arrived(pe, C2_WOUT + h)
                    w = ring.view(C2_WOUT + h, DT, CH)
                    for a in range(TT):
                        for k in range(DT):
                            ins = pe.matmul(ps[:, 2 * a + h, :], YF[:, k, a * P:(a + 1) * P], w[:, k, :],
                                            start=(k == 0), stop=(k == DT - 1))
                    ins.then_inc(ring.used, 1)

            @block.scalar
            def _(act):
                for a in range(TT):
                    act.wait_ge(turned, a + 1)
                    act.activation(YF[:, :, a * P:(a + 1) * P],
                                   ps[:, 4 + 2 * a:6 + 2 * a, :].rearrange("p a (d t) -> p (a d) t", d=4),
                                   ACT.Copy).then_inc(yf_ready, 1)
        return sems


def route(nc, S, l):
    ps, XT, WR, BR, gates, rank = S["ps"], S["XT"], S["WR"], S["BR"], S["gates"], S["rank"]
    with ExitStack() as ctx:
        sb = lambda n, s: ctx.enter_context(nc.sbuf_tensor(f"rt_{n}", s, F32))
        lg = sb("lg", [P, TT, 36])
        keep = sb("keep", [P, 8])
        gmax, gsum, m1, m2, ws = (sb(n, [P, TT]) for n in ("gmax", "gsum", "m1", "m2", "ws"))
        eg, ohg, cg = (sb(n, [P, TT, 4]) for n in ("eg", "ohg", "cg"))
        tmp = sb("tmp", [P, TT, 32])
        el, oh1, oh2, c8 = (sb(n, [P, TT, 8]) for n in ("el", "oh1", "oh2", "c8"))
        chosen = sb("chosen", [P, TT, N_EXP])
        most, more = sb("most", [P, 1]), sb("more", [P, 1])
        total = sb("total", [P, 1])
        logits, group_diff, group_exp, pair_diff, pair_exp, chosen_ready, ranked, dve_step = semaphores(
            ctx, nc, "rt_logits rt_group_diff rt_group_exp rt_pair_diff rt_pair_exp rt_chosen_ready rt_ranked rt_dve_step")
        block = ctx.enter_context(nc.Block())

        @block.sync
        def _(sp):
            for j in (4, 5):
                load_expert_chunk(sp, S, l, 0, j)

        @block.tensor
        def _(pe):
            for a in range(TT):
                for k in range(DT):
                    ins = pe.matmul(ps[:, 4, a * 64:a * 64 + 36], XT[:, k, a * P:(a + 1) * P], WR[:, k, :],
                                    start=(k == 0), stop=(k == DT - 1))
            ins.then_inc(logits, 1)
            pe.wait_ge(chosen_ready, 1)
            strict, ones = S["triu_strict"], S["ones"]
            pe.matmul(ps[:, 5, 0:32], strict[:], chosen[:, 0, :], start=True, stop=True)
            pe.matmul(ps[:, 5, 32:64], strict[:], chosen[:, 1, :], start=True, stop=False)
            pe.matmul(ps[:, 5, 32:64], ones[:], chosen[:, 0, :], start=False, stop=True)
            pe.matmul(ps[:, 5, 64:96], ones[:], chosen[:, 0, :], start=True, stop=False)
            pe.matmul(ps[:, 5, 64:96], ones[:], chosen[:, 1, :], start=False, stop=True).then_inc(ranked, 1)

        @block.scalar
        def _(act):
            act.wait_ge(group_diff, 1)
            act.activation(eg[:], eg[:], ACT.Exp).then_inc(group_exp, 1)
            act.wait_ge(pair_diff, 1)
            act.activation(ws[:], ws[:], ACT.Exp).then_inc(pair_exp, 1)

        @block.vector
        def _(dve):
            step = Chain(dve, dve_step)
            wide = lambda v, n: v.unsqueeze(2).to_broadcast([P, TT, n])

            def first_of(out, count, values, best, n):
                step(dve.tensor_tensor(out[:], values, wide(best[:], n), ALU.is_ge))
                for a in range(TT):
                    ins = dve.tensor_tensor_scan(count[:, a, :], keep[:, 0:n], out[:, a, :], 0.0, ALU.mult, ALU.add)
                step(ins)
                step(dve.tensor_scalar(count[:], count[:], 1.0, None, ALU.is_equal))
                step(dve.tensor_tensor(out[:], out[:], count[:], ALU.mult))

            dve.memset(keep[:], 1.0)
            dve.wait_ge(logits, 1)
            step(dve.tensor_tensor(lg[:], ps[:, 4, 0:128].rearrange("p (a n) -> p a n", a=TT)[:, :, 0:36],
                                   BR[:].unsqueeze(1).to_broadcast([P, TT, 36]), ALU.add))
            step(dve.tensor_reduce(gmax[:], lg[:, :, 0:4], AX.X, ALU.max))
            dve.tensor_tensor(eg[:], lg[:, :, 0:4], wide(gmax[:], 4), ALU.subtract).then_inc(group_diff, 1)
            first_of(ohg, cg, lg[:, :, 0:4], gmax, 4)
            for a in range(TT):
                ins = dve.tensor_tensor(tmp[:, a, :].rearrange("p (g e) -> p g e", g=4),
                                        lg[:, a, 4:36].rearrange("p (g e) -> p g e", g=4),
                                        ohg[:, a, :].unsqueeze(2).to_broadcast([P, 4, 8]), ALU.mult)
            step(ins)
            step(dve.tensor_reduce(el[:], tmp[:].rearrange("p a (g e) -> p a e g", g=4), AX.X, ALU.add))
            step(dve.tensor_reduce(m1[:], el[:], AX.X, ALU.max))
            first_of(oh1, c8, el[:], m1, 8)
            step(dve.scalar_tensor_tensor(el[:], oh1[:], -1.0e30, el[:], ALU.mult, ALU.add))
            step(dve.tensor_reduce(m2[:], el[:], AX.X, ALU.max))
            dve.tensor_tensor(ws[:], m2[:], m1[:], ALU.subtract).then_inc(pair_diff, 1)
            first_of(oh2, c8, el[:], m2, 8)
            dve.wait_ge(group_exp, 1)
            step(dve.tensor_reduce(gsum[:], eg[:], AX.X, ALU.add))
            dve.wait_ge(pair_exp, 1)
            step(dve.tensor_scalar(m1[:], ws[:], 1.0, None, ALU.add))
            step(dve.tensor_tensor(m1[:], m1[:], gsum[:], ALU.mult))
            step(dve.reciprocal(m1[:], m1[:]))
            step(dve.tensor_tensor(m2[:], ws[:], m1[:], ALU.mult))
            dve.tensor_tensor(oh1[:], oh1[:], wide(m1[:], 8), ALU.mult)
            step(dve.tensor_tensor(oh2[:], oh2[:], wide(m2[:], 8), ALU.mult))
            step(dve.tensor_tensor(oh1[:], oh1[:], oh2[:], ALU.add))
            dve.memset(gates[:, :, N_EXP:], 0.0)
            dve.memset(rank[:, :, N_EXP:], -1.0)
            for a in range(TT):
                ins = dve.tensor_tensor(gates[:, a, 0:N_EXP].rearrange("p (g e) -> p g e", g=4),
                                        ohg[:, a, :].unsqueeze(2).to_broadcast([P, 4, 8]),
                                        oh1[:, a, :].unsqueeze(1).to_broadcast([P, 4, 8]), ALU.mult)
            step(ins)
            dve.tensor_scalar(chosen[:], gates[:, :, 0:N_EXP], 0.0, None, ALU.is_gt).then_inc(chosen_ready, 1)
            dve.wait_ge(ranked, 1)
            v = rank[:, :, 0:N_EXP]
            step(dve.scalar_tensor_tensor(v, ps[:, 5, 0:64].rearrange("p (a e) -> p a e", a=TT), 1.0, chosen[:],
                                          ALU.add, ALU.mult))
            dve.tensor_scalar(v, v, 1.0, None, ALU.subtract)
            step(dve.tensor_reduce(most[:], ps[:, 5, 64:96], AX.X, ALU.max))
            step(dve.tensor_scalar(total[:], most[:], float(CAP), 1.0, ALU.is_gt, ALU.add))
            for n in range(2, T // CAP):
                step(dve.tensor_scalar(more[:], most[:], float(CAP * n), None, ALU.is_gt))
                step(dve.tensor_tensor(total[:], total[:], more[:], ALU.add))
            dve.tensor_copy(S["rounds"][:], total[:])


EPB = 4
PAIRS = EPB // 2
CPB = 3 * EPB
NB = N_EXP // EPB
CAP = 64


def experts(nc, S, l):
    ps, zeros = S["ps"], S["zeros"]
    with ExitStack() as ctx:
        zero_ready, = semaphores(ctx, nc, "ex_zero_ready")
        block = ctx.enter_context(nc.Block())

        @block.vector
        def _(dve):
            dve.memset(zeros[:], 0.0).then_inc(zero_ready, 1)

        @block.tensor
        def _(pe):
            pe.wait_ge(zero_ready, 1)
            for b in range(4):
                pe.matmul(ps[:, b, :], zeros[:, 0:P], zeros[:], start=True, stop=False, skip_group_check=True)

    expert_round(nc, S, l, True)
    rounds = nc.values_load(S["rounds"][0:1, 0:1], min_val=1, max_val=T // CAP)
    with nc.If(rounds > 1):
        with nc.Fori(1, rounds) as _:
            expert_round(nc, S, l, False)


def chunk_of(j):
    return 2 * (j // 6) + j % 2, (j % 6) // 2


def expert_slot(S, j):
    j %= SLOTS + EXTRA_SLOTS
    return S["weights"][:, (1, 2, None, None, 3, 0)[j], :] if j not in (2, 3) else S["more"][:, j - 2, :]


def expert_view(S, j, a, b):
    return expert_slot(S, j).rearrange("p (a b) -> p a b", a=a)


def load_expert_chunk(sp, S, l, i, j):
    e, part = chunk_of(j)
    a, b = (DT, CH) if part < 2 else (4, D)
    sp.dma_start(expert_view(S, j, a, b), expert_chunk(S["t"], l * N_EXP + EPB * i + e, part)).then_inc(
        S["expert_landed"][j % (SLOTS + EXTRA_SLOTS)], 16)


def expert_round(nc, S, l, first):
    ps, ident, X, gates, rank, iota = (S[n] for n in ("ps", "ident", "X", "gates", "rank", "iota"))
    xc = S["XT"]
    ye = S["YT"]
    with ExitStack() as ctx:
        sb = lambda n, s: ctx.enter_context(nc.sbuf_tensor(f"ex_{int(first)}_{n}", s, F32))
        NS = SLOTS + EXTRA_SLOTS
        sel = sb("sel", [P, TT, EPB, CAP])
        selg = sb("selg", [P, TT, EPB, CAP])
        GT = sb("GT", [P, PAIRS, T])
        sg, hs = sb("sg", [P, E_FF]), sb("hs", [P, E_FF])
        hT = sb("hT", [P, 4, P])
        (used, sel_ready, selg_ready, gathered, xc_low_ready, xc_high_ready, gt_turned, gt_ready, silu_ready, h_ready,
         turned, ht_ready, ye_low_ready, ye_high_ready, dve_step) = semaphores(
            ctx, nc, " ".join(f"ex_{int(first)}_{s}" for s in """used sel_ready selg_ready gathered xc_low_ready
            xc_high_ready gt_turned gt_ready silu_ready h_ready turned ht_ready ye_low_ready ye_high_ready
            dve_step""".split()), EXPERT_LANDED)
        landed = S["expert_landed"]
        block = ctx.enter_context(nc.Block())
        bank_pair = lambda b: ps[:, b:b + 2, :].rearrange("p a (k c) -> p (a k) c", c=EPB * CAP)

        view = lambda j, a, b: expert_view(S, j, a, b)

        @block.sync
        def _(sp):
            for j in range(CPB):
                if j >= NS:
                    sp.wait_ge(used, j - NS + 1)
                if j >= NS or not first:
                    load_expert_chunk(sp, S, l, 0, j)
            with sp.Fori(1, NB) as i:
                for j in range(CPB):
                    sp.wait_ge(used, CPB * i + (j - NS + 1))
                    load_expert_chunk(sp, S, l, i, j)

        @block.tensor
        def _(pe):
            def arrived(i, j):
                pe.wait_ge(landed[j % NS], (16 * CPB // NS) * i + 16 * (j // NS + 1))

            def gather(i):
                pe.wait_ge(sel_ready, i + 1)
                for part in range(2):
                    for k in range(4 * part, 4 * part + 4):
                        out = bank_pair(4 + 2 * part)[:, k % 4, :]
                        for a in range(TT):
                            ins = pe.matmul(out, X[:, a, k * P:(k + 1) * P], sel[:, a].rearrange("p e c -> p (e c)"),
                                            start=(a == 0), stop=(a == TT - 1))
                    ins.then_inc(gathered, 1)

            def expert_products(i, p, part):
                j = 6 * p + 2 * part
                a, b = (DT, CH)
                w = [view(j + h, a, b) for h in range(2)]
                for h in range(2):
                    arrived(i, j + h)
                for k in range(DT):
                    if p == 0 and part == 0 and k % 4 == 0:
                        pe.wait_ge((xc_low_ready, xc_high_ready)[k // 4], i + 1)
                    for h in range(2):
                        e = 2 * p + h
                        ins = pe.matmul(ps[h * CAP:(h + 1) * CAP, 4 + part, :], xc[:, k, e * CAP:(e + 1) * CAP],
                                        w[h][:, k, :], start=(k == 0), stop=(k == DT - 1))
                        if k == DT - 1:
                            ins.then_inc(used, 1)

            def turn_gates(i, p):
                pe.wait_ge(selg_ready, PAIRS * i + p + 1)
                if p:
                    pe.wait_ge(ye_low_ready, PAIRS * i + p)
                    pe.wait_ge(ye_high_ready, PAIRS * i + p)
                for a in range(TT):
                    ins = pe.transpose(ps[:, 6, a * P:(a + 1) * P],
                                       selg[:, a, 2 * p:2 * p + 2, :].rearrange("p e c -> p (e c)"), ident[:])
                ins.then_inc(gt_turned, 1)

            def down(i, p):
                j = 6 * p + 4
                w = [view(j + h, 4, D) for h in range(2)]
                for h in range(2):
                    arrived(i, j + h)
                pe.wait_ge(gt_ready, PAIRS * i + p + 1)
                pe.wait_ge(ht_ready, PAIRS * i + p + 1)
                for half in range(2):
                    for f in range(4):
                        for h in range(2):
                            ins = pe.matmul(ps[h * CAP:(h + 1) * CAP, 6 + half, :], hT[:, f, h * CAP:(h + 1) * CAP],
                                            w[h][:, f, half * CH:(half + 1) * CH], start=(f == 0), stop=(f == 3))
                            if half == 1 and f == 3:
                                ins.then_inc(used, 1)

            def turn_hidden(i, p):
                pe.wait_ge(h_ready, PAIRS * i + p + 1)
                for f in range(4):
                    ins = pe.transpose(ps[:, 4, f * P:(f + 1) * P], hs[:, f * P:(f + 1) * P], ident[:])
                ins.then_inc(turned, 1)

            def scatter(i, p):
                pe.wait_ge(ye_low_ready, PAIRS * i + p + 1)
                pe.wait_ge(ye_high_ready, PAIRS * i + p + 1)
                for a in range(TT):
                    for half in range(2):
                        pe.matmul(ps[:, 2 * a + half, :], GT[:, p, a * P:(a + 1) * P], ye[:, p, half * CH:(half + 1) * CH],
                                  start=False, stop=False, skip_group_check=True)

            with pe.Fori(0, NB) as i:
                gather(i)
                for p in range(PAIRS):
                    if p == 0:
                        expert_products(i, p, 0)
                        turn_gates(i, p)
                    else:
                        turn_gates(i, p)
                        expert_products(i, p, 0)
                    expert_products(i, p, 1)
                    if p:
                        scatter(i, p - 1)
                    turn_hidden(i, p)
                    down(i, p)
                scatter(i, PAIRS - 1)

        @block.scalar
        def _(act):
            with act.Fori(0, NB) as i:
                act.wait_ge(gathered, 2 * i + 1)
                act.activation(xc[:, 0:4, :], bank_pair(4), ACT.Copy).then_inc(xc_low_ready, 1)
                for p in range(PAIRS):
                    act.wait_ge(gt_turned, PAIRS * i + p + 1)
                    act.activation(GT[:, p, :], ps[:, 6, 0:T], ACT.Copy).then_inc(gt_ready, 1)
                    act.wait_ge(used, CPB * i + (6 * p + 2))
                    act.activation(sg[:], ps[:, 4, :], ACT.Silu).then_inc(silu_ready, 1)
                    act.wait_ge(turned, PAIRS * i + p + 1)
                    act.activation(hT[:], ps[:, 4, :].rearrange("p (f t) -> p f t", f=4), ACT.Copy).then_inc(ht_ready, 1)
                    act.wait_ge(used, CPB * i + (6 * p + 6))
                    act.activation(ye[:, p, 0:CH], ps[:, 6, :], ACT.Copy).then_inc(ye_low_ready, 1)

        @block.vector
        def _(dve):
            def select(i, out, gated, sem):
                for e in range(EPB):
                    for a in range(TT):
                        r = rank[:, a, bass.ds(EPB * i + e, 1)]
                        if gated:
                            ins = dve.tensor_scalar(out[:, a, e, :], iota[:], r, gates[:, a, bass.ds(EPB * i + e, 1)],
                                                    ALU.is_equal, ALU.mult)
                        else:
                            ins = dve.tensor_scalar(out[:, a, e, :], iota[:], r, None, ALU.is_equal)
                    if not gated and e == EPB - 1 or gated and e % 2 == 1:
                        ins.then_inc(sem, 1)

            select(0, sel, False, sel_ready)
            select(0, selg, True, selg_ready)
            with dve.Fori(0, NB) as i:
                dve.wait_ge(gathered, 2 * i + 2)
                dve.tensor_copy(xc[:, 4:8, :], bank_pair(6)).then_inc(xc_high_ready, 1)
                select(i + 1, sel, False, sel_ready)
                for p in range(PAIRS):
                    dve.wait_ge(silu_ready, PAIRS * i + p + 1)
                    dve.wait_ge(used, CPB * i + (6 * p + 4))
                    dve.tensor_tensor(hs[:], sg[:], ps[:, 5, :], ALU.mult).then_inc(h_ready, 1)
                    dve.wait_ge(used, CPB * i + (6 * p + 6))
                    dve.tensor_copy(ye[:, p, CH:D], ps[:, 7, :]).then_inc(ye_high_ready, 1)
                dve.wait_ge(gt_turned, PAIRS * (i + 1))
                select(i + 1, selg, True, selg_ready)
            dve.wait_ge(selg_ready, PAIRS * (NB + 1))
            dve.tensor_scalar(rank[:], rank[:], float(CAP), None, ALU.subtract)


def program(nc, t, out):
    t = dict(t)
    with ExitStack() as ctx:
        sb = lambda n, s, c=ctx: c.enter_context(nc.sbuf_tensor(n, s, F32))
        S = {"t": t, "ps": ctx.enter_context(nc.psum_tensor("ps", [P, 8, 512], F32))}
        buf = S["weights"] = sb("weights", [P, SLOTS, SLOT])
        for name, shape in (("ident", [P, P]), ("ones", [P, P]), ("masks", [P, 2, LEVELS + 1, P]), ("X", [P, TT, D])):
            S[name] = sb(name, shape)
        with ExitStack() as one:
            first_block(nc, t, S, Ring(one, nc, "ring", buf), lambda n, s: sb(n, s, one))
        with ExitStack() as two:
            second_block(nc, t, S, Ring(two, nc, "ring2", buf), two, lambda n, s: sb(n, s, two),
                         lambda n, s: two.enter_context(nc.sbuf_tensor(n, s, mybir.dt.int32)))
        with ExitStack() as last:
            (stored,) = semaphores(last, nc, "stored")
            block = last.enter_context(nc.Block())

            @block.sync
            def _(sp):
                sp.dma_start(out[0].rearrange("(a p) d -> p a d", p=P), S["X"][:]).then_inc(stored, 16)
                sp.wait_ge(stored, 16)


def first_block(nc, t, S, ring, sb):
    for name, shape in (("H", [P, DT, 2 * T]), ("modv", [P, 2, N_MOD * DT]), ("VA", [P, VA_ROWS]),
                        ("VB", [P, VB_ROWS]), ("VC", [64, 4])):
        S[name] = sb(name, shape)
    chunks = first_block_chunks(t)
    S["spectra"] = nc.dram_tensor("spectra", (P, 2, 4, BW), F32).ap()
    with ExitStack() as ctx:
        (set_ones,) = semaphores(ctx, nc, "set_ones")
        block = ctx.enter_context(nc.Block())

        @block.gpsimd
        def _(pool):
            pool.memset(S["ones"][:], 1.0).then_inc(set_ones, 1)

    modulation(nc, t, S, ring, chunks)

    def split_norm(c, W, part, name, room=None):
        for x in ("NH", "NL"):
            S[x] = c.enter_context(nc.sbuf_tensor(f"{name}_{x}", [P, DT, W], F32R))
        norm_modulate(nc, S, W, part, name, room)
        for x in ("w_high", "w_low"):
            S[x] = c.enter_context(nc.sbuf_tensor(f"{name}_{x}", [P, SplitTiles.DEPTH * CH], F32R))

    with ExitStack() as half:
        split_norm(half, 2 * T, 0, "n0")
        feed_forward(nc, S, ring, chunks, 2 * T, 2, C_FFN0, "f0")
    with ExitStack() as mix:
        for name, shape in (("V", [P, 2 * TT, 512]), ("SG", [P, 2, HEADS_A, 2 * T]), ("MG", [P, 2 * DT, T]),
                            ("Q", [P, HEADS_A, T]), ("G", [P, HEADS_A, T]), ("HY", [P, 12, T + 2])):
            S[name] = mix.enter_context(nc.sbuf_tensor(name, shape, F32))
        with ExitStack() as half:
            split_norm(half, 2 * T, 3, "n1", S["SG"][:].rearrange("p r h t -> p (r h) t"))
            input_projection(nc, S, ring, chunks)
        S["N"] = mix.enter_context(nc.sbuf_tensor("N", [P, DT, 2 * T], F32))
        hgrn2(nc, S)
        hyena_mix(nc, S)
        merge_heads(nc, S, ring, chunks)
    with ExitStack() as half:
        split_norm(half, T, 6, "n2")
        feed_forward(nc, S, ring, chunks, T, 8, C_FFN1, "f1")
    to_tokens(nc, t, S)
    ring.clear(nc)


def second_block(nc, t, S, ring, two, sb, sb_int):
    for name, shape in (("XT", [P, DT, T]), ("YT", [P, TT, D]), ("RW", [P, 7, T + 1]), ("DTR", [P, TT, 8]),
                        ("VL", [P, VL_ROWS]), ("RB", [P, RB_END]), ("LR", [P, 3, 256]), ("WA2", [16, P]),
                        ("WR", [P, DT, 36]), ("BR", [P, 36]), ("triu", [P, P]), ("triu_strict", [P, P]),
                        ("blockones", [P, P]), ("hm2", [P, 2]), ("hm4", [P, 4]), ("gates", [P, TT, N_EXP + EPB]), ("rank", [P, TT, N_EXP + EPB]), ("iota", [P, CAP]),
                        ("arena", [P, 4400])):
        S[name] = sb(name, shape)
    at = 0
    for name, shape in (("Z", [TT, BW]), ("XBC", [6, T + 3]), ("GV", [TT, 256]), ("GG", [TT, 256])):
        n = shape[0] * shape[1]
        S[name] = S["arena"][:, at:at + n].rearrange("p (a b) -> p a b", a=shape[0])
        at += n
    S["GQ"], S["GK"] = S["arena"][:, at:at + T], S["arena"][:, at + T:at + 2 * T]
    S["GA"] = S["arena"][0:16, at + 2 * T:at + 3 * T]
    S["YF"] = S["arena"][:, 0:DT * T].rearrange("p (k t) -> p k t", k=DT)
    S["rounds"] = sb_int("rounds", [P, 1])
    S["zeros"] = S["arena"][:, 2048:2048 + CH]
    with ExitStack() as ctx:
        const_in, lr_zero = semaphores(ctx, nc, "const_in lr_zero")
        block = ctx.enter_context(nc.Block())

        @block.sync
        def _(sp):
            for name in ("triu", "triu_strict", "blockones", "hm2", "hm4", "iota"):
                sp.dma_start(S[name][:], t["c_" + name]).then_inc(const_in, 16)
            sp.wait_ge(const_in, 96)

        @block.gpsimd
        def _(pool):
            pool.memset(S["LR"][:], 0.0).then_inc(lr_zero, 1)

    S["expert_landed"] = [two.enter_context(nc.semaphore(f"expert_landed{i}", num=EXPERT_LANDED + i))
                          for i in range(SLOTS + EXTRA_SLOTS)]
    residual_norm(nc, S, "l0", t["ln_in_g_2"], t["ln_in_b_2"], False)
    with nc.Fori(0, 2) as l:
        row = lambda name: t[name][bass.ds(l, 1)].rearrange("a n -> (a n)")
        project_and_mix(nc, S, ring, l)
        rwkv_mixer(nc, S)
        with ExitStack() as moe:
            S["more"] = moe.enter_context(nc.sbuf_tensor("more", [P, EXTRA_SLOTS, SLOT], F32))
            output_projection(nc, S, ring, l)
            residual_norm(nc, S, "l1", row("ln1_g_2"), row("ln1_b_2"), True)
            route(nc, S, l)
            experts(nc, S, l)
        residual_norm(nc, S, "l2", row("ln2_g_2"), row("ln2_b_2"), True)
        ring.clear(nc)


def constants():
    c = {"c_ident": np.eye(P, dtype=np.float32)}
    c["c_fold"] = (np.arange(P)[:, None] % 32 == np.arange(2)[None]).astype(np.float32)
    quarter, grid_w = D // 4, 64
    omega = 1.0 / (10000.0 ** (np.arange(quarter, dtype=np.float32) / np.float32(quarter)))
    ar = np.arange(T // grid_w, dtype=np.float32)[:, None] * omega
    ac = np.arange(grid_w, dtype=np.float32)[:, None] * omega
    er = np.concatenate([np.sin(ar), np.cos(ar)], -1)
    ec = np.concatenate([np.sin(ac), np.cos(ac)], -1)
    c["c_pos"] = np.concatenate([np.broadcast_to(er[:, None], (T // grid_w, grid_w, D // 2)),
                                 np.broadcast_to(ec[None], (T // grid_w, grid_w, D // 2))], -1)\
        .reshape(T, D).astype(np.float32)
    i = np.arange(P)
    fw = [np.eye(P, dtype=bool)]
    for l in range(LEVELS):
        size = 2 << l
        same = (i[:, None] // size) == (i[None] // size)
        fw.append(same & (i[:, None] % size < size // 2) & (i[None] % size >= size // 2))
    fw = np.stack(fw, 1)
    c["c_masks"] = np.stack([fw, fw.transpose(2, 1, 0)], 1).reshape(P, -1).astype(np.float32)
    p = np.arange(T, dtype=np.float64)
    tn = p / (T - 1)
    ang = (2.0 * math.pi * p / T)[:, None] * np.linspace(1e-4, 15, 16)[None]
    c["c_feat"] = np.concatenate([tn[:, None], np.cos(ang), -np.sin(ang)], -1).T.astype(np.float32)
    deltas = np.abs(np.linspace(math.log(1e-2) / 1.5, math.log(1e-2) / 0.3, BW))
    c["c_window"] = (np.exp(-tn[:, None] * deltas[None]) + 0.05).astype(np.float32)
    theta = math.pi * (2 * np.arange(T) + 1) / (2 * T)
    at = theta[None] * p[:, None]
    c["c_cf"] = np.concatenate([np.cos(at), -np.sin(at)], 1).astype(np.float32)
    at1 = theta[None] * (p[:, None] + 1)
    cg = np.concatenate([np.cos(at1), np.sin(at1)], 1)
    cg[T - 1] = 0.0
    c["c_cg"] = cg.astype(np.float32)
    c["c_ci"] = (np.concatenate([np.cos(at.T), -np.sin(at.T)], 0) / T).astype(np.float32)
    c["c_triu"] = (i[:, None] <= i[None]).astype(np.float32)
    c["c_triu_strict"] = (i[:, None] < i[None]).astype(np.float32)
    c["c_blockones"] = (i[:, None] // 64 == i[None] // 64).astype(np.float32)
    c["c_hm2"] = (i[:, None] // 64 == np.arange(2)[None]).astype(np.float32)
    c["c_hm4"] = (i[:, None] // 32 == np.arange(4)[None]).astype(np.float32)
    c["c_iota"] = np.broadcast_to(np.arange(CAP, dtype=np.float32), (P, CAP)).copy()
    return c


def kernel(**inputs):
    import concourse.bacc as bacc
    from concourse.bass_utils import run_bass_kernel_spmd

    nc = bacc.Bacc("TRN2", target_bir_lowering=False, num_devices=1)
    arrays, t = {}, {}
    for name, a in list(inputs.items()) + list(constants().items()):
        a = np.ascontiguousarray(a)
        arrays[f"in_{name}"] = a
        t[name] = nc.dram_tensor(f"in_{name}", a.shape, mybir.dt.from_np(a.dtype), kind="ExternalInput").ap()
    out = nc.dram_tensor("out", (1, T, D), F32, kind="ExternalOutput").ap()
    program(nc, t, out)
    r = run_bass_kernel_spmd(nc, [arrays], core_ids=[0])
    return r.results[0]["out"]
```
